# Optimizing a Trainium2 kernel written in Bass

```python
import jax, jax.numpy as jnp
from jax import lax
import numpy as np

D_MODEL = 1024
BATCH = 1
SEQ = 128
DEPTH = 2
DEC_BATCH = 1
DEC_SEQ = 256
PAST_LEN = 128

GRID_W = 64
HEAD_DIM = 64
N_HEADS = 8
N_KV_HEADS = 2
GQA_GROUPS = N_HEADS // N_KV_HEADS
ATTN_W = N_HEADS * HEAD_DIM
KV_W = N_KV_HEADS * HEAD_DIM
WINDOW = 128
BLOCK = 128
SPAN = BLOCK + 2 * WINDOW
ROPE_BASE = 10000.0
AXIS_PAIRS = HEAD_DIM // 4
CONV_W = D_MODEL // 2
CONV_K = 31
CONV_PAD = CONV_K // 2
N_EXPERTS = 16
N_GROUPS = 4
EXPERTS_PER_GROUP = N_EXPERTS // N_GROUPS
TOPK_GROUPS = 1
TOP_K = 2
D_EXPERT = 512
IN_W = ATTN_W + 2 * KV_W + 2 * CONV_W + 2 * D_MODEL
SPLITS = (ATTN_W, ATTN_W + KV_W, ATTN_W + 2 * KV_W, ATTN_W + 2 * KV_W + 2 * CONV_W)
EPS = 1e-6
NEG = -1e30

kernel_name = "hybrid_dit_swa_conformer_moe_step"

def rms_norm(x, g):
    xf = x.astype(jnp.float32)
    y = xf * lax.rsqrt(jnp.mean(xf * xf, axis=-1, keepdims=True) + EPS)
    return (y * g.astype(jnp.float32)).astype(x.dtype)

def layer_norm(x, g, b):
    xf = x.astype(jnp.float32)
    mu = jnp.mean(xf, axis=-1, keepdims=True)
    var = jnp.mean(jnp.square(xf - mu), axis=-1, keepdims=True)
    y = (xf - mu) * lax.rsqrt(var + EPS) * g.astype(jnp.float32) + b.astype(jnp.float32)
    return y.astype(x.dtype)

def modulate(x, g, shift, scale):
    return rms_norm(x, g) * (1 + scale) + shift

def axial_angles(L):
    rows = L // GRID_W
    row = jnp.repeat(jnp.arange(rows), GRID_W).astype(jnp.float32)
    col = jnp.tile(jnp.arange(GRID_W), rows).astype(jnp.float32)
    inv = ROPE_BASE ** (-jnp.arange(AXIS_PAIRS, dtype=jnp.float32) / AXIS_PAIRS)
    return row[:, None] * inv, col[:, None] * inv

def rope_half(x, ang):
    cos = jnp.cos(ang)[:, None, :]
    sin = jnp.sin(ang)[:, None, :]
    cos = jnp.concatenate([cos, cos], axis=-1)
    sin = jnp.concatenate([sin, sin], axis=-1)
    xf = x.astype(jnp.float32)
    x1, x2 = jnp.split(xf, 2, axis=-1)
    return xf * cos + jnp.concatenate([-x2, x1], axis=-1) * sin

def axial_rope(x, ang_r, ang_c):
    xr, xc = jnp.split(x, 2, axis=-1)
    return jnp.concatenate([rope_half(xr, ang_r), rope_half(xc, ang_c)], axis=-1).astype(x.dtype)

def sink_softmax(logits, sink):
    s = jnp.broadcast_to(sink.astype(jnp.float32).reshape(N_KV_HEADS, GQA_GROUPS)[None, :, :, None, None],
                         logits.shape[:-1] + (1,))
    return jax.nn.softmax(jnp.concatenate([logits, s], axis=-1), axis=-1)[..., :-1]

def context_attention(q, k, v, sink):
    B, S = q.shape[:2]
    nb = S // BLOCK
    scale = HEAD_DIM ** -0.5
    qb = q.reshape(B, nb, BLOCK, N_KV_HEADS, GQA_GROUPS, HEAD_DIM).swapaxes(0, 1)

    def one_block(qi):
        s = jnp.einsum('bqhgd,bkhd->bhgqk', qi, k).astype(jnp.float32) * scale
        p = sink_softmax(s, sink).astype(v.dtype)
        return jnp.einsum('bhgqk,bkhd->bqhgd', p, v)

    o = lax.map(one_block, qb)
    return o.swapaxes(0, 1).reshape(B, S, ATTN_W)

def latent_attention(q, k, v, kc, vc, sink):
    B, L = q.shape[:2]
    nb = L // BLOCK
    scale = HEAD_DIM ** -0.5
    pad = ((0, 0), (WINDOW, WINDOW), (0, 0), (0, 0))
    kp = jnp.pad(k, pad)
    vp = jnp.pad(v, pad)
    qb = q.reshape(B, nb, BLOCK, N_KV_HEADS, GQA_GROUPS, HEAD_DIM).swapaxes(0, 1)

    def one_block(args):
        i, qi = args
        start = i * BLOCK
        kb = lax.dynamic_slice_in_dim(kp, start, SPAN, axis=1)
        vb = lax.dynamic_slice_in_dim(vp, start, SPAN, axis=1)
        qpos = start + jnp.arange(BLOCK)
        kpos = start - WINDOW + jnp.arange(SPAN)
        mask = (jnp.abs(qpos[:, None] - kpos[None, :]) <= WINDOW) & (kpos >= 0)[None, :] & (kpos < L)[None, :]
        s_loc = jnp.einsum('bqhgd,bkhd->bhgqk', qi, kb).astype(jnp.float32) * scale
        s_loc = jnp.where(mask, s_loc, NEG)
        s_ctx = jnp.einsum('bqhgd,bchd->bhgqc', qi, kc).astype(jnp.float32) * scale
        p = sink_softmax(jnp.concatenate([s_loc, s_ctx], axis=-1), sink).astype(v.dtype)
        return (jnp.einsum('bhgqk,bkhd->bqhgd', p[..., :SPAN], vb)
                + jnp.einsum('bhgqc,bchd->bqhgd', p[..., SPAN:], vc))

    o = lax.map(one_block, (jnp.arange(nb), qb))
    return o.swapaxes(0, 1).reshape(B, L, ATTN_W)

def conv_module(u, dw_w, dw_b, ln_g, ln_b):
    a, b = jnp.split(u, 2, axis=-1)
    y = a * jax.nn.sigmoid(b)
    y = lax.conv_general_dilated(y, dw_w[:, None, :].astype(y.dtype), window_strides=(1,),
                                 padding=[(CONV_PAD, CONV_PAD)],
                                 dimension_numbers=('NWC', 'WIO', 'NWC'),
                                 feature_group_count=CONV_W) + dw_b
    return jax.nn.silu(layer_norm(y, ln_g, ln_b))

def mixer(h, p, attend):
    B, L, _ = h.shape
    q, k, v, u, gates = jnp.split(h @ p['w_in'], SPLITS, axis=-1)
    q = rms_norm(q.reshape(B, L, N_HEADS, HEAD_DIM), p['q_norm'])
    k = rms_norm(k.reshape(B, L, N_KV_HEADS, HEAD_DIM), p['k_norm'])
    v = v.reshape(B, L, N_KV_HEADS, HEAD_DIM)
    attn = attend(q, k, v) @ p['w_attn_proj']
    conv = conv_module(u, p['dw_w'], p['dw_b'], p['cln_g'], p['cln_b']) @ p['w_conv_proj']
    g_attn, g_conv = jnp.split(jax.nn.sigmoid(gates), 2, axis=-1)
    return (g_attn * attn + g_conv * conv) @ p['w_out'], k, v

def moe(h, w_router, router_bias, w_gate, w_up, w_down):
    B, L, D = h.shape
    t = h.reshape(B * L, D)
    scores = jax.nn.sigmoid((t @ w_router).astype(jnp.float32))
    sel = scores + router_bias.astype(jnp.float32)
    grp_score = lax.top_k(sel.reshape(-1, N_GROUPS, EXPERTS_PER_GROUP), 2)[0].sum(-1)
    _, gidx = lax.top_k(grp_score, TOPK_GROUPS)
    gmask = jax.nn.one_hot(gidx, N_GROUPS, dtype=jnp.float32).sum(-2) > 0
    emask = jnp.repeat(gmask, EXPERTS_PER_GROUP, axis=-1)
    _, eidx = lax.top_k(jnp.where(emask, sel, NEG), TOP_K)
    w = jnp.take_along_axis(scores, eidx, axis=-1)
    w = w / jnp.sum(w, axis=-1, keepdims=True)
    combine = jnp.einsum('tk,tke->te', w, jax.nn.one_hot(eidx, N_EXPERTS, dtype=jnp.float32))
    hid = jax.nn.silu(jnp.einsum('td,edf->tef', t, w_gate)) * jnp.einsum('td,edf->tef', t, w_up)
    hid = hid * combine.astype(hid.dtype)[..., None]
    return jnp.einsum('tef,efd->td', hid, w_down).reshape(B, L, D)

def trunk_layer(x, cond, attend, p, w_router, router_bias):
    mod = jax.nn.silu(cond) @ p['w_ada'] + p['b_ada']
    sh1, sc1, g1, sh2, sc2, g2 = jnp.split(mod, 6, axis=-1)
    mix, k, v = mixer(modulate(x, p['norm1'], sh1, sc1), p, attend)
    x = x + g1 * mix
    h = modulate(x, p['norm2'], sh2, sc2)
    x = x + g2 * moe(h, w_router, router_bias, p['w_e_gate'], p['w_e_up'], p['w_e_down'])
    return x, k, v

def setup_inputs(seed: int = 0) -> dict:
    key = jax.random.key(seed)
    ks = iter(jax.random.split(key, 40))
    f32 = jnp.float32
    nrm = lambda shape, s=1.0: jax.random.normal(next(ks), shape, f32) * s
    gain = lambda shape: 1.0 + 0.02 * jax.random.normal(next(ks), shape, f32)
    D = D_MODEL
    return {
        'x_prompt': nrm((BATCH, SEQ, D)),
        'x_sample': nrm((DEC_BATCH, DEC_SEQ, D)),
        'cache_k': nrm((DEC_BATCH, DEPTH, PAST_LEN, N_KV_HEADS, HEAD_DIM)),
        'cache_v': nrm((DEC_BATCH, DEPTH, PAST_LEN, N_KV_HEADS, HEAD_DIM)),
        'c': nrm((DEC_BATCH, D)),
        'c_ctx': nrm((D,)),
        'w_ada': nrm((DEPTH, D, 6 * D), 0.5 * D ** -0.5),
        'b_ada': nrm((DEPTH, 6 * D), 0.02),
        'norm1': gain((DEPTH, D)),
        'norm2': gain((DEPTH, D)),
        'w_in': nrm((DEPTH, D, IN_W), D ** -0.5),
        'q_norm': gain((DEPTH, HEAD_DIM)),
        'k_norm': gain((DEPTH, HEAD_DIM)),
        'sink': nrm((DEPTH, N_HEADS), 0.5),
        'w_attn_proj': nrm((DEPTH, ATTN_W, D), ATTN_W ** -0.5),
        'dw_w': nrm((DEPTH, CONV_K, CONV_W), CONV_K ** -0.5),
        'dw_b': nrm((DEPTH, CONV_W), 0.02),
        'cln_g': gain((DEPTH, CONV_W)),
        'cln_b': nrm((DEPTH, CONV_W), 0.02),
        'w_conv_proj': nrm((DEPTH, CONV_W, D), CONV_W ** -0.5),
        'w_out': nrm((DEPTH, D, D), D ** -0.5),
        'w_router': nrm((D, N_EXPERTS), D ** -0.5),
        'router_bias': nrm((N_EXPERTS,), 0.01),
        'w_e_gate': nrm((DEPTH, N_EXPERTS, D, D_EXPERT), D ** -0.5),
        'w_e_up': nrm((DEPTH, N_EXPERTS, D, D_EXPERT), D ** -0.5),
        'w_e_down': nrm((DEPTH, N_EXPERTS, D_EXPERT, D), D_EXPERT ** -0.5),
        'final_norm': gain((D,)),
    }

def reference(x_prompt, x_sample, cache_k, cache_v, c, c_ctx, w_ada, b_ada, norm1, norm2,
              w_in, q_norm, k_norm, sink, w_attn_proj, dw_w, dw_b, cln_g, cln_b, w_conv_proj,
              w_out, w_router, router_bias, w_e_gate, w_e_up, w_e_down, final_norm):
    ang_r, ang_c = axial_angles(x_sample.shape[1])
    cond_ctx = c_ctx[None, None, :]
    cond_lat = c[:, None, :]
    xp, xs = x_prompt, x_sample
    new_ks, new_vs = [], []
    for l in range(DEPTH):
        p = {
            'w_ada': w_ada[l], 'b_ada': b_ada[l], 'norm1': norm1[l], 'norm2': norm2[l],
            'w_in': w_in[l], 'q_norm': q_norm[l], 'k_norm': k_norm[l],
            'w_attn_proj': w_attn_proj[l], 'dw_w': dw_w[l], 'dw_b': dw_b[l],
            'cln_g': cln_g[l], 'cln_b': cln_b[l], 'w_conv_proj': w_conv_proj[l],
            'w_out': w_out[l], 'w_e_gate': w_e_gate[l], 'w_e_up': w_e_up[l],
            'w_e_down': w_e_down[l],
        }
        sink_l = sink[l]
        kc_l = cache_k[:, l]
        vc_l = cache_v[:, l]

        ctx_attend = lambda q, k, v: context_attention(q, k, v, sink_l)
        xp, k_ctx, v_ctx = trunk_layer(xp, cond_ctx, ctx_attend, p, w_router, router_bias)
        new_ks.append(k_ctx)
        new_vs.append(v_ctx)

        lat_attend = lambda q, k, v: latent_attention(axial_rope(q, ang_r, ang_c),
                                                      axial_rope(k, ang_r, ang_c),
                                                      v, kc_l, vc_l, sink_l)
        xs, _, _ = trunk_layer(xs, cond_lat, lat_attend, p, w_router, router_bias)

    y_prompt = rms_norm(xp, final_norm)
    y_sample = rms_norm(xs, final_norm)
    new_k = jnp.stack(new_ks, axis=1)
    new_v = jnp.stack(new_vs, axis=1)
    return (y_prompt, y_sample, new_k, new_v)


_drawn_inputs = setup_inputs


def setup_inputs(seed=0):
    import zlib

    import numpy as np

    out = dict(_drawn_inputs(seed))
    spreads = {}
    factors = {'cache_k': 2.817,
     'norm1': 2.942,
     'q_norm': 8.0,
     'k_norm': 3.074,
     'sink': 8.0,
     'dw_b': 3.563,
     'cln_g': 4.255,
     'cln_b': 2.783,
     'final_norm': 2.782}
    for name, (base, spread) in spreads.items():
        noise = np.random.default_rng([zlib.crc32(name.encode()), seed]).standard_normal(out[name].shape)
        drawn = base * np.exp(spread * noise) if base else spread * noise
        out[name] = __import__('jax').numpy.asarray(drawn.astype(out[name].dtype))
    for name, factor in factors.items():
        out[name] = (out[name] * factor).astype(out[name].dtype)
    return out
```

```python
from contextlib import ExitStack

import concourse.bass as bass
from concourse import mybir

F32 = mybir.dt.float32
I32 = mybir.dt.int32
ALU = mybir.AluOpType
ACT = mybir.ActivationFunctionType
AX = mybir.AxisListType

P = 128
D = 1024
KD = D // P
DEPTH = 2
TC, TL = 128, 256
T = TC + TL
NT = T // P
HD = 64
NH, NKV = 8, 2
AW, KVW = NH * HD, NKV * HD
CW = D // 2
KC = CW // P
CK, PAD = 31, 15
NE, NG, EG = 16, 4, 4
DE = 512
KE = DE // P
EPS = 1e-6
NEG = -1e30
SEG = TC + 2 * PAD
UW = SEG + TL + 2 * PAD
CO = UW - 2 * PAD
LAT0 = SEG
ROWS = 2 * T
BLOCKS = NT
SROWS = ROWS + BLOCKS * P

SLOTS = 6
SLOT = 2048
ADA_CHUNKS, DENSE_CHUNKS, MOE_CHUNKS = 24, 24, 6
SLOT_USES = (ADA_CHUNKS + DENSE_CHUNKS + MOE_CHUNKS * NE) // SLOTS

INIT_USES = [("x", [0, 1, 0, 1, 0, 1]), ("cond", [7])]
PRE_USES = [
    ("params", [7]), ("ada", [0, 1] * 6), ("mod", [2]), ("rms1", [3]),
    ("qkv", [4, 5, 6] * 3), ("u", [0, 1, 2, 3] * 2), ("gate", [0, 1, 2, 3] * 4),
    ("qT", [4, 5, 6]), ("kT", [7, 4]), ("scores", [0, 1, 2, 3] * 6), ("probsT", [4, 5] * 12),
    ("pv", [6, 7] * 6), ("ln", [2, 4]), ("aproj", [0, 1, 2, 3] * 2), ("cproj", [4, 5, 6, 7] * 2),
    ("out", [0, 1, 2, 3] * 2), ("rms2", [4]), ("logitsT", [5]), ("h2n", [0, 1, 2] * 2),
    ("logits", [6]), ("rank", [7]), ("xT0", [0, 1]),
]
MOE_BANKS = (2, 3, 0, 1, 4, 5, 6)
POST_USES = [("y", [0, 1, 2] * 2)]


def bank_table():
    init = [0] * 8
    table = {}
    for stage, banks in INIT_USES:
        table[stage] = []
        for b in banks:
            table[stage].append((b, init[b]))
            init[b] += 1
    at = [0] * 8
    for stage, banks in PRE_USES:
        table[stage] = []
        for b in banks:
            table[stage].append((b, at[b]))
            at[b] += 1
    moe = list(at)
    for b in MOE_BANKS:
        at[b] += NE
    for stage, banks in POST_USES:
        table[stage] = []
        for b in banks:
            table[stage].append((b, at[b]))
            at[b] += 1
    return table, [n + 1 for n in init], moe, at


def build(nc, A):
    USES, INIT, MOE_AT, PER = bank_table()
    ctx = ExitStack()
    with ctx:
        def sb(name, shape, dt=F32):
            return ctx.enter_context(nc.sbuf_tensor(name, shape, dt))

        def sem(name):
            return ctx.enter_context(nc.semaphore(name))

        rows_in = nc.dram_tensor("rows_in", (SROWS, D), F32, kind="Internal").ap()
        rows_out = nc.dram_tensor("rows_out", (SROWS, D), F32, kind="Internal").ap()

        ring = [sb(f"ring{s}", [P, SLOT]) for s in range(SLOTS)]
        xT = sb("xT", [P, KD, T])
        hT = sb("hT", [P, KD, T])
        nat = sb("nat", [P, NT, D])
        qkv = sb("qkv", [P, NT, 768])
        qtmp = sb("qtmp", [P, NT, 640])
        qtmp2 = sb("qtmp2", [P, 2, 640])
        kdup = sb("kdup", [P, 4, 2, P])
        qT = sb("qT", [P, 4, T])
        kT = sb("kT", [P, 2, 4 * P])
        cache_k = sb("cache_k_sb", [P, P])
        cache_v = sb("cache_v_sb", [P, P])
        ub = sb("ub", [P, KC, UW])
        sig = sb("sig", [P, 2, T])
        conv = sb("conv", [P, KC, CO])
        csq = sb("csq", [P, KC, CO])
        gates = sb("gates", [P, 2 * KD, T])
        gath = gates[:].rearrange("p a b -> p (a b)").rearrange("p (s n) -> p s n", n=D)
        attnT = sb("attnT", [P, 4, T])
        probs = sb("probs", [P, 2, 2, 3 * P])
        probsT = sb("probsT", [P, 2, 3, P])
        mixtmp = sb("mixtmp", [P, 2, T])
        rstd = sb("rstd", [P, T])
        rms = sb("rms", [P, T])
        mu = sb("mu", [P, CO])
        xg = csq[:].rearrange("p a b -> p (a b)")[:, 0:D]
        xgT = qtmp[:].rearrange("p a b -> p (a b)")[:, 0:D].rearrange("p (k n) -> p k n", k=KD)
        silu = qtmp[:].rearrange("p a b -> p (a b)")[:, D:D + DE]
        hid = csq[:].rearrange("p a b -> p (a b)")[:, D:D + DE]
        hidT = conv[:].rearrange("p a b -> p (a b)")[:, D:D + DE].rearrange("p (k n) -> p k n", k=KE)
        orow = conv[:].rearrange("p a b -> p (a b)")[:, 0:D]
        ident = sb("ident", [P, P])
        ones = sb("ones", [P, P])
        before = sb("before", [P, P])
        sel = sb("sel", [P, 2])
        mask = sb("mask", [P, 2, 3 * P])
        rope = sb("rope", [P, 2, 2, HD])
        eps = sb("eps", [P, 1])
        crow = sb("crow", [24, P])
        fnorm = sb("fnorm", [P, KD])
        condT = sb("condT", [P, KD, 32])
        csig = sb("csig", [P, 16])
        modrow = qtmp2[:].rearrange("p a b -> p (a b)")[:, 0:1024].rearrange("p (i n) -> p i n", i=2)
        prow = sb("prow", [76, P])
        dwrow = sb("dwrow", [CK * KC, P])
        par = sb("par", [P, 76])
        dw = sb("dw", [P, CK * KC])
        mod = sb("mod", [P, 48, 2])
        coef = sb("coef", [P, 2, KD, 2])
        qkn = sb("qkn", [P, 2, HD])
        sinkb = sb("sinkb", [P, NH])
        nsink = sb("nsink", [P, NH])
        rbias = sb("rbias", [P, NE])
        ss = sb("ss", [P, NT * 10])
        st = sb("st", [P, 2, 8])
        lgT = sb("lgT", [NE, T])
        sc = sb("sc", [P, NT, NE])
        se = sb("se", [P, NT, NE])
        m1 = sb("m1", [P, NT, NE])
        m2 = sb("m2", [P, NT, NE])
        ra = sb("ra", [P, NT, NE])
        rb = sb("rb", [P, NT, NE])
        pair = sb("pair", [P, NT * NG, 6])
        gs = sb("gs", [P, NT, NG])
        gt = sb("gt", [P, NT, NG])
        r1 = sb("r1", [P, NT])
        wk = sb("wk", [P, 2, NT])
        ws = sb("ws", [P, NT])
        cnt = sb("cnt", [P, NE])
        off = sb("off", [P, NE])
        down_i = sb("down_i", [P, NT, NE])
        down_g = sb("down_g", [P, NT, NG])
        zero16 = sb("zero16", [P, NE])
        posf = sb("posf", [P, 2, NT])
        pos = sb("pos", [P, 2, NT], I32)
        rowsf = sb("rowsf", [1, 18])
        orowsf = sb("orowsf", [1, 52])
        row_at = sb("row_at", [1, 18], I32)
        orow_at = sb("orow_at", [1, 52], I32)
        full_f = sb("full_f", [1, 1])
        overfull = sb("overfull", [1, 1], I32)

        ps = ctx.enter_context(nc.psum_tensor("ps", [P, 8, 512], F32))

        landed = [sem(f"landed{s}") for s in range(SLOTS)]
        full = [sem(f"full{b}") for b in range(8)]
        freed = [sem(f"freed{b}") for b in range(8)]
        settled = sem("settled")
        half = sem("half")
        consts = sem("consts")
        consts_v = sem("consts_v")
        consts2 = sem("consts2")
        chain_p = sem("chain_p")
        x_in = sem("x_in")
        c_in = sem("c_in")
        t_in = sem("t_in")
        scratch0 = sem("scratch0")
        zeroed = sem("zeroed")
        par_in = sem("par_in")
        bc_in = sem("bc_in")
        cache_in = sem("cache_in")
        csig_r = sem("csig_r")
        modrow_used = sem("modrow_used")
        mod_r = sem("mod_r")
        xsq = sem("xsq")
        xn_r = sem("xn_r")
        h_r = sem("h_r")
        usig_used = sem("usig_used")
        qsq_r = sem("qsq_r")
        qss_r = sem("qss_r")
        qrms_r = sem("qrms_r")
        k_pre = sem("k_pre")
        q_r = sem("q_r")
        kv_out = sem("kv_out")
        sm_max = sem("sm_max")
        sm_exp = sem("sm_exp")
        p_r = sem("p_r")
        conv_c = sem("conv_c")
        csq_r = sem("csq_r")
        cn_r = sem("cn_r")
        convT_r = sem("convT_r")
        route_r = sem("route_r")
        pos_r = sem("pos_r")
        scat = sem("scat")
        xg_in = sem("xg_in")
        out_wr = sem("out_wr")
        gat = [sem(f"gat{t}") for t in range(NT)]
        comb_r = sem("comb_r")
        chain = sem("chain")
        tapped = sem("tapped")
        y_out = sem("y_out")
        landed_o = [sem(f"landed_o{s}") for s in range(SLOTS)]
        full_o = [sem(f"full_o{b}") for b in range(7)]
        freed_o = [sem(f"freed_o{b}") for b in range(7)]
        half_o = sem("half_o")
        xg_in_o = sem("xg_in_o")
        out_wr_o = sem("out_wr_o")

        CHAIN = 200
        OSTEPS = NE * BLOCKS

        def use(stage, i, l):
            b, n = USES[stage][i]
            return b, l * PER[b] + (INIT[b] + n)

        def init_use(stage, i):
            b, n = USES[stage][i]
            return b, n + 1

        w_ada = A["w_ada"].rearrange("l (c k p) n -> l c p k n", c=2, p=P)
        w_in = A["w_in"].rearrange("l (k p) n -> l p k n", p=P)
        w_ap = A["w_attn_proj"].rearrange("l (k p) n -> l p k n", p=P)
        w_cp = A["w_conv_proj"].rearrange("l (k p) n -> l p k n", p=P)
        w_out = A["w_out"].rearrange("l (k p) n -> l p k n", p=P)
        w_r = A["w_router"].rearrange("(k p) n -> p k n", p=P)
        w_g = A["w_e_gate"].rearrange("l e (k p) n -> (l e) p k n", p=P)
        w_u = A["w_e_up"].rearrange("l e (k p) n -> (l e) p k n", p=P)
        w_d = A["w_e_down"].rearrange("l e (k p) n -> (l e) p k n", p=P)

        ENDS = [("half", g, None) if c == 0 else ("full", "ada", g) for g in range(12) for c in range(2)]
        ENDS += [("full", "qkv", 3 * c + 2) for c in range(3)]
        ENDS += [("full", "u", 2 * c + 1) for c in range(4)]
        ENDS += [("full", "gate", 2 * c + 1) for c in range(8)]
        ENDS += [("full", "aproj", 3), ("full", "aproj", 7), ("full", "cproj", 3), ("full", "cproj", 7)]
        ENDS += [("full", "out", 2 * c + 1) for c in range(4)]
        ENDS += [("full", "logitsT", 0)]
        HALF_PER = 12 + 2 * NE

        def settle(eng):
            eng.sem_inc(settled, 1)

        with nc.Block() as start:
            @start.sync
            def _(sp):
                for s in [*full, *freed, half, out_wr, *full_o, *freed_o, half_o, out_wr_o]:
                    sp.sem_inc(s, 1)

        block = ctx.enter_context(nc.Block())

        @block.sync
        def _(sp):
            def wait_chunk_used(c, l):
                kind, a, i = ENDS[c]
                if kind == "half":
                    sp.wait_ge(half, l * HALF_PER + (a + 2))
                else:
                    b, n = use(a, i, l)
                    sp.wait_ge(full[b], n + 1)

            def load(slot, landed_sem, src):
                n = src.shape[-1]
                k = src.shape[-2]
                dst = ring[slot][:, 0:k * n].rearrange("p (k n) -> p k n", k=k)
                sp.dma_start(dst, src).then_inc(landed_sem, 16)

            def expert_chunk(j, w):
                if j < 4:
                    src = w_g if j < 2 else w_u
                    return src[bass.ds(w, 1), :, :, (j % 2) * 256:(j % 2 + 1) * 256].rearrange("o p k n -> p (o k) n")
                return w_d[bass.ds(w, 1), :, :, (j - 4) * 512:(j - 3) * 512].rearrange("o p k n -> p (o k) n")

            with sp.Fori(0, DEPTH) as l:
                for c in range(ADA_CHUNKS + DENSE_CHUNKS):
                    s = c % SLOTS
                    if c < SLOTS:
                        if c in (0, 2):
                            sp.wait_ge(half, l * HALF_PER + 1)
                        else:
                            b = {1: 2, 3: 3, 4: 5, 5: 6}[c]
                            sp.wait_ge(full[b], l * PER[b] + INIT[b])
                    else:
                        wait_chunk_used(c - SLOTS, l)
                    if c < 24:
                        g, cc = c // 2, c % 2
                        src = w_ada[bass.ds(l, 1), cc, :, :, g * 512:(g + 1) * 512].rearrange("o p k n -> p (o k) n")
                    elif c < 39:
                        m = c - 24
                        src = w_in[bass.ds(l, 1), :, :, m * 256:(m + 1) * 256].rearrange("o p k n -> p (o k) n")
                    elif c < 43:
                        w = w_ap if c < 41 else w_cp
                        h = (c - 39) % 2
                        src = w[bass.ds(l, 1), :, :, h * 512:(h + 1) * 512].rearrange("o p k n -> p (o k) n")
                    elif c < 47:
                        h = c - 43
                        src = w_out[bass.ds(l, 1), :, :, h * 256:(h + 1) * 256].rearrange("o p k n -> p (o k) n")
                    else:
                        src = w_r
                    load(s, landed[s], src)
                for j in range(MOE_CHUNKS):
                    wait_chunk_used(ADA_CHUNKS + DENSE_CHUNKS - SLOTS + j, l)
                    load(j, landed[j], expert_chunk(j, l * NE))
                with sp.Fori(1, NE) as e:
                    for j in range(MOE_CHUNKS):
                        if j in (0, 2):
                            sp.wait_ge(half, l * HALF_PER + e * 2 + (12 - 2 + (2 if j == 0 else 3)))
                        else:
                            b = {1: 2, 3: 3, 4: 5, 5: 6}[j]
                            sp.wait_ge(full[b], l * PER[b] + e + (INIT[b] + MOE_AT[b]))
                        load(j, landed[j], expert_chunk(j, l * NE + e))

                sp.wait_ge(pos_r, l + 1)
                settle(sp)
                over = sp.value_load(overfull[0:1, 0:1], min_val=0, max_val=1)
                sp.wait_ge(full[6], l * PER[6] + (INIT[6] + MOE_AT[6] + NE))
                settle(sp)
                with sp.If(over > 0):
                    with sp.Fori(0, NE) as e:
                        for bl in range(BLOCKS):
                            for j in range(MOE_CHUNKS):
                                if j in (0, 2):
                                    if bl == 0:
                                        sp.wait_ge(half_o, l * (2 * OSTEPS) + e * (2 * BLOCKS) + 1)
                                    else:
                                        sp.wait_ge(half_o, l * (2 * OSTEPS) + e * (2 * BLOCKS) + (2 * bl - 2 + (2 if j == 0 else 3)))
                                else:
                                    b = {1: 2, 3: 3, 4: 5, 5: 6}[j]
                                    sp.wait_ge(full_o[b], l * OSTEPS + e * BLOCKS + (bl + 1))
                                load(j, landed_o[j], expert_chunk(j, l * NE + e))
                    sp.wait_ge(full_o[6], l * OSTEPS + (OSTEPS + 1))
                    settle(sp)
                with sp.Else():
                    for s in range(SLOTS):
                        sp.sem_inc(landed_o[s], 16 * OSTEPS)
                sp.nop()

        def conv_tokens(k):
            return csq[:, k, 0:T]

        @block.tensor
        def _(pe):
            def begin(b, n):
                pe.wait_ge(freed[b], n)

            def chunk_in(c, l):
                pe.wait_ge(landed[c % SLOTS], l * (16 * SLOT_USES) + 16 * (c // SLOTS + 1))

            pe.wait_ge(consts, 3)
            pe.wait_ge(x_in, 48)
            for i in range(6):
                b, n = init_use("x", i)
                begin(b, n)
                t, h = i // 2, i % 2
                for k in range(4):
                    last = pe.transpose(ps[:, b, k * P:(k + 1) * P], nat[:, t, (4 * h + k) * P:(4 * h + k + 1) * P], ident[:])
                last.then_inc(full[b], 1)
            pe.wait_ge(c_in, 48)
            pe.wait_ge(chain_p, 8)
            pe.matmul(ps[:, 7, 0:24], crow[:, :], ident[0:24, 0:24], start=True, stop=True).then_inc(full[7], 1)
            pe.wait_ge(freed[7], 2)

            def moe_step(c_ring, f):
                free_at, full_s, landed_s, land_at, half_s, xg_s, xg_at = c_ring
                for which, b in ((0, 2), (1, 3)):
                    pe.wait_ge(f[b], free_at(b))
                    if which == 0:
                        pe.wait_ge(f[0], free_at(0))
                        pe.wait_ge(f[1], free_at(1))
                    for hh in range(2):
                        s = 2 * which + hh
                        pe.wait_ge(landed_s[s], land_at)
                        for k in range(KD):
                            last = pe.matmul(ps[:, b, hh * 256:(hh + 1) * 256], xgT[:, k, :],
                                             ring[s][:, k * 256:(k + 1) * 256], start=(k == 0), stop=(k == KD - 1))
                        last.then_inc(half_s if hh == 0 else full_s[b], 1)
                pe.wait_ge(xg_s, xg_at)
                for h in range(2):
                    for k in range(4):
                        last = pe.transpose(ps[:, h, k * P:(k + 1) * P], xg[:, (4 * h + k) * P:(4 * h + k + 1) * P], ident[:])
                    last.then_inc(full_s[h], 1)
                pe.wait_ge(f[3], free_at(3) + 1)
                pe.wait_ge(f[4], free_at(4))
                for k in range(KE):
                    last = pe.transpose(ps[:, 4, k * P:(k + 1) * P], hid[:, k * P:(k + 1) * P], ident[:])
                last.then_inc(full_s[4], 1)
                pe.wait_ge(f[4], free_at(4) + 1)
                for h in range(2):
                    pe.wait_ge(f[5 + h], free_at(5 + h))
                    pe.wait_ge(landed_s[4 + h], land_at)
                    for k in range(KE):
                        last = pe.matmul(ps[:, 5 + h, :], hidT[:, k, :], ring[4 + h][:, k * 512:(k + 1) * 512],
                                         start=(k == 0), stop=(k == KE - 1))
                    last.then_inc(full_s[5 + h], 1)

            def rms_sum(stage, l, q):
                b, n = use(stage, 0, l)
                begin(b, n)
                for k in range(KD):
                    pe.wait_ge(xsq, q * KD + (k + 1))
                    last = pe.matmul(ps[:, b, 0:T], ones[:], hT[:, k, :], start=(k == 0), stop=(k == KD - 1))
                last.then_inc(full[b], 1)

            with pe.Fori(0, DEPTH) as l:
                b, n = use("params", 0, l)
                begin(b, n)
                pe.wait_ge(par_in, l * 128 + 128)
                pe.matmul(ps[:, b, 0:76], prow[:, :], ident[0:76, 0:76], start=True, stop=True)
                pe.matmul(ps[:, b, 128:128 + CK * KC], dwrow[:, :], ident[0:CK * KC, 0:CK * KC],
                          start=True, stop=True).then_inc(full[b], 1)

                mb, mn = use("mod", 0, l)

                def mod_cols(g):
                    ab, an = use("ada", g, l)
                    pe.wait_ge(freed[ab], an + 1)
                    if g == 0:
                        begin(mb, mn)
                    for m in range(4):
                        last = pe.matmul(ps[:, mb, 2 * (4 * g + m):2 * (4 * g + m) + 2],
                                         modrow[:, g % 2, m * P:(m + 1) * P], sel[:, :], start=True, stop=True)
                    last.then_inc(full[mb] if g == 11 else modrow_used, 1)

                for g in range(12):
                    b, n = use("ada", g, l)
                    begin(b, n)
                    for cc in range(2):
                        chunk_in(2 * g + cc, l)
                        s = (2 * g + cc) % SLOTS
                        for k in range(4):
                            last = pe.matmul(ps[32 * k:32 * k + 32, b, :], condT[:, 4 * cc + k, :],
                                             ring[s][:, k * 512:(k + 1) * 512], start=(cc == 0), stop=(cc == 1))
                        last.then_inc(half if cc == 0 else full[b], 1)
                    if g >= 1:
                        mod_cols(g - 1)
                mod_cols(11)

                rms_sum("rms1", l, l * 2)

                for c in range(3):
                    chunk_in(24 + c, l)
                    for t in range(NT):
                        b, n = use("qkv", 3 * c + t, l)
                        begin(b, n)
                        for k in range(KD):
                            if c == 0 and t == 0:
                                pe.wait_ge(h_r, l * (4 * KD) + 2 * (k + 1))
                            last = pe.matmul(ps[:, b, 0:256], hT[:, k, t * P:(t + 1) * P],
                                             ring[c][:, k * 256:(k + 1) * 256], start=(k == 0), stop=(k == KD - 1))
                        last.then_inc(full[b], 1)

                def wide(stage, c0, m, l, k_tiles, per_chunk, rhs):
                    c = c0 + m // per_chunk
                    if m % per_chunk == 0:
                        chunk_in(c, l)
                    b, n = use(stage, m, l)
                    begin(b, n)
                    w = per_chunk * P
                    for k in range(k_tiles):
                        o = k * w + (m % per_chunk) * P
                        last = pe.matmul(ps[:, b, 0:T], ring[c % SLOTS][:, o:o + P], rhs(k),
                                         start=(k == 0), stop=(k == k_tiles - 1))
                    last.then_inc(full[b], 1)

                for m in range(2 * KC):
                    wide("u", 27, m, l, KD, 2, lambda k: hT[:, k, :])
                for m in range(2 * KD):
                    wide("gate", 31, m, l, KD, 2, lambda k: hT[:, k, :])

                pe.wait_ge(q_r, l + 1)
                for t in range(NT):
                    b, n = use("qT", t, l)
                    begin(b, n)
                    for p in range(4):
                        last = pe.transpose(ps[:, b, p * P:(p + 1) * P], qkv[:, t, p * P:(p + 1) * P], ident[:])
                    last.then_inc(full[b], 1)
                for i in range(2):
                    b, n = use("kT", i, l)
                    begin(b, n)
                    for j in range(4):
                        last = pe.transpose(ps[:, b, j * P:(j + 1) * P], kdup[:, 2 * i + j // 2, j % 2, :], ident[:])
                    last.then_inc(full[b], 1)

                units = [(bk, p) for bk in range(NT) for p in range(4)]

                def scores(i):
                    bk, p = units[i]
                    if i == 0:
                        for st_, q in (("qT", 0), ("qT", 1), ("qT", 2), ("kT", 0), ("kT", 1)):
                            b, n = use(st_, q, l)
                            pe.wait_ge(freed[b], n + 1)
                    k0, nk = (0, P) if bk == 0 else (P, 3 * P)
                    for e in range(2):
                        b, n = use("scores", 2 * i + e, l)
                        begin(b, n)
                        pe.matmul(ps[:, b, 0:nk], qT[64 * e:64 * e + 64, p, bk * P:(bk + 1) * P],
                                  kT[64 * e:64 * e + 64, p // 2, k0:k0 + nk], start=True, stop=True).then_inc(full[b], 1)

                def turn_probs(i):
                    bk, p = units[i]
                    pe.wait_ge(p_r, l * 12 + (i + 1))
                    for e in range(2):
                        b, n = use("probsT", 2 * i + e, l)
                        begin(b, n)
                        for kt in range(1 if bk == 0 else 3):
                            last = pe.transpose(ps[:, b, kt * P:(kt + 1) * P], probs[:, i % 2, e, kt * P:(kt + 1) * P], ident[:])
                        last.then_inc(full[b], 1)

                def pv(i):
                    bk, p = units[i]
                    for e in range(2):
                        b, n = use("probsT", 2 * i + e, l)
                        pe.wait_ge(freed[b], n + 1)
                    b, n = use("pv", i, l)
                    begin(b, n)
                    g = p // 2
                    for e in range(2):
                        tiles = [qkv[:, 0, :]] if bk == 0 else [qkv[:, 1, :], qkv[:, 2, :], None]
                        for kt, v in enumerate(tiles):
                            vv = cache_v[:, g * HD:(g + 1) * HD] if v is None else v[:, 640 + g * HD:640 + (g + 1) * HD]
                            last = pe.matmul(ps[64 * e:64 * e + 64, b, 0:P], vv, probsT[:, e, kt, :],
                                             start=(kt == 0), stop=(kt == len(tiles) - 1))
                    last.then_inc(full[b], 1)

                scores(0)
                for i in range(12):
                    if i + 1 < 12:
                        scores(i + 1)
                    turn_probs(i)
                    pv(i)

                for i, (s, v) in enumerate(((tapped, l * (CK * KC) + CK * KC), (csq_r, l + 1))):
                    b, n = use("ln", i, l)
                    begin(b, n)
                    pe.wait_ge(s, v)
                    for k in range(KC):
                        last = pe.matmul(ps[:, b, 0:CO], ones[:], (conv if i == 0 else csq)[:, k, :],
                                         start=(k == 0), stop=(k == KC - 1))
                    last.then_inc(full[b], 1)
                    if i == 0:
                        for q in (10, 11):
                            pb, pn = use("pv", q, l)
                            pe.wait_ge(freed[pb], pn + 1)
                        for m in range(4):
                            wide("aproj", 39, m, l, KC, 4, lambda k: attnT[:, k, :])
                for m in range(4, KD):
                    wide("aproj", 39, m, l, KC, 4, lambda k: attnT[:, k, :])
                pe.wait_ge(convT_r, l * KC + KC)
                for m in range(KD):
                    wide("cproj", 41, m, l, KC, 4, lambda k: conv_tokens(k))
                for m in range(4):
                    b, n = use("cproj", 4 + m, l)
                    pe.wait_ge(freed[b], n + 1)
                for m in range(KD):
                    wide("out", 43, m, l, KD, 2, lambda k: hT[:, k, :])

                rms_sum("rms2", l, l * 2 + 1)
                b, n = use("logitsT", 0, l)
                begin(b, n)
                chunk_in(47, l)
                for k in range(KD):
                    pe.wait_ge(h_r, l * (4 * KD) + 2 * KD + 2 * (k + 1))
                    last = pe.matmul(ps[0:NE, b, 0:T], ring[5][:, k * NE:(k + 1) * NE], hT[:, k, :],
                                     start=(k == 0), stop=(k == KD - 1))
                last.then_inc(full[b], 1)

                def h2n(i):
                    b, n = use("h2n", i, l)
                    begin(b, n)
                    t, h = i // 2, i % 2
                    for k in range(4):
                        last = pe.transpose(ps[:, b, k * P:(k + 1) * P], hT[:, 4 * h + k, t * P:(t + 1) * P], ident[:])
                    last.then_inc(full[b], 1)

                h2n(0)
                h2n(1)
                b, n = use("logitsT", 0, l)
                pe.wait_ge(freed[b], n + 1)
                b, n = use("logits", 0, l)
                begin(b, n)
                for t in range(NT):
                    last = pe.matmul(ps[:, b, t * NE:(t + 1) * NE], lgT[:, t * P:(t + 1) * P], ident[0:NE, 0:NE],
                                     start=True, stop=True)
                last.then_inc(full[b], 1)
                for i in range(2, 6):
                    h2n(i)
                pe.wait_ge(route_r, l + 1)
                b, n = use("rank", 0, l)
                begin(b, n)
                for t in range(NT):
                    for i in range(t + 1):
                        pe.matmul(ps[:, b, t * NE:(t + 1) * NE], before[:] if i == t else ones[:], ra[:, i, :],
                                  start=(i == 0), stop=(i == t))
                for i in range(NT):
                    last = pe.matmul(ps[:, b, NT * NE:(NT + 1) * NE], ones[:], ra[:, i, :], start=(i == 0), stop=(i == NT - 1))
                last.then_inc(full[b], 1)

                pe.wait_ge(xg_in, l * (16 * (NE + 2)) + 16)
                for h in range(2):
                    b, n = use("xT0", h, l)
                    begin(b, n)
                    for k in range(4):
                        last = pe.transpose(ps[:, b, k * P:(k + 1) * P], xg[:, (4 * h + k) * P:(4 * h + k + 1) * P], ident[:])
                    last.then_inc(full[b], 1)
                with pe.Fori(0, NE) as e:
                    moe_step((lambda b: l * PER[b] + e + (INIT[b] + MOE_AT[b]), full, landed,
                              l * (16 * SLOT_USES) + e * 16 + 16 * 9, half,
                              xg_in, l * (16 * (NE + 2)) + e * 16 + 32), freed)

                over = pe.value_load(overfull[0:1, 0:1], min_val=0, max_val=1)
                with pe.If(over > 0):
                    for b in MOE_BANKS:
                        pe.wait_ge(freed[b], l * PER[b] + (INIT[b] + MOE_AT[b] + NE))
                    pe.wait_ge(xg_in_o, l * (16 * (OSTEPS + 2)) + 16)
                    for h in range(2):
                        for k in range(4):
                            last = pe.transpose(ps[:, h, k * P:(k + 1) * P], xg[:, (4 * h + k) * P:(4 * h + k + 1) * P], ident[:])
                        last.then_inc(full_o[h], 1)
                    with pe.Fori(0, OSTEPS) as i:
                        moe_step((lambda b: (l * (OSTEPS + 1) + i + 2) if b < 2 else l * OSTEPS + i + 1, full_o, landed_o,
                                  l * (16 * OSTEPS) + i * 16 + 16, half_o,
                                  xg_in_o, l * (16 * (OSTEPS + 2)) + i * 16 + 32), freed_o)
                with pe.Else():
                    for b in MOE_BANKS:
                        pe.sem_inc(full_o[b], OSTEPS + 1 if b < 2 else OSTEPS)
                    pe.sem_inc(half_o, 2 * OSTEPS)
                pe.nop()

                for i in range(6):
                    b, n = use("y", i, l)
                    begin(b, n)
                    t, h = i // 2, i % 2
                    if i == 0:
                        for q in range(7):
                            pe.wait_ge(freed_o[q], l * (OSTEPS + 1) + (OSTEPS + 2) if q < 2 else l * OSTEPS + (OSTEPS + 1))
                    if h == 0:
                        pe.wait_ge(comb_r, l * NT + (t + 1))
                    for k in range(4):
                        last = pe.transpose(ps[:, b, k * P:(k + 1) * P], nat[:, t, (4 * h + k) * P:(4 * h + k + 1) * P], ident[:])
                    last.then_inc(full[b], 1)

            pe.wait_ge(freed[3], DEPTH * PER[3] + INIT[3])
            for k in range(KD):
                pe.wait_ge(xsq, 2 * DEPTH * KD + k + 1)
                last = pe.matmul(ps[:, 3, 0:T], ones[:], hT[:, k, :], start=(k == 0), stop=(k == KD - 1))
            last.then_inc(full[3], 1)
            pe.wait_ge(h_r, DEPTH * 4 * KD + KD)
            for i in range(6):
                b = i % 3
                pe.wait_ge(freed[b], DEPTH * PER[b] + INIT[b] + i // 3)
                t, h = i // 2, i % 2
                for k in range(4):
                    last = pe.transpose(ps[:, b, k * P:(k + 1) * P], hT[:, 4 * h + k, t * P:(t + 1) * P], ident[:])
                last.then_inc(full[b], 1)

        @block.scalar
        def _(act):
            for t in range(NT):
                src = A["x_prompt"][0] if t == 0 else A["x_sample"][0, (t - 1) * P:t * P, :]
                act.dma_start(nat[:, t, :], src).then_inc(x_in, 16)
            act.dma_start(crow[0:8, :], A["c_ctx"].rearrange("(k p) -> k p", p=P)).then_inc(c_in, 16)
            act.dma_start(crow[8:16, :], A["c"].rearrange("o (k p) -> (o k) p", p=P)).then_inc(c_in, 16)
            act.dma_start(crow[16:24, :], A["final_norm"].rearrange("(k p) -> k p", p=P)).then_inc(c_in, 16)
            act.dma_start(rope[:], A["rope"].rearrange("(t p) c d -> p t c d", p=P)).then_inc(t_in, 16)
            act.dma_start(rbias[:], A["router_bias"].rearrange("(o n) -> o n", o=1).broadcast_to([P, NE])).then_inc(t_in, 16)
            act.wait_ge(zeroed, 1)
            for r in range(BLOCKS):
                for dst in (rows_in, rows_out):
                    act.dma_start(dst[ROWS + r * P:ROWS + (r + 1) * P, :], orow).then_inc(scratch0, 16)
            act.wait_ge(full[7], 2)
            act.activation(csig[:], ps[:, 7, 0:16], ACT.Sigmoid).then_inc(csig_r, 1)

            def squares(q):
                for k in range(KD):
                    act.activation(hT[:, k, :], xT[:, k, :], ACT.Square).then_inc(xsq, 1)

            def root(bank, n):
                act.wait_ge(full[bank], n + 1)
                act.activation(rms[:], ps[:, bank, 0:T], ACT.Sqrt, scale=1.0 / D, bias=eps[:]).then_inc(freed[bank], 1)

            def affine(q, which):
                for k in range(KD):
                    act.wait_ge(xn_r, q * KD + (k + 1))
                    for c, (a, z) in enumerate(((0, TC), (TC, T))):
                        sh = 24 * which + k
                        act.activation(hT[:, k, a:z], hT[:, k, a:z], ACT.Identity, scale=coef[:, which, k, c:c + 1],
                                       bias=mod[:, sh, c:c + 1]).then_inc(h_r, 1)

            act.wait_ge(freed[0], INIT[0])
            act.wait_ge(freed[1], INIT[1])
            act.wait_ge(consts_v, 1)

            def moe_act(fs, fr, n_of, xg_s, wr_s, wr_at, row, row2):
                act.wait_ge(fs[2], n_of(2) + 1)
                act.wait_ge(fr[3], n_of(3))
                act.activation(silu, ps[:, 2, :], ACT.Silu).then_inc(fr[2], 1)
                for h in range(2):
                    act.wait_ge(fs[h], n_of(h) + 1)
                    if h == 0:
                        act.wait_ge(fs[3], n_of(3) + 1)
                    act.activation(xgT[:, 4 * h:4 * h + 4, :], ps[:, h, :].rearrange("p (k n) -> p k n", k=4),
                                   ACT.Copy).then_inc(fr[h], 1)
                act.dma_start(xg, rows_in[bass.ds(row2, P), :]).then_inc(xg_s, 16)
                act.wait_ge(wr_s, wr_at)
                for h in range(2):
                    act.wait_ge(fs[5 + h], n_of(5 + h) + 1)
                    act.activation(orow[:, h * 512:(h + 1) * 512], ps[:, 5 + h, :], ACT.Copy).then_inc(fr[5 + h], 1)
                for h in range(2):
                    act.wait_ge(fr[5 + h], n_of(5 + h) + 1)
                act.dma_start(rows_out[bass.ds(row, P), :], orow).then_inc(wr_s, 16)

            with act.Fori(0, DEPTH) as l:
                act.wait_ge(full[7], l * PER[7] + INIT[7])
                pr = [("b_ada", 48), ("norm1", 8), ("norm2", 8), ("dw_b", 4), ("cln_g", 4), ("cln_b", 4)]
                at = 0
                for name, n in pr:
                    act.dma_start(prow[at:at + n, :], A[name][bass.ds(l, 1), :].rearrange("o (k p) -> (o k) p", p=P)
                                  ).then_inc(par_in, 16)
                    at += n
                act.dma_start(dwrow[:, :], A["dw_w"][bass.ds(l, 1), :, :].rearrange("o t (j p) -> (o t j) p", p=P)
                              ).then_inc(par_in, 16)
                act.dma_start(cache_v[:], A["cache_v"][0, bass.ds(l, 1)].rearrange("o t h d -> (o t) (h d)")).then_inc(par_in, 16)
                act.dma_start(qkn[:, 0, :], A["q_norm"][bass.ds(l, 1), :].broadcast_to([P, HD])).then_inc(bc_in, 16)
                act.dma_start(qkn[:, 1, :], A["k_norm"][bass.ds(l, 1), :].broadcast_to([P, HD])).then_inc(bc_in, 16)
                act.dma_start(sinkb[:], A["sink"][bass.ds(l, 1), :].broadcast_to([P, NH])).then_inc(bc_in, 16)
                act.dma_start(cache_k[:], A["cache_k"][0, bass.ds(l, 1)].rearrange("o t h d -> (o t) (h d)")).then_inc(cache_in, 16)

                squares(l * 2)
                b, n = use("rms1", 0, l)
                root(b, n)
                act.wait_ge(mod_r, l + 1)
                affine(l * 2, 0)

                for i in range(9):
                    b, n = use("qkv", i, l)
                    act.wait_ge(full[b], n + 1)
                    c, t = i // 3, i % 3
                    act.activation(qkv[:, t, c * 256:(c + 1) * 256], ps[:, b, 0:256], ACT.Copy).then_inc(freed[b], 1)
                act.wait_ge(freed[6], use("qkv", 8, l)[1] + 1)
                act.wait_ge(freed[5], use("qkv", 7, l)[1] + 1)
                act.wait_ge(freed[4], use("qkv", 6, l)[1] + 1)
                act.activation(qtmp[:, :, :], qkv[:, :, 0:640], ACT.Square).then_inc(qsq_r, 1)
                act.wait_ge(qss_r, l + 1)
                act.activation(ss[:], ss[:], ACT.Sqrt, scale=1.0 / HD, bias=eps[:]).then_inc(qrms_r, 1)

                for i in range(KC, 2 * KC):
                    b, n = use("u", i, l)
                    act.wait_ge(full[b], n + 1)
                    j = i - KC
                    if j >= 2:
                        act.wait_ge(usig_used, l * KC + (j - 1))
                    act.activation(sig[:, j % 2, :], ps[:, b, 0:T], ACT.Sigmoid).then_inc(freed[b], 1)
                for i in range(2 * KD):
                    b, n = use("gate", i, l)
                    act.wait_ge(full[b], n + 1)
                    act.activation(gates[:, i, :], ps[:, b, 0:T], ACT.Sigmoid).then_inc(freed[b], 1)
                for t in range(NT):
                    b, n = use("qT", t, l)
                    act.wait_ge(full[b], n + 1)
                    act.activation(qT[:, :, t * P:(t + 1) * P], ps[:, b, :].rearrange("p (k n) -> p k n", k=4),
                                   ACT.Copy).then_inc(freed[b], 1)
                for i in range(2):
                    b, n = use("kT", i, l)
                    act.wait_ge(full[b], n + 1)
                    for j in range(2):
                        last = act.activation(kT[:, :, (2 * i + j) * P:(2 * i + j + 1) * P],
                                              ps[:, b, 2 * j * P:2 * (j + 1) * P].rearrange("p (g n) -> p g n", g=2), ACT.Copy)
                    last.then_inc(freed[b], 1)

                for i in range(12 + 1):
                    if i < 12:
                        nk = P if i < 4 else 3 * P
                        act.wait_ge(sm_max, l * 12 + (i + 1))
                        for e in range(2):
                            act.activation(probs[:, i % 2, e, 0:nk], probs[:, i % 2, e, 0:nk], ACT.Exp,
                                           bias=st[:, i % 2, e:e + 1], accum_out=st[:, i % 2, 4 + e:5 + e])
                        act.activation(st[:, i % 2, 2:4], st[:, i % 2, 2:4], ACT.Exp).then_inc(sm_exp, 1)
                    if i >= 1:
                        q = i - 1
                        nkt = 1 if q < 4 else 3
                        for e in range(2):
                            b, n = use("probsT", 2 * q + e, l)
                            act.wait_ge(full[b], n + 1)
                            if q >= 1:
                                vb, vn = use("pv", q - 1, l)
                                act.wait_ge(full[vb], vn + 1)
                            act.activation(probsT[:, e, 0:nkt, :], ps[:, b, 0:nkt * P].rearrange("p (k n) -> p k n", k=nkt),
                                           ACT.Copy).then_inc(freed[b], 1)
                        bk, p = q // 4, q % 4
                        b, n = use("pv", q, l)
                        act.wait_ge(full[b], n + 1)
                        act.activation(attnT[:, p, bk * P:(bk + 1) * P], ps[:, b, 0:P], ACT.Copy).then_inc(freed[b], 1)

                act.wait_ge(conv_c, l + 1)
                act.activation(csq[:], conv[:], ACT.Square).then_inc(csq_r, 1)
                b, n = use("ln", 1, l)
                act.wait_ge(full[b], n + 1)
                act.activation(mu[:], ps[:, b, 0:CO], ACT.Sqrt, scale=1.0 / CW, bias=eps[:]).then_inc(freed[b], 1)
                for k in range(KC):
                    act.wait_ge(cn_r, l * KC + (k + 1))
                    act.activation(csq[:, k, 0:TC], conv[:, k, 0:TC], ACT.Silu, scale=par[:, 68 + k:69 + k], bias=par[:, 72 + k:73 + k])
                    act.activation(csq[:, k, TC:T], conv[:, k, LAT0:LAT0 + TL], ACT.Silu, scale=par[:, 68 + k:69 + k],
                                   bias=par[:, 72 + k:73 + k]).then_inc(convT_r, 1)

                for q in range(4):
                    b, n = use("out", 4 + q, l)
                    act.wait_ge(freed[b], n + 1)
                squares(l * 2 + 1)
                b, n = use("rms2", 0, l)
                root(b, n)
                affine(l * 2 + 1, 1)
                for i in range(6):
                    b, n = use("h2n", i, l)
                    act.wait_ge(full[b], n + 1)
                    t, h = i // 2, i % 2
                    act.activation(nat[:, t, h * 512:(h + 1) * 512], ps[:, b, :], ACT.Copy).then_inc(freed[b], 1)
                    if i == 1:
                        b, n = use("logits", 0, l)
                        act.wait_ge(full[b], n + 1)
                        act.activation(sc[:], ps[:, b, 0:NT * NE].rearrange("p (t n) -> p t n", t=NT), ACT.Sigmoid).then_inc(freed[b], 1)

                act.wait_ge(scat, l * 96 + 96)
                act.wait_ge(scratch0, 96)
                act.dma_start(xg, rows_in[0:P, :]).then_inc(xg_in, 16)
                for h in range(2):
                    b, n = use("xT0", h, l)
                    act.wait_ge(full[b], n + 1)
                    act.activation(xgT[:, 4 * h:4 * h + 4, :], ps[:, b, :].rearrange("p (k n) -> p k n", k=4),
                                   ACT.Copy).then_inc(freed[b], 1)
                r1_ = act.value_load(row_at[0:1, 1:2], min_val=0, max_val=ROWS)
                act.dma_start(xg, rows_in[bass.ds(r1_, P), :]).then_inc(xg_in, 16)
                with act.Fori(0, NE) as e:
                    row = act.value_load(row_at[0:1, bass.ds(e, 1)], min_val=0, max_val=ROWS)
                    row2 = act.value_load(row_at[0:1, bass.ds(e + 2, 1)], min_val=0, max_val=ROWS)
                    moe_act(full, freed, lambda b: l * PER[b] + e + (INIT[b] + MOE_AT[b]),
                            xg_in, out_wr, l * (16 * NE) + e * 16 + 1, row, row2)
                act.wait_ge(out_wr, l * (16 * NE) + 16 * NE + 1)
                act.wait_ge(xg_in, l * (16 * (NE + 2)) + 16 * (NE + 2))
                settle(act)
                over = act.value_load(overfull[0:1, 0:1], min_val=0, max_val=1)
                with act.If(over > 0):
                    act.dma_start(xg, rows_in[0:P, :]).then_inc(xg_in_o, 16)
                    for h in range(2):
                        act.wait_ge(full_o[h], l * (OSTEPS + 1) + 2)
                        act.activation(xgT[:, 4 * h:4 * h + 4, :], ps[:, h, :].rearrange("p (k n) -> p k n", k=4),
                                       ACT.Copy).then_inc(freed_o[h], 1)
                    r1_ = act.value_load(orow_at[0:1, 1:2], min_val=0, max_val=ROWS + 2 * P)
                    act.dma_start(xg, rows_in[bass.ds(r1_, P), :]).then_inc(xg_in_o, 16)
                    with act.Fori(0, OSTEPS) as i:
                        row = act.value_load(orow_at[0:1, bass.ds(i, 1)], min_val=0, max_val=ROWS + 2 * P)
                        row2 = act.value_load(orow_at[0:1, bass.ds(i + 2, 1)], min_val=0, max_val=ROWS + 2 * P)
                        moe_act(full_o, freed_o, lambda b: (l * (OSTEPS + 1) + i + 2) if b < 2 else l * OSTEPS + i + 1,
                                xg_in_o, out_wr_o, l * (16 * OSTEPS) + i * 16 + 1, row, row2)
                    act.wait_ge(out_wr_o, l * (16 * OSTEPS) + 16 * OSTEPS + 1)
                    act.wait_ge(xg_in_o, l * (16 * (OSTEPS + 2)) + 16 * (OSTEPS + 2))
                    settle(act)
                with act.Else():
                    for b in (0, 1, 2, 5, 6):
                        act.sem_inc(freed_o[b], OSTEPS + 1 if b < 2 else OSTEPS)
                    act.sem_inc(xg_in_o, 16 * (OSTEPS + 2))
                    act.sem_inc(out_wr_o, 16 * OSTEPS)
                act.nop()
                act.wait_ge(kv_out, l * 32 + 32)
                for q in range(3):
                    b, n = use("y", 3 + q, l)
                    act.wait_ge(freed[b], n + 1)

            squares(2 * DEPTH)
            root(3, DEPTH * PER[3] + INIT[3])
            for k in range(KD):
                act.wait_ge(xn_r, 2 * DEPTH * KD + k + 1)
                act.activation(hT[:, k, :], hT[:, k, :], ACT.Copy, scale=fnorm[:, k:k + 1]).then_inc(h_r, 1)
            for i in range(6):
                b = i % 3
                act.wait_ge(full[b], DEPTH * PER[b] + INIT[b] + i // 3 + 1)
                t, h = i // 2, i % 2
                act.activation(nat[:, t, h * 512:(h + 1) * 512], ps[:, b, :], ACT.Copy).then_inc(freed[b], 1)
                if h == 1:
                    for j in (i - 1, i):
                        act.wait_ge(freed[j % 3], DEPTH * PER[j % 3] + INIT[j % 3] + j // 3 + 1)
                    dst = A["y_prompt"][0] if t == 0 else A["y_sample"][0, (t - 1) * P:t * P, :]
                    act.dma_start(dst, nat[:, t, :]).then_inc(y_out, 16)
            act.wait_ge(y_out, 48)

        @block.gpsimd
        def _(pool):
            pool.memset(orow, 0.0).then_inc(zeroed, 1)
            pool.memset(ident[:], 0.0).then_inc(chain_p, 1)
            pool.memset(ones[:], 1.0).then_inc(consts, 1)
            pool.memset(before[:], 1.0).then_inc(chain_p, 1)
            pool.memset(sel[:], 0.0).then_inc(chain_p, 1)
            pool.memset(mask[:], 0.0).then_inc(chain_p, 1)
            pool.wait_ge(chain_p, 4)
            pool.affine_select(out=ident[:], in_=ident[:], compare_op=ALU.not_equal, fill=1.0, base=0,
                               pattern=[[-1, P]], channel_multiplier=1).then_inc(consts, 1)
            pool.affine_select(out=before[:], in_=before[:], compare_op=ALU.is_gt, fill=0.0, base=0,
                               pattern=[[1, P]], channel_multiplier=-1).then_inc(consts, 1)
            pool.affine_select(out=mask[:, 0, 0:TL], in_=mask[:, 0, 0:TL], compare_op=ALU.is_ge, fill=NEG, base=P,
                               pattern=[[-1, TL]], channel_multiplier=1).then_inc(consts2, 1)
            pool.affine_select(out=mask[:, 1, 0:TL], in_=mask[:, 1, 0:TL], compare_op=ALU.is_ge, fill=NEG, base=0,
                               pattern=[[1, TL]], channel_multiplier=-1).then_inc(consts2, 1)
            for j in range(4):
                pool.affine_select(out=sel[:], in_=sel[:], compare_op=ALU.not_equal, fill=1.0, base=-32 * j,
                                   pattern=[[-1, 2]], channel_multiplier=1).then_inc(chain_p, 1)
                pool.wait_ge(chain_p, 5 + j)
            pool.iota(down_i[:], pattern=[[0, NT], [-1, NE]], base=NE, channel_multiplier=0,
                      allow_small_or_imprecise_dtypes=True).then_inc(consts2, 1)
            pool.iota(down_g[:], pattern=[[0, NT], [-1, NG]], base=NG, channel_multiplier=0,
                      allow_small_or_imprecise_dtypes=True).then_inc(consts2, 1)
            pool.memset(zero16[:], 0.0).then_inc(consts2, 1)

            with pool.Fori(0, DEPTH) as l:
                pool.wait_ge(k_pre, l + 1)
                pool.dma_start(A["new_k"][0, bass.ds(l, 1)].rearrange("o t h d -> (o t) (h d)"), qkv[:, 0, 512:640]).then_inc(kv_out, 16)
                pool.dma_start(A["new_v"][0, bass.ds(l, 1)].rearrange("o t h d -> (o t) (h d)"), qkv[:, 0, 640:768]).then_inc(kv_out, 16)

                pool.wait_ge(pos_r, l + 1)
                for b in range(3):
                    n = use("h2n", 3 + b, l)[1]
                    pool.wait_ge(freed[USES["h2n"][3 + b][0]], n + 1)
                settle(pool)
                for t in range(NT):
                    for j in range(2):
                        pool.indirect_dma_start(out=rows_in[:, :], out_offset=bass.IndirectOffsetOnAxis(ap=pos[:, j, t:t + 1], axis=0),
                                                in_=nat[:, t, :], in_offset=None).then_inc(scat, 16)
                pool.wait_ge(out_wr, l * (16 * NE) + 16 * NE + 1)
                pool.wait_ge(out_wr_o, l * (16 * OSTEPS) + 16 * OSTEPS + 1)
                settle(pool)
                for t in range(NT):
                    for j in range(2):
                        pool.indirect_dma_start(out=gath[:, 2 * t + j, :], out_offset=None, in_=rows_out[:, :],
                                                in_offset=bass.IndirectOffsetOnAxis(ap=pos[:, j, t:t + 1], axis=0)
                                                ).then_inc(gat[t], 16)
            pool.wait_ge(kv_out, 32 * DEPTH)

        @block.vector
        def _(dve):
            steps = [0]
            layer = [None]

            def link(ins):
                steps[0] += 1
                ins.then_inc(chain, 1)
                dve.wait_ge(chain, (layer[0] * CHAIN + steps[0]) if layer[0] is not None else steps[0])

            BASE = 4
            link(dve.memset(condT[:], 0.0))
            link(dve.memset(ub[:], 0.0))
            link(dve.memset(posf[:], 0.0))
            link(dve.memset(orowsf[:], float(ROWS)))
            dve.memset(eps[:], EPS).then_inc(consts_v, 1)
            for i in range(6):
                b, n = init_use("x", i)
                t, h = i // 2, i % 2
                dve.wait_ge(full[b], n + 1)
                dve.tensor_copy(xT[:, 4 * h:4 * h + 4, t * P:(t + 1) * P],
                                ps[:, b, :].rearrange("p (k n) -> p k n", k=4)).then_inc(freed[b], 1)
            dve.wait_ge(csig_r, 1)
            for c in range(2):
                dve.tensor_tensor(condT[:, :, c], ps[:, 7, 8 * c:8 * c + 8], csig[:, 8 * c:8 * c + 8], ALU.mult)
            dve.tensor_copy(fnorm[:], ps[:, 7, 16:24]).then_inc(freed[7], 1)
            dve.wait_ge(consts2, 5)
            dve.wait_ge(t_in, 32)
            assert steps[0] == BASE
            steps[0] = 0

            def ready(ins, s, value):
                ins.then_inc(s, 1)
                dve.wait_ge(s, value)

            def norm_tiles(q):
                for k in range(KD):
                    dve.tensor_tensor(hT[:, k, :], xT[:, k, :], rstd[:], ALU.mult).then_inc(xn_r, 1)

            def moe_dve(fs, fr, n_of):
                dve.wait_ge(fr[2], n_of(2) + 1)
                dve.wait_ge(fs[3], n_of(3) + 1)
                dve.wait_ge(fs[4], n_of(4))
                dve.tensor_tensor(hid, silu, ps[:, 3, :], ALU.mult).then_inc(fr[3], 1)
                dve.wait_ge(fs[4], n_of(4) + 1)
                dve.wait_ge(fs[6], n_of(6))
                dve.tensor_copy(hidT, ps[:, 4, :].rearrange("p (k n) -> p k n", k=KE)).then_inc(fr[4], 1)

            with dve.Fori(0, DEPTH) as l:
                def link(ins):
                    steps[0] += 1
                    ins.then_inc(chain, 1)
                    dve.wait_ge(chain, l * CHAIN + (BASE + steps[0]))

                b, n = use("params", 0, l)
                dve.wait_ge(full[b], n + 1)
                dve.tensor_copy(par[:], ps[:, b, 0:76])
                ready(dve.tensor_copy(dw[:], ps[:, b, 128:128 + CK * KC]), freed[b], n + 1)
                dve.wait_ge(bc_in, l * 48 + 48)
                dve.tensor_scalar(nsink[:], sinkb[:], -1.0, None, ALU.mult)

                for g in range(12):
                    b, n = use("ada", g, l)
                    dve.wait_ge(full[b], n + 1)
                    if g >= 2:
                        dve.wait_ge(modrow_used, l * 11 + (g - 1))
                    else:
                        dve.wait_ge(full[2], l * PER[2] + INIT[2])
                    dve.tensor_copy(modrow[:, g % 2, :], ps[:, b, :]).then_inc(freed[b], 1)

                b, n = use("rms1", 0, l)
                dve.wait_ge(freed[b], n + 1)
                link(dve.reciprocal(rstd[:], rms[:]))
                norm_tiles(l * 2)

                b, n = use("mod", 0, l)
                dve.wait_ge(full[b], n + 1)
                ready(dve.tensor_tensor(mod[:], ps[:, b, 0:96].rearrange("p (m c) -> p m c", c=2),
                                        par[:, 0:48].unsqueeze(2).to_broadcast([P, 48, 2]), ALU.add), freed[b], n + 1)
                for w in range(2):
                    for c in range(2):
                        last = dve.scalar_tensor_tensor(coef[:, w, :, c], mod[:, 24 * w + 8:24 * w + 16, c], 1.0,
                                                        par[:, 48 + 8 * w:56 + 8 * w], ALU.add, ALU.mult)
                last.then_inc(mod_r, 1)

                dve.wait_ge(qsq_r, l + 1)
                dve.tensor_reduce(ss[:], qtmp[:].rearrange("p t (h d) -> p (t h) d", d=HD), AX.X, ALU.add).then_inc(qss_r, 1)
                dve.wait_ge(qrms_r, l + 1)
                link(dve.reciprocal(ss[:], ss[:]))
                for t in range(NT):
                    qk = qkv[:, t, 0:640].rearrange("p (h d) -> p h d", d=HD)
                    tmp = qtmp[:, t, :].rearrange("p (h d) -> p h d", d=HD)
                    link(dve.tensor_tensor(tmp, qk, ss[:, 10 * t:10 * t + 10].unsqueeze(2).to_broadcast([P, 10, HD]), ALU.mult))
                    dve.tensor_tensor(qk[:, 0:NH, :], tmp[:, 0:NH, :], qkn[:, 0:1, :].to_broadcast([P, NH, HD]), ALU.mult)
                    i2 = dve.tensor_tensor(qk[:, NH:10, :], tmp[:, NH:10, :], qkn[:, 1:2, :].to_broadcast([P, 2, HD]), ALU.mult)
                    if t == 0:
                        ready(i2, k_pre, l + 1)
                    else:
                        link(i2)
                for t in range(1, NT):
                    qk = qkv[:, t, 0:640].rearrange("p (h d) -> p h d", d=HD)
                    tmp = qtmp[:, t, :].rearrange("p (h d) -> p h d", d=HD)
                    dve.tensor_tensor(tmp, qk, rope[:, t - 1, 0:1, :].to_broadcast([P, 10, HD]), ALU.mult)
                    t2 = qtmp2[:, t - 1, :].rearrange("p (h a s i) -> p h a s i", h=10, a=2, s=2)
                    qs = qkv[:, t, 0:640].rearrange("p (h a s i) -> p h a s i", h=10, a=2, s=2)
                    sn = rope[:, t - 1, 1:2, :].rearrange("p o (a s i) -> p o a s i", a=2, s=2)
                    for s_ in range(2):
                        for a_ in range(2):
                            last = dve.tensor_tensor(t2[:, :, a_, s_, :], qs[:, :, a_, 1 - s_, :],
                                                     sn[:, :, a_, s_, :].to_broadcast([P, 10, 16]), ALU.mult)
                    link(last)
                    link(dve.tensor_tensor(qk, tmp, qtmp2[:, t - 1, :].rearrange("p (h d) -> p h d", d=HD), ALU.add))
                dve.wait_ge(cache_in, l * 16 + 16)
                for t in range(4):
                    src = cache_k[:].rearrange("p (g d) -> p g d", g=2) if t == 3 else \
                        qkv[:, t, 512:640].rearrange("p (g d) -> p g d", g=2)
                    last = dve.tensor_copy(kdup[:, t, :, :].rearrange("p g (u d) -> p g u d", u=2),
                                           src.unsqueeze(2).to_broadcast([P, 2, 2, HD]))
                last.then_inc(q_r, 1)

                for i in range(KC):
                    b, n = use("u", i, l)
                    dve.wait_ge(full[b], n + 1)
                    dve.tensor_copy(ub[:, i, PAD:PAD + TC], ps[:, b, 0:TC])
                    ready(dve.tensor_copy(ub[:, i, SEG + PAD:SEG + PAD + TL], ps[:, b, TC:T]), freed[b], n + 1)
                for i in range(KC):
                    b, n = use("u", KC + i, l)
                    dve.wait_ge(freed[b], n + 1)
                    dve.tensor_tensor(ub[:, i, PAD:PAD + TC], ub[:, i, PAD:PAD + TC], sig[:, i % 2, 0:TC], ALU.mult)
                    u0 = SEG + PAD
                    ready(dve.tensor_tensor(ub[:, i, u0:u0 + TL], ub[:, i, u0:u0 + TL], sig[:, i % 2, TC:T], ALU.mult),
                          usig_used, l * KC + (i + 1))
                for j in range(CK):
                    for i in range(KC):
                        src = ub[:, i, j:j + CO]
                        w = dw[:, j * KC + i:j * KC + i + 1]
                        if j == 0:
                            dve.tensor_scalar(conv[:, i, :], src, w, par[:, 64 + i:65 + i], ALU.mult, ALU.add).then_inc(tapped, 1)
                        else:
                            dve.wait_ge(tapped, l * (CK * KC) + ((j - 1) * KC + i + 1))
                            dve.scalar_tensor_tensor(conv[:, i, :], src, w, conv[:, i, :], ALU.mult, ALU.add).then_inc(tapped, 1)

                def soft_a(i):
                    bk, p = i // 4, i % 4
                    nk = P if bk == 0 else 3 * P
                    bs = [use("scores", 2 * i + e, l) for e in range(2)]
                    for b, n in bs:
                        dve.wait_ge(full[b], n + 1)
                    if i >= 2:
                        for e in range(2):
                            tb, tn = use("probsT", 2 * (i - 2) + e, l)
                            dve.wait_ge(full[tb], tn + 1)
                    b0 = bs[0][0]
                    pr_ = probs[:, i % 2, :, 0:nk]
                    if bk == 0:
                        ins = dve.tensor_scalar(pr_, ps[:, b0:b0 + 2, 0:nk], HD ** -0.5, None, ALU.mult)
                    else:
                        ins = dve.scalar_tensor_tensor(pr_, ps[:, b0:b0 + 2, 0:nk], HD ** -0.5,
                                                       mask[:, bk - 1:bk, :].to_broadcast([P, 2, nk]), ALU.mult, ALU.add)
                    ready(ins, freed[b0], bs[0][1] + 1)
                    dve.sem_inc(freed[b0 + 1], 1)
                    s_ = st[:, i % 2, :]
                    link(dve.tensor_reduce(s_[:, 6:8], pr_, AX.X, ALU.max))
                    link(dve.scalar_tensor_tensor(s_[:, 0:2], s_[:, 6:8], -1.0, nsink[:, 2 * p:2 * p + 2], ALU.mult, ALU.min))
                    dve.tensor_tensor(s_[:, 2:4], s_[:, 0:2], sinkb[:, 2 * p:2 * p + 2], ALU.add).then_inc(sm_max, 1)

                def soft_b(i):
                    nk = P if i < 4 else 3 * P
                    s_ = st[:, i % 2, :]
                    dve.wait_ge(sm_exp, l * 12 + (i + 1))
                    link(dve.tensor_tensor(s_[:, 6:8], s_[:, 2:4], s_[:, 4:6], ALU.add))
                    link(dve.reciprocal(s_[:, 6:8], s_[:, 6:8]))
                    for e in range(2):
                        last = dve.tensor_scalar(probs[:, i % 2, e, 0:nk], probs[:, i % 2, e, 0:nk], s_[:, 6 + e:7 + e], None, ALU.mult)
                    last.then_inc(p_r, 1)

                soft_a(0)
                for i in range(12):
                    if i + 1 < 12:
                        soft_a(i + 1)
                    soft_b(i)

                b, n = use("ln", 0, l)
                dve.wait_ge(full[b], n + 1)
                ready(dve.tensor_scalar(mu[:], ps[:, b, 0:CO], 1.0 / CW, None, ALU.mult), freed[b], n + 1)
                dve.tensor_tensor(conv[:], conv[:], mu[:].unsqueeze(1).to_broadcast([P, KC, CO]), ALU.subtract).then_inc(conv_c, 1)
                def aproj(m):
                    b, n = use("aproj", m, l)
                    dve.wait_ge(full[b], n + 1)
                    dve.tensor_tensor(hT[:, m, :], ps[:, b, 0:T], gates[:, m, :], ALU.mult).then_inc(freed[b], 1)
                for m in range(4):
                    aproj(m)
                b, n = use("ln", 1, l)
                dve.wait_ge(freed[b], n + 1)
                link(dve.reciprocal(mu[:], mu[:]))
                for k in range(KC):
                    dve.tensor_tensor(conv[:, k, :], conv[:, k, :], mu[:], ALU.mult).then_inc(cn_r, 1)
                for m in range(4, KD):
                    aproj(m)
                for m in range(KD):
                    b, n = use("cproj", m, l)
                    dve.wait_ge(full[b], n + 1)
                    if m == 0:
                        for q in range(4, KD):
                            ab, an = use("aproj", q, l)
                            dve.wait_ge(freed[ab], an + 1)
                    link(dve.tensor_tensor(mixtmp[:, m % 2, :], ps[:, b, 0:T], gates[:, KD + m, :], ALU.mult))
                    dve.tensor_tensor(hT[:, m, :], hT[:, m, :], mixtmp[:, m % 2, :], ALU.add).then_inc(freed[b], 1)
                for m in range(KD):
                    b, n = use("out", m, l)
                    dve.wait_ge(full[b], n + 1)
                    dve.scalar_tensor_tensor(xT[:, m, 0:TC], ps[:, b, 0:TC], mod[:, 16 + m, 0:1], xT[:, m, 0:TC], ALU.mult, ALU.add)
                    dve.scalar_tensor_tensor(xT[:, m, TC:T], ps[:, b, TC:T], mod[:, 16 + m, 1:2], xT[:, m, TC:T],
                                             ALU.mult, ALU.add).then_inc(freed[b], 1)
                b, n = use("rms2", 0, l)
                dve.wait_ge(freed[b], n + 1)
                link(dve.reciprocal(rstd[:], rms[:]))
                norm_tiles(l * 2 + 1)

                b, n = use("logitsT", 0, l)
                dve.wait_ge(full[b], n + 1)
                dve.tensor_copy(lgT[:], ps[0:NE, b, 0:T]).then_inc(freed[b], 1)
                b, n = use("logits", 0, l)
                dve.wait_ge(freed[b], n + 1)
                link(dve.tensor_tensor(se[:], sc[:], rbias[:].unsqueeze(1).to_broadcast([P, NT, NE]), ALU.add))
                s4 = se[:].rearrange("p t (g e) -> p (t g) e", e=EG)
                q = 0
                for a_ in range(EG):
                    for b_ in range(a_ + 1, EG):
                        last = dve.tensor_tensor(pair[:, :, q], s4[:, :, a_], s4[:, :, b_], ALU.add)
                        q += 1
                link(last)
                gsf = gs[:].rearrange("p t g -> p (t g)")
                link(dve.tensor_reduce(gsf, pair[:], AX.X, ALU.max))

                def first_max(out, x, tmp, downs, width):
                    link(dve.tensor_reduce(r1[:], x, AX.X, ALU.max))
                    link(dve.tensor_tensor(tmp, x, r1[:].unsqueeze(2).to_broadcast([P, NT, width]), ALU.is_equal))
                    link(dve.tensor_tensor(tmp, tmp, downs, ALU.mult))
                    link(dve.tensor_reduce(r1[:], tmp, AX.X, ALU.max))
                    link(dve.tensor_tensor(out, tmp, r1[:].unsqueeze(2).to_broadcast([P, NT, width]), ALU.is_equal))

                first_max(gt[:], gs[:], gs[:], down_g[:], NG)
                g4 = gt[:].rearrange("p t g -> p (t g)").unsqueeze(2).to_broadcast([P, NT * NG, EG])
                ra4 = ra[:].rearrange("p t (g e) -> p (t g) e", e=EG)
                rb4 = rb[:].rearrange("p t (g e) -> p (t g) e", e=EG)
                link(dve.tensor_tensor(rb4, s4, g4, ALU.mult))
                link(dve.tensor_scalar(ra4, g4, -NEG, NEG, ALU.mult, ALU.add))
                link(dve.tensor_tensor(ra[:], ra[:], rb[:], ALU.add))
                first_max(m1[:], ra[:], rb[:], down_i[:], NE)
                link(dve.scalar_tensor_tensor(ra[:], m1[:], 4 * NEG, ra[:], ALU.mult, ALU.add))
                first_max(m2[:], ra[:], rb[:], down_i[:], NE)
                dve.tensor_tensor(ra[:], m1[:], m2[:], ALU.add).then_inc(route_r, 1)
                for j, m_ in enumerate((m1, m2)):
                    link(dve.tensor_tensor(rb[:], sc[:], m_[:], ALU.mult))
                    link(dve.tensor_reduce(wk[:, j, :], rb[:], AX.X, ALU.add))
                link(dve.tensor_tensor(ws[:], wk[:, 0, :], wk[:, 1, :], ALU.add))
                link(dve.reciprocal(ws[:], ws[:]))
                dve.tensor_tensor(wk[:, 0, :], wk[:, 0, :], ws[:], ALU.mult)
                link(dve.tensor_tensor(wk[:, 1, :], wk[:, 1, :], ws[:], ALU.mult))
                b, n = use("rank", 0, l)
                dve.wait_ge(full[b], n + 1)
                link(dve.tensor_copy(cnt[:], ps[:, b, NT * NE:(NT + 1) * NE]))
                link(dve.tensor_tensor_scan(off[:], cnt[:], zero16[:], 0.0, ALU.add, ALU.add))
                link(dve.tensor_tensor(off[:], off[:], cnt[:], ALU.subtract))
                ready(dve.tensor_tensor(rb[:], ps[:, b, 0:NT * NE].rearrange("p (t n) -> p t n", t=NT),
                                        off[:].unsqueeze(1).to_broadcast([P, NT, NE]), ALU.add), freed[b], n + 1)
                for j, m_ in enumerate((m1, m2)):
                    link(dve.tensor_tensor(se[:], rb[:], m_[:], ALU.mult))
                    link(dve.tensor_reduce(posf[:, j, :], se[:], AX.X, ALU.add))
                dve.memset(rowsf[:], float(ROWS))
                link(dve.memset(full_f[:], 0.0))
                dve.tensor_copy(rowsf[:, 0:NE], off[0:1, :])
                for q in range(BLOCKS):
                    dve.tensor_scalar(orowsf[:, 0:OSTEPS].rearrange("p (e q) -> p e q", q=BLOCKS)[:, :, q], off[0:1, :],
                                      float(q * P), None, ALU.add)
                link(dve.tensor_reduce(full_f[:], cnt[0:1, :], AX.X, ALU.max))
                link(dve.tensor_scalar(full_f[:], full_f[:], float(P), None, ALU.is_gt))
                dve.tensor_copy(pos[:], posf[:])
                dve.tensor_copy(row_at[:], rowsf[:])
                dve.tensor_copy(orow_at[:], orowsf[:])
                dve.tensor_copy(overfull[:], full_f[:]).then_inc(pos_r, 1)
                dve.wait_ge(pos_r, l + 1)
                settle(dve)

                with dve.Fori(0, NE) as e:
                    moe_dve(full, freed, lambda b: l * PER[b] + e + (INIT[b] + MOE_AT[b]))
                over = dve.value_load(overfull[0:1, 0:1], min_val=0, max_val=1)
                with dve.If(over > 0):
                    with dve.Fori(0, OSTEPS) as i:
                        moe_dve(full_o, freed_o, lambda b: l * OSTEPS + i + 1)
                with dve.Else():
                    for b in (3, 4):
                        dve.sem_inc(freed_o[b], OSTEPS)
                dve.nop()

                for t in range(NT):
                    dve.wait_ge(gat[t], l * 32 + 32)
                    link(dve.tensor_scalar(nat[:, t, :], gath[:, 2 * t, :], wk[:, 0, t:t + 1], None, ALU.mult))
                    dve.scalar_tensor_tensor(nat[:, t, :], gath[:, 2 * t + 1, :], wk[:, 1, t:t + 1], nat[:, t, :],
                                             ALU.mult, ALU.add).then_inc(comb_r, 1)
                for i in range(6):
                    b, n = use("y", i, l)
                    dve.wait_ge(full[b], n + 1)
                    t, h = i // 2, i % 2
                    for k in range(4):
                        kk = 4 * h + k
                        x_ = xT[:, kk, t * P:(t + 1) * P]
                        last = dve.scalar_tensor_tensor(x_, ps[:, b, k * P:(k + 1) * P], mod[:, 40 + kk, min(t, 1):min(t, 1) + 1],
                                                        x_, ALU.mult, ALU.add)
                    last.then_inc(freed[b], 1)
                assert steps[0] <= CHAIN, steps
                dve.sem_inc(chain, CHAIN - steps[0])

            dve.wait_ge(freed[3], DEPTH * PER[3] + INIT[3] + 1)
            dve.reciprocal(rstd[:], rms[:]).then_inc(chain, 1)
            dve.wait_ge(chain, DEPTH * CHAIN + BASE + 1)
            norm_tiles(2 * DEPTH)


INPUTS = ["x_prompt", "x_sample", "cache_k", "cache_v", "c", "c_ctx", "w_ada", "b_ada", "norm1", "norm2", "w_in",
          "q_norm", "k_norm", "sink", "w_attn_proj", "dw_w", "dw_b", "cln_g", "cln_b", "w_conv_proj", "w_out",
          "w_router", "router_bias", "w_e_gate", "w_e_up", "w_e_down", "final_norm"]
OUTPUTS = [("y_prompt", (1, TC, D)), ("y_sample", (1, TL, D)), ("new_k", (1, DEPTH, TC, NKV, HD)),
           ("new_v", (1, DEPTH, TC, NKV, HD))]


def kernel(**inputs):
    import numpy as np
    import concourse.bacc as bacc
    from concourse.bass_utils import run_bass_kernel_spmd as run

    nc = bacc.Bacc("TRN2", target_bir_lowering=False, num_devices=1)
    arrays = {name: np.ascontiguousarray(inputs[name]) for name in INPUTS}
    grid_w, pairs = 64, HD // 4
    inv = (np.float32(10000.0) ** (-np.arange(pairs, dtype=np.float32) / np.float32(pairs))).astype(np.float32)
    tok = np.arange(TL)
    halves = [(tok // grid_w).astype(np.float32)[:, None] * inv, (tok % grid_w).astype(np.float32)[:, None] * inv]
    cos = np.concatenate([np.cos(h) for h in halves for _ in range(2)], axis=1)
    sin = np.concatenate([s * np.sin(h) for h in halves for s in (-1, 1)], axis=1)
    arrays["rope"] = np.stack([cos, sin], axis=1).astype(np.float32)
    A = {}
    for name, a in arrays.items():
        A[name] = nc.dram_tensor("in_" + name, a.shape, mybir.dt.from_np(a.dtype), kind="ExternalInput").ap()
    for name, shape in OUTPUTS:
        A[name] = nc.dram_tensor("out_" + name, shape, F32, kind="ExternalOutput").ap()
    build(nc, A)
    r = run(nc, [{"in_" + name: a for name, a in arrays.items()}], core_ids=[0])
    return tuple(r.results[0]["out_" + name] for name, _ in OUTPUTS)
```

```python
from contextlib import ExitStack

import concourse.bass as bass
from concourse import mybir

F32 = mybir.dt.float32
I32 = mybir.dt.int32
ALU = mybir.AluOpType
ACT = mybir.ActivationFunctionType
AX = mybir.AxisListType

P = 128
D = 1024
KD = D // P
DEPTH = 2
TC, TL = 128, 256
T = TC + TL
NT = T // P
HD = 64
NH, NKV = 8, 2
AW, KVW = NH * HD, NKV * HD
CW = D // 2
KC = CW // P
CK, PAD = 31, 15
NE, NG, EG = 16, 4, 4
DE = 512
KE = DE // P
EPS = 1e-6
NEG = -1e30
SEG = TC + 2 * PAD
UW = SEG + TL + 2 * PAD
CO = UW - 2 * PAD
LAT0 = SEG
ROWS = 2 * T
BLOCKS = NT
SROWS = ROWS + BLOCKS * P

SLOTS = 6
SLOT = 2048
MOE_CHUNKS = 6
CHUNKS = [("ada", g, c) for g in range(4) for c in range(2)]
CHUNKS += [("qkv", c, 0) for c in range(3)] + [("u", c, 0) for c in range(4)]
for _g in range(8):
    CHUNKS += [("gate", _g, 0), ("ada", 4 + _g, 0), ("ada", 4 + _g, 1)]
CHUNKS += [("aproj", 0, 0), ("aproj", 1, 0), ("cproj", 0, 0), ("cproj", 1, 0)]
CHUNKS += [("out", c, 0) for c in range(4)] + [("router", 0, 0)]
CHUNK_AT = {c: i for i, c in enumerate(CHUNKS)}
NCHUNKS = len(CHUNKS)
assert NCHUNKS % SLOTS == 0
SLOT_USES = (NCHUNKS + MOE_CHUNKS * NE) // SLOTS

UNITS = NT * NH // 2
FILLERS = []
for _g in range(8):
    FILLERS += [("gate", 2 * _g), ("gate", 2 * _g + 1), ("ada2", _g)]
assert len(FILLERS) == 2 * UNITS


def attention_uses():
    uses = [("scores", [0, 1])]
    for i in range(UNITS):
        if i + 1 < UNITS:
            uses += [("scores", [0, 1])]
        uses += [(FILLERS[2 * i][0], [2]), ("probsT", [4, 5]), (FILLERS[2 * i + 1][0], [3]), ("pv", [6])]
    return uses


INIT_USES = [("x", [0, 1, 0, 1, 0, 1]), ("cond", [7])]
PRE_USES = [
    ("params", [7]), ("ada", [0, 1] * 2), ("mod", [2]), ("rms1", [3]),
    ("qkv", [4, 5, 6] * 3), ("u", [0, 1, 2, 3] * 2), ("qT", [4, 5, 6]), ("kT", [7, 4]),
    ("mod2", [7]), *attention_uses(), ("ln", [2, 4]), ("aproj", [0, 1, 2, 3] * 2), ("cproj", [4, 5, 6, 7] * 2),
    ("out", [0, 1, 2, 3] * 2), ("rms2", [4]), ("logitsT", [5]), ("h2n", [0, 1, 2] * 2),
    ("logits", [6]), ("rank", [7]), ("xT0", [0, 1]),
]
MOE_BANKS = (2, 3, 0, 1, 4, 5, 6)
POST_USES = [("y", [0, 1, 2] * 2)]


def bank_table():
    init = [0] * 8
    table = {}
    for stage, banks in INIT_USES:
        table[stage] = []
        for b in banks:
            table[stage].append((b, init[b]))
            init[b] += 1
    at = [0] * 8
    for stage, banks in PRE_USES:
        table.setdefault(stage, [])
        for b in banks:
            table[stage].append((b, at[b]))
            at[b] += 1
    moe = list(at)
    for b in MOE_BANKS:
        at[b] += NE
    for stage, banks in POST_USES:
        table[stage] = []
        for b in banks:
            table[stage].append((b, at[b]))
            at[b] += 1
    return table, [n + 1 for n in init], moe, at


def build(nc, A):
    USES, INIT, MOE_AT, PER = bank_table()
    ctx = ExitStack()
    with ctx:
        def sb(name, shape, dt=F32):
            return ctx.enter_context(nc.sbuf_tensor(name, shape, dt))

        def sem(name):
            return ctx.enter_context(nc.semaphore(name))

        rows_in = nc.dram_tensor("rows_in", (SROWS, D), F32, kind="Internal").ap()
        rows_out = nc.dram_tensor("rows_out", (SROWS, D), F32, kind="Internal").ap()

        ring = [sb(f"ring{s}", [P, SLOT]) for s in range(SLOTS)]
        xT = sb("xT", [P, KD, T])
        hT = sb("hT", [P, KD, T])
        nat = sb("nat", [P, NT, D])
        qkv = sb("qkv", [P, NT, 768])
        qtmp = sb("qtmp", [P, NT, 640])
        qtmp2 = sb("qtmp2", [P, 2, 640])
        kdup = sb("kdup", [P, 4, 2, P])
        qT = sb("qT", [P, 4, T])
        kT = sb("kT", [P, 2, 4 * P])
        cache_k = sb("cache_k_sb", [P, P])
        cache_v = sb("cache_v_sb", [P, P])
        ub = sb("ub", [P, KC, UW])
        sig = sb("sig", [P, 2, T])
        conv = sb("conv", [P, KC, CO])
        csq = sb("csq", [P, KC, CO])
        gates = sb("gates", [P, 2 * KD, T])
        squared = gates[:, 0:KD, :]
        gath = gates[:].rearrange("p a b -> p (a b)").rearrange("p (s n) -> p s n", n=D)
        attnT = sb("attnT", [P, 4, T])
        probs = sb("probs", [P, 2, 2, 3 * P])
        probsT = sb("probsT", [P, 2, 3, P])
        mixtmp = sb("mixtmp", [P, 2, T])
        rstd = sb("rstd", [P, T])
        rms = sb("rms", [P, T])
        mu = sb("mu", [P, CO])
        xg = csq[:].rearrange("p a b -> p (a b)")[:, 0:D]
        xgT = qtmp[:].rearrange("p a b -> p (a b)")[:, 0:D].rearrange("p (k n) -> p k n", k=KD)
        silu = qtmp[:].rearrange("p a b -> p (a b)")[:, D:D + DE]
        hid = csq[:].rearrange("p a b -> p (a b)")[:, D:D + DE]
        hidT = conv[:].rearrange("p a b -> p (a b)")[:, D:D + DE].rearrange("p (k n) -> p k n", k=KE)
        orow = conv[:].rearrange("p a b -> p (a b)")[:, 0:D]
        ident = sb("ident", [P, P])
        ones = sb("ones", [P, P])
        before = sb("before", [P, P])
        sel = sb("sel", [P, 2])
        mask = sb("mask", [P, 2, 3 * P])
        rope = sb("rope", [P, 2, 2, HD])
        eps = sb("eps", [P, 1])
        crow = sb("crow", [24, P])
        fnorm = sb("fnorm", [P, KD])
        condT = sb("condT", [P, KD, 32])
        csig = sb("csig", [P, 16])
        modrow = nat[:, 0, :].rearrange("p (i n) -> p i n", i=2)
        prow = sb("prow", [76, P])
        dwrow = sb("dwrow", [CK * KC, P])
        par = sb("par", [P, 76])
        dw = sb("dw", [P, CK * KC])
        mod = sb("mod", [P, 48, 2])
        coef = sb("coef", [P, 2, KD, 2])
        every = sb("every", [P, 2 * HD + NH])
        qkn = every[:, 0:2 * HD].rearrange("p (i d) -> p i d", i=2)
        sinkb = every[:, 2 * HD:]
        nsink = sb("nsink", [P, NH])
        rbias = sb("rbias", [P, NE])
        ss = sb("ss", [P, NT * 10])
        st = sb("st", [P, 2, 8])
        lgT = sb("lgT", [NE, T])
        sc = sb("sc", [P, NT, NE])
        se = sb("se", [P, NT, NE])
        m1 = sb("m1", [P, NT, NE])
        m2 = sb("m2", [P, NT, NE])
        ra = sb("ra", [P, NT, NE])
        rb = sb("rb", [P, NT, NE])
        pair = sb("pair", [P, NT * NG, 6])
        gs = sb("gs", [P, NT, NG])
        gt = sb("gt", [P, NT, NG])
        r1 = sb("r1", [P, NT])
        wk = sb("wk", [P, 2, NT])
        ws = sb("ws", [P, NT])
        cnt = sb("cnt", [P, NE])
        off = sb("off", [P, NE])
        down_i = sb("down_i", [P, NT, NE])
        down_g = sb("down_g", [P, NT, NG])
        zero16 = sb("zero16", [P, NE])
        posf = sb("posf", [P, 2, NT])
        pos = sb("pos", [P, 2, NT], I32)
        rowsf = sb("rowsf", [1, 18])
        orowsf = sb("orowsf", [1, 52])
        row_at = sb("row_at", [1, 18], I32)
        orow_at = sb("orow_at", [1, 52], I32)
        narrow_f = sb("narrow_f", [1, NE])
        narrow_e = sb("narrow_e", [1, NE], I32)
        full_f = sb("full_f", [1, 1])
        overfull = sb("overfull", [1, 1], I32)

        ps = ctx.enter_context(nc.psum_tensor("ps", [P, 8, 512], F32))

        landed = [sem(f"landed{s}") for s in range(SLOTS)]
        full = [sem(f"full{b}") for b in range(8)]
        freed = [sem(f"freed{b}") for b in range(8)]
        settled = sem("settled")
        half = sem("half")
        consts = sem("consts")
        consts_v = sem("consts_v")
        consts2 = sem("consts2")
        chain_p = sem("chain_p")
        x_in = sem("x_in")
        c_in = sem("c_in")
        t_in = sem("t_in")
        scratch0 = sem("scratch0")
        zeroed = sem("zeroed")
        par_in = sem("par_in")
        bc_in = sem("bc_in")
        cache_in = sem("cache_in")
        csig_r = sem("csig_r")
        modrow_used = sem("modrow_used")
        mod_r = sem("mod_r")
        xsq = sem("xsq")
        sq_added = sem("sq_added")
        sq_sum = sem("sq_sum")
        xn_r = sem("xn_r")
        h_r = sem("h_r")
        h_ctx = sem("h_ctx")
        usig_used = sem("usig_used")
        qsq_r = sem("qsq_r")
        qss_r = sem("qss_r")
        qrms_r = sem("qrms_r")
        k_pre = sem("k_pre")
        q_r = sem("q_r")
        kv_out = sem("kv_out")
        sm_max = sem("sm_max")
        sm_exp = sem("sm_exp")
        p_r = sem("p_r")
        conv_c = sem("conv_c")
        csq_r = sem("csq_r")
        cn_r = sem("cn_r")
        convT_r = sem("convT_r")
        route_r = sem("route_r")
        pos_r = sem("pos_r")
        scat = sem("scat")
        xg_in = sem("xg_in")
        out_wr = sem("out_wr")
        gat = [sem(f"gat{t}") for t in range(NT)]
        comb_r = sem("comb_r")
        chain = sem("chain")
        tapped = sem("tapped")
        y_out = sem("y_out")
        landed_o = [sem(f"landed_o{s}") for s in range(SLOTS)]
        full_o = [sem(f"full_o{b}") for b in range(7)]
        freed_o = [sem(f"freed_o{b}") for b in range(7)]
        half_o = sem("half_o")
        xg_in_o = sem("xg_in_o")
        out_wr_o = sem("out_wr_o")

        CHAIN = 200
        OSTEPS = NE * BLOCKS

        def use(stage, i, l):
            b, n = USES[stage][i]
            return b, l * PER[b] + (INIT[b] + n)

        def init_use(stage, i):
            b, n = USES[stage][i]
            return b, n + 1

        w_ada = A["w_ada"].rearrange("l (c k p) n -> l c p k n", c=2, p=P)
        w_in = A["w_in"].rearrange("l (k p) n -> l p k n", p=P)
        w_ap = A["w_attn_proj"].rearrange("l (k p) n -> l p k n", p=P)
        w_cp = A["w_conv_proj"].rearrange("l (k p) n -> l p k n", p=P)
        w_out = A["w_out"].rearrange("l (k p) n -> l p k n", p=P)
        w_r = A["w_router"].rearrange("(k p) n -> p k n", p=P)
        w_g = A["w_e_gate"].rearrange("l e (k p) n -> (l e) p k n", p=P)
        w_u = A["w_e_up"].rearrange("l e (k p) n -> (l e) p k n", p=P)
        w_d = A["w_e_down"].rearrange("l e (k p) n -> (l e) p k n", p=P)

        def chunk_end(c):
            kind, i, part = CHUNKS[c]
            if kind == "ada":
                return ("half", i) if part == 0 else (("ada", i) if i < 4 else ("ada2", i - 4))
            return {"qkv": ("qkv", 3 * i + 2), "u": ("u", 2 * i + 1), "gate": ("gate", 2 * i + 1),
                    "aproj": ("aproj", 4 * i + 3), "cproj": ("cproj", 4 * i + 3), "out": ("out", 2 * i + 1),
                    "router": ("logitsT", 0)}[kind]

        HALF_PER = 12 + 2 * NE

        def settle(eng):
            eng.sem_inc(settled, 1)

        with nc.Block() as start:
            @start.sync
            def _(sp):
                for s in [*full, *freed, half, out_wr, *full_o, *freed_o, half_o, out_wr_o]:
                    sp.sem_inc(s, 1)

        block = ctx.enter_context(nc.Block())

        @block.sync
        def _(sp):
            def wait_chunk_used(c, l):
                stage, i = chunk_end(c)
                if stage == "half":
                    sp.wait_ge(half, l * HALF_PER + (i + 2))
                else:
                    b, n = use(stage, i, l)
                    sp.wait_ge(full[b], n + 1)

            def load(slot, landed_sem, src):
                n = src.shape[-1]
                k = src.shape[-2]
                dst = ring[slot][:, 0:k * n].rearrange("p (k n) -> p k n", k=k)
                sp.dma_start(dst, src).then_inc(landed_sem, 16)

            def expert_chunk(j, w):
                if j < 4:
                    src = w_g if j < 2 else w_u
                    return src[bass.ds(w, 1), :, :, (j % 2) * 256:(j % 2 + 1) * 256].rearrange("o p k n -> p (o k) n")
                return w_d[bass.ds(w, 1), :, :, (j - 4) * 512:(j - 3) * 512].rearrange("o p k n -> p (o k) n")

            with sp.Fori(0, DEPTH) as l:
                for c in range(NCHUNKS):
                    s = c % SLOTS
                    if c < SLOTS:
                        if c in (0, 2):
                            sp.wait_ge(half, l * HALF_PER + 1)
                        else:
                            b = {1: 2, 3: 3, 4: 5, 5: 6}[c]
                            sp.wait_ge(full[b], l * PER[b] + INIT[b])
                    else:
                        wait_chunk_used(c - SLOTS, l)
                    kind, i, part = CHUNKS[c]
                    if kind == "ada":
                        src = w_ada[bass.ds(l, 1), part, :, :, i * 512:(i + 1) * 512].rearrange("o p k n -> p (o k) n")
                    elif kind in ("aproj", "cproj"):
                        w = w_ap if kind == "aproj" else w_cp
                        src = w[bass.ds(l, 1), :, :, i * 512:(i + 1) * 512].rearrange("o p k n -> p (o k) n")
                    elif kind == "router":
                        src = w_r
                    else:
                        w = w_out if kind == "out" else w_in
                        m = i + {"qkv": 0, "u": 3, "gate": 7, "out": 0}[kind]
                        src = w[bass.ds(l, 1), :, :, m * 256:(m + 1) * 256].rearrange("o p k n -> p (o k) n")
                    load(s, landed[s], src)
                for j in range(MOE_CHUNKS):
                    wait_chunk_used(NCHUNKS - SLOTS + j, l)
                    load(j, landed[j], expert_chunk(j, l * NE))
                with sp.Fori(1, NE) as e:
                    for j in range(MOE_CHUNKS):
                        if j in (0, 2):
                            sp.wait_ge(half, l * HALF_PER + e * 2 + (12 - 2 + (2 if j == 0 else 3)))
                        else:
                            b = {1: 2, 3: 3, 4: 5, 5: 6}[j]
                            sp.wait_ge(full[b], l * PER[b] + e + (INIT[b] + MOE_AT[b]))
                        load(j, landed[j], expert_chunk(j, l * NE + e))

                sp.wait_ge(pos_r, l + 1)
                settle(sp)
                over = sp.value_load(overfull[0:1, 0:1], min_val=0, max_val=1)
                sp.wait_ge(full[6], l * PER[6] + (INIT[6] + MOE_AT[6] + NE))
                settle(sp)
                with sp.If(over > 0):
                    with sp.Fori(0, NE) as e:
                        for bl in range(BLOCKS):
                            for j in range(MOE_CHUNKS):
                                if j in (0, 2):
                                    if bl == 0:
                                        sp.wait_ge(half_o, l * (2 * OSTEPS) + e * (2 * BLOCKS) + 1)
                                    else:
                                        sp.wait_ge(half_o, l * (2 * OSTEPS) + e * (2 * BLOCKS) + (2 * bl - 2 + (2 if j == 0 else 3)))
                                else:
                                    b = {1: 2, 3: 3, 4: 5, 5: 6}[j]
                                    sp.wait_ge(full_o[b], l * OSTEPS + e * BLOCKS + (bl + 1))
                                load(j, landed_o[j], expert_chunk(j, l * NE + e))
                    sp.wait_ge(full_o[6], l * OSTEPS + (OSTEPS + 1))
                    settle(sp)
                with sp.Else():
                    for s in range(SLOTS):
                        sp.sem_inc(landed_o[s], 16 * OSTEPS)
                sp.nop()

        def conv_tokens(k):
            return csq[:, k, 0:T]

        @block.tensor
        def _(pe):
            def begin(b, n):
                pe.wait_ge(freed[b], n)

            def chunk_in(c, l):
                pe.wait_ge(landed[c % SLOTS], l * (16 * SLOT_USES) + 16 * (c // SLOTS + 1))

            pe.wait_ge(consts, 3)
            pe.wait_ge(x_in, 48)
            for i in range(6):
                b, n = init_use("x", i)
                begin(b, n)
                t, h = i // 2, i % 2
                for k in range(4):
                    last = pe.transpose(ps[:, b, k * P:(k + 1) * P], nat[:, t, (4 * h + k) * P:(4 * h + k + 1) * P], ident[:])
                last.then_inc(full[b], 1)
            pe.wait_ge(c_in, 48)
            pe.wait_ge(chain_p, 8)
            pe.matmul(ps[:, 7, 0:24], crow[:, :], ident[0:24, 0:24], start=True, stop=True).then_inc(full[7], 1)
            pe.wait_ge(freed[7], 2)

            def moe_step(c_ring, f, narrow=None):
                free_at, full_s, landed_s, land_at, half_s, xg_s, xg_at = c_ring
                def products(which, b, small):
                    pe.wait_ge(f[b], free_at(b))
                    if which == 0:
                        pe.wait_ge(f[0], free_at(0))
                        pe.wait_ge(f[1], free_at(1))
                    if small:
                        for hh in range(2):
                            pe.wait_ge(landed_s[2 * which + hh], land_at)
                        for k in range(KD):
                            for hh in range(2):
                                last = pe.matmul(ps[64 * hh:64 * hh + 64, b, 0:256], xgT[:, k, 0:64],
                                                 ring[2 * which + hh][:, k * 256:(k + 1) * 256],
                                                 start=(k == 0), stop=(k == KD - 1))
                                if k == KD - 1:
                                    last.then_inc(half_s if hh == 0 else full_s[b], 1)
                        return
                    for hh in range(2):
                        s = 2 * which + hh
                        pe.wait_ge(landed_s[s], land_at)
                        for k in range(KD):
                            last = pe.matmul(ps[:, b, hh * 256:(hh + 1) * 256], xgT[:, k, :],
                                             ring[s][:, k * 256:(k + 1) * 256], start=(k == 0), stop=(k == KD - 1))
                        last.then_inc(half_s if hh == 0 else full_s[b], 1)

                def next_rows():
                    pe.wait_ge(xg_s, xg_at)
                    for h in range(2):
                        for k in range(4):
                            last = pe.transpose(ps[:, h, k * P:(k + 1) * P], xg[:, (4 * h + k) * P:(4 * h + k + 1) * P], ident[:])
                        last.then_inc(full_s[h], 1)

                def down(small):
                    pe.wait_ge(f[3], free_at(3) + 1)
                    pe.wait_ge(f[4], free_at(4))
                    for k in range(2 if small else KE):
                        last = pe.transpose(ps[:, 4, k * P:(k + 1) * P], hid[:, k * P:(k + 1) * P], ident[:])
                    last.then_inc(full_s[4], 1)
                    pe.wait_ge(f[4], free_at(4) + 1)
                    if small:
                        for h in range(2):
                            pe.wait_ge(f[5 + h], free_at(5 + h))
                            pe.wait_ge(landed_s[4 + h], land_at)
                        for k in range(KE):
                            for h in range(2):
                                last = pe.matmul(ps[64 * h:64 * h + 64, 5 + h, :], hidT[:, k % 2, 64 * (k // 2):64 * (k // 2) + 64],
                                                 ring[4 + h][:, k * 512:(k + 1) * 512], start=(k == 0), stop=(k == KE - 1))
                                if k == KE - 1:
                                    last.then_inc(full_s[5 + h], 1)
                        return
                    for h in range(2):
                        pe.wait_ge(f[5 + h], free_at(5 + h))
                        pe.wait_ge(landed_s[4 + h], land_at)
                        for k in range(KE):
                            last = pe.matmul(ps[:, 5 + h, :], hidT[:, k, :], ring[4 + h][:, k * 512:(k + 1) * 512],
                                             start=(k == 0), stop=(k == KE - 1))
                        last.then_inc(full_s[5 + h], 1)

                def whole(small):
                    products(0, 2, small)
                    products(1, 3, small)
                    next_rows()
                    down(small)

                if narrow is None:
                    whole(False)
                else:
                    with pe.If(narrow > 0):
                        whole(True)
                    with pe.Else():
                        whole(False)
                    pe.nop()

            def rms_sum(stage, l, q):
                b, n = use(stage, 0, l)
                begin(b, n)
                pe.wait_ge(sq_sum, q + 1)
                pe.matmul(ps[:, b, 0:T], ones[:], rstd[:], start=True, stop=True).then_inc(full[b], 1)

            with pe.Fori(0, DEPTH) as l:
                b, n = use("params", 0, l)
                begin(b, n)
                pe.wait_ge(par_in, l * 32 + 32)
                pe.matmul(ps[:, b, 0:76], prow[:, :], ident[0:76, 0:76], start=True, stop=True)
                pe.matmul(ps[:, b, 128:128 + CK * KC], dwrow[:, :], ident[0:CK * KC, 0:CK * KC],
                          start=True, stop=True).then_inc(full[b], 1)

                def ada_group(g):
                    stage, q = ("ada", g) if g < 4 else ("ada2", g - 4)
                    b, n = use(stage, q, l)
                    begin(b, n)
                    for cc in range(2):
                        c = CHUNK_AT["ada", g, cc]
                        chunk_in(c, l)
                        for k in range(4):
                            last = pe.matmul(ps[32 * k:32 * k + 32, b, :], condT[:, 4 * cc + k, :],
                                             ring[c % SLOTS][:, k * 512:(k + 1) * 512], start=(cc == 0), stop=(cc == 1))
                        last.then_inc(half if cc == 0 else full[b], 1)

                def mod_cols(g):
                    mb, mn = use("mod" if g < 4 else "mod2", 0, l)
                    ab, an = use("ada", g, l) if g < 4 else use("ada2", g - 4, l)
                    pe.wait_ge(freed[ab], an + 1)
                    if g in (0, 4):
                        begin(mb, mn)
                    for m in range(4):
                        last = pe.matmul(ps[:, mb, 2 * (4 * g + m):2 * (4 * g + m) + 2],
                                         modrow[:, g % 2, m * P:(m + 1) * P], sel[:, :], start=True, stop=True)
                    last.then_inc(full[mb] if g in (3, 11) else modrow_used, 1)

                for g in range(4):
                    ada_group(g)
                    if g >= 1:
                        mod_cols(g - 1)
                mod_cols(3)

                rms_sum("rms1", l, l * 2)

                def h_wait(which, k):
                    pe.wait_ge(h_ctx, l * (2 * KD) + (which * KD + k + 1))
                    pe.wait_ge(h_r, l * (2 * KD) + (which * KD + k + 1))

                for c in range(3):
                    q = CHUNK_AT["qkv", c, 0]
                    chunk_in(q, l)
                    for t in range(NT):
                        b, n = use("qkv", 3 * c + t, l)
                        begin(b, n)
                        for k in range(KD):
                            if c == 0 and t == 0:
                                h_wait(0, k)
                            last = pe.matmul(ps[:, b, 0:256], hT[:, k, t * P:(t + 1) * P],
                                             ring[q % SLOTS][:, k * 256:(k + 1) * 256], start=(k == 0), stop=(k == KD - 1))
                        last.then_inc(full[b], 1)

                def wide(stage, m, k_tiles, per_chunk, rhs):
                    c = CHUNK_AT[stage, m // per_chunk, 0]
                    if m % per_chunk == 0:
                        chunk_in(c, l)
                    b, n = use(stage, m, l)
                    begin(b, n)
                    w = per_chunk * P
                    for k in range(k_tiles):
                        o = k * w + (m % per_chunk) * P
                        last = pe.matmul(ps[:, b, 0:T], ring[c % SLOTS][:, o:o + P], rhs(k),
                                         start=(k == 0), stop=(k == k_tiles - 1))
                    last.then_inc(full[b], 1)

                for m in range(2 * KC):
                    wide("u", m, KD, 2, lambda k: hT[:, k, :])

                def filler(j):
                    kind, q = FILLERS[j]
                    if kind == "gate":
                        wide("gate", q, KD, 2, lambda k: hT[:, k, :])
                    else:
                        ada_group(4 + q)
                        if q > 0:
                            mod_cols(3 + q)

                pe.wait_ge(q_r, l + 1)
                for t in range(NT):
                    b, n = use("qT", t, l)
                    begin(b, n)
                    for p in range(4):
                        last = pe.transpose(ps[:, b, p * P:(p + 1) * P], qkv[:, t, p * P:(p + 1) * P], ident[:])
                    last.then_inc(full[b], 1)
                for i in range(2):
                    b, n = use("kT", i, l)
                    begin(b, n)
                    for j in range(4):
                        last = pe.transpose(ps[:, b, j * P:(j + 1) * P], kdup[:, 2 * i + j // 2, j % 2, :], ident[:])
                    last.then_inc(full[b], 1)

                units = [(bk, p) for bk in range(NT) for p in range(4)]

                def scores(i):
                    bk, p = units[i]
                    if i == 0:
                        for st_, q in (("qT", 0), ("qT", 1), ("qT", 2), ("kT", 0), ("kT", 1)):
                            b, n = use(st_, q, l)
                            pe.wait_ge(freed[b], n + 1)
                    k0, nk = (0, P) if bk == 0 else (P, 3 * P)
                    for e in range(2):
                        b, n = use("scores", 2 * i + e, l)
                        begin(b, n)
                        pe.matmul(ps[:, b, 0:nk], qT[64 * e:64 * e + 64, p, bk * P:(bk + 1) * P],
                                  kT[64 * e:64 * e + 64, p // 2, k0:k0 + nk], start=True, stop=True).then_inc(full[b], 1)

                def turn_probs(i):
                    bk, p = units[i]
                    pe.wait_ge(p_r, l * UNITS + (i + 1))
                    for e in range(2):
                        b, n = use("probsT", 2 * i + e, l)
                        begin(b, n)
                        for kt in range(1 if bk == 0 else 3):
                            last = pe.transpose(ps[:, b, kt * P:(kt + 1) * P], probs[:, i % 2, e, kt * P:(kt + 1) * P], ident[:])
                        last.then_inc(full[b], 1)

                def pv(i):
                    bk, p = units[i]
                    for e in range(2):
                        b, n = use("probsT", 2 * i + e, l)
                        pe.wait_ge(freed[b], n + 1)
                    b, n = use("pv", i, l)
                    begin(b, n)
                    g = p // 2
                    for e in range(2):
                        tiles = [qkv[:, 0, :]] if bk == 0 else [qkv[:, 1, :], qkv[:, 2, :], None]
                        for kt, v in enumerate(tiles):
                            vv = cache_v[:, g * HD:(g + 1) * HD] if v is None else v[:, 640 + g * HD:640 + (g + 1) * HD]
                            last = pe.matmul(ps[64 * e:64 * e + 64, b, 0:P], vv, probsT[:, e, kt, :],
                                             start=(kt == 0), stop=(kt == len(tiles) - 1))
                    last.then_inc(full[b], 1)

                scores(0)
                for i in range(UNITS):
                    if i + 1 < UNITS:
                        scores(i + 1)
                    filler(2 * i)
                    turn_probs(i)
                    filler(2 * i + 1)
                    pv(i)
                mod_cols(11)

                for i, (s, v) in enumerate(((tapped, l * (CK * KC) + CK * KC), (csq_r, l + 1))):
                    b, n = use("ln", i, l)
                    begin(b, n)
                    pe.wait_ge(s, v)
                    for k in range(KC):
                        last = pe.matmul(ps[:, b, 0:CO], ones[:], (conv if i == 0 else csq)[:, k, :],
                                         start=(k == 0), stop=(k == KC - 1))
                    last.then_inc(full[b], 1)
                    if i == 0:
                        for q in (10, 11):
                            pb, pn = use("pv", q, l)
                            pe.wait_ge(freed[pb], pn + 1)
                        for m in range(4):
                            wide("aproj", m, KC, 4, lambda k: attnT[:, k, :])
                for m in range(4, KD):
                    wide("aproj", m, KC, 4, lambda k: attnT[:, k, :])
                pe.wait_ge(convT_r, l * KC + KC)
                for m in range(KD):
                    wide("cproj", m, KC, 4, lambda k: conv_tokens(k))
                for m in range(4):
                    b, n = use("cproj", 4 + m, l)
                    pe.wait_ge(freed[b], n + 1)
                for m in range(KD):
                    wide("out", m, KD, 2, lambda k: hT[:, k, :])

                rms_sum("rms2", l, l * 2 + 1)
                b, n = use("logitsT", 0, l)
                begin(b, n)
                chunk_in(CHUNK_AT["router", 0, 0], l)
                for k in range(KD):
                    h_wait(1, k)
                    last = pe.matmul(ps[0:NE, b, 0:T], ring[CHUNK_AT["router", 0, 0] % SLOTS][:, k * NE:(k + 1) * NE], hT[:, k, :],
                                     start=(k == 0), stop=(k == KD - 1))
                last.then_inc(full[b], 1)

                def h2n(i):
                    b, n = use("h2n", i, l)
                    begin(b, n)
                    t, h = i // 2, i % 2
                    for k in range(4):
                        last = pe.transpose(ps[:, b, k * P:(k + 1) * P], hT[:, 4 * h + k, t * P:(t + 1) * P], ident[:])
                    last.then_inc(full[b], 1)

                h2n(0)
                h2n(1)
                b, n = use("logitsT", 0, l)
                pe.wait_ge(freed[b], n + 1)
                b, n = use("logits", 0, l)
                begin(b, n)
                for t in range(NT):
                    last = pe.matmul(ps[:, b, t * NE:(t + 1) * NE], lgT[:, t * P:(t + 1) * P], ident[0:NE, 0:NE],
                                     start=True, stop=True)
                last.then_inc(full[b], 1)
                for i in range(2, 6):
                    h2n(i)
                pe.wait_ge(route_r, l + 1)
                b, n = use("rank", 0, l)
                begin(b, n)
                for t in range(NT):
                    for i in range(t + 1):
                        pe.matmul(ps[:, b, t * NE:(t + 1) * NE], before[:] if i == t else ones[:], ra[:, i, :],
                                  start=(i == 0), stop=(i == t))
                for i in range(NT):
                    last = pe.matmul(ps[:, b, NT * NE:(NT + 1) * NE], ones[:], ra[:, i, :], start=(i == 0), stop=(i == NT - 1))
                last.then_inc(full[b], 1)

                pe.wait_ge(xg_in, l * (16 * (NE + 2)) + 16)
                for h in range(2):
                    b, n = use("xT0", h, l)
                    begin(b, n)
                    for k in range(4):
                        last = pe.transpose(ps[:, b, k * P:(k + 1) * P], xg[:, (4 * h + k) * P:(4 * h + k + 1) * P], ident[:])
                    last.then_inc(full[b], 1)
                with pe.Fori(0, NE) as e:
                    moe_step((lambda b: l * PER[b] + e + (INIT[b] + MOE_AT[b]), full, landed,
                              l * (16 * SLOT_USES) + e * 16 + 16 * 9, half,
                              xg_in, l * (16 * (NE + 2)) + e * 16 + 32), freed,
                             pe.value_load(narrow_e[0:1, bass.ds(e, 1)], min_val=0, max_val=1))

                over = pe.value_load(overfull[0:1, 0:1], min_val=0, max_val=1)
                with pe.If(over > 0):
                    for b in MOE_BANKS:
                        pe.wait_ge(freed[b], l * PER[b] + (INIT[b] + MOE_AT[b] + NE))
                    pe.wait_ge(xg_in_o, l * (16 * (OSTEPS + 2)) + 16)
                    for h in range(2):
                        for k in range(4):
                            last = pe.transpose(ps[:, h, k * P:(k + 1) * P], xg[:, (4 * h + k) * P:(4 * h + k + 1) * P], ident[:])
                        last.then_inc(full_o[h], 1)
                    with pe.Fori(0, OSTEPS) as i:
                        moe_step((lambda b: (l * (OSTEPS + 1) + i + 2) if b < 2 else l * OSTEPS + i + 1, full_o, landed_o,
                                  l * (16 * OSTEPS) + i * 16 + 16, half_o,
                                  xg_in_o, l * (16 * (OSTEPS + 2)) + i * 16 + 32), freed_o)
                with pe.Else():
                    for b in MOE_BANKS:
                        pe.sem_inc(full_o[b], OSTEPS + 1 if b < 2 else OSTEPS)
                    pe.sem_inc(half_o, 2 * OSTEPS)
                pe.nop()

                for i in range(6):
                    b, n = use("y", i, l)
                    begin(b, n)
                    t, h = i // 2, i % 2
                    if i == 0:
                        for q in range(7):
                            pe.wait_ge(freed_o[q], l * (OSTEPS + 1) + (OSTEPS + 2) if q < 2 else l * OSTEPS + (OSTEPS + 1))
                    if h == 0:
                        pe.wait_ge(comb_r, l * NT + (t + 1))
                    for k in range(4):
                        last = pe.transpose(ps[:, b, k * P:(k + 1) * P], nat[:, t, (4 * h + k) * P:(4 * h + k + 1) * P], ident[:])
                    last.then_inc(full[b], 1)

            pe.wait_ge(freed[3], DEPTH * PER[3] + INIT[3])
            pe.wait_ge(sq_sum, 2 * DEPTH + 1)
            pe.matmul(ps[:, 3, 0:T], ones[:], rstd[:], start=True, stop=True).then_inc(full[3], 1)
            pe.wait_ge(h_r, DEPTH * 2 * KD + KD)
            for i in range(6):
                b = i % 3
                pe.wait_ge(freed[b], DEPTH * PER[b] + INIT[b] + i // 3)
                t, h = i // 2, i % 2
                for k in range(4):
                    last = pe.transpose(ps[:, b, k * P:(k + 1) * P], hT[:, 4 * h + k, t * P:(t + 1) * P], ident[:])
                last.then_inc(full[b], 1)

        @block.scalar
        def _(act):
            for t in range(NT):
                src = A["x_prompt"][0] if t == 0 else A["x_sample"][0, (t - 1) * P:t * P, :]
                act.dma_start(nat[:, t, :], src).then_inc(x_in, 16)
            def load_params(row):
                act.dma_start(prow[:, :], A["features"][row].rearrange("o r p -> (o r) p")).then_inc(par_in, 16)
                act.dma_start(dwrow[:, :], A["taps"][row].rearrange("o r p -> (o r) p")).then_inc(par_in, 16)
                act.dma_start(every[:], A["every"][row, :].broadcast_to([P, 2 * HD + NH])).then_inc(bc_in, 16)

            act.dma_start(crow[0:8, :], A["c_ctx"].rearrange("(k p) -> k p", p=P)).then_inc(c_in, 16)
            act.dma_start(crow[8:16, :], A["c"].rearrange("o (k p) -> (o k) p", p=P)).then_inc(c_in, 16)
            act.dma_start(crow[16:24, :], A["final_norm"].rearrange("(k p) -> k p", p=P)).then_inc(c_in, 16)
            load_params(slice(0, 1))
            act.dma_start(rope[:], A["rope"].rearrange("(t p) c d -> p t c d", p=P)).then_inc(t_in, 16)
            act.dma_start(rbias[:], A["router_bias"].rearrange("(o n) -> o n", o=1).broadcast_to([P, NE])).then_inc(t_in, 16)
            act.wait_ge(full[7], 2)
            act.activation(csig[:], ps[:, 7, 0:16], ACT.Sigmoid).then_inc(csig_r, 1)

            def squares(q, tile_ready=None):
                for k in range(KD):
                    if tile_ready:
                        tile_ready(k)
                    act.activation(squared[:, k, :], xT[:, k, :], ACT.Square).then_inc(xsq, 1)

            def root(bank, n):
                act.wait_ge(full[bank], n + 1)
                act.activation(rms[:], ps[:, bank, 0:T], ACT.Sqrt, scale=1.0 / D, bias=eps[:]).then_inc(freed[bank], 1)

            def affine(q, which):
                for k in range(KD):
                    act.wait_ge(xn_r, q * KD + (k + 1))
                    act.activation(hT[:, k, TC:T], hT[:, k, TC:T], ACT.Identity, scale=coef[:, which, k, 1:2],
                                   bias=mod[:, 24 * which + k, 1:2]).then_inc(h_r, 1)

            act.wait_ge(freed[0], INIT[0])
            act.wait_ge(freed[1], INIT[1])
            act.wait_ge(consts_v, 1)

            def moe_act(fs, fr, n_of, xg_s, wr_s, wr_at, row, row2, narrow=None):
                def start_step(cols):
                    act.wait_ge(fs[2], n_of(2) + 1)
                    act.wait_ge(fr[3], n_of(3))
                    act.activation(silu[:, 0:cols], ps[:, 2, 0:cols], ACT.Silu).then_inc(fr[2], 1)
                    for h in range(2):
                        act.wait_ge(fs[h], n_of(h) + 1)
                        if h == 0:
                            act.wait_ge(fs[3], n_of(3) + 1)
                        act.activation(xgT[:, 4 * h:4 * h + 4, :], ps[:, h, :].rearrange("p (k n) -> p k n", k=4),
                                       ACT.Copy).then_inc(fr[h], 1)
                    act.dma_start(xg, rows_in[bass.ds(row2, P), :]).then_inc(xg_s, 16)
                    act.wait_ge(wr_s, wr_at)

                def whole(small):
                    start_step(256 if small else DE)
                    for h in range(2):
                        act.wait_ge(fs[5 + h], n_of(5 + h) + 1)
                        a, z, o = (64 * h, 64 * h + 64, 0) if small else (0, P, 512 * h)
                        act.activation(orow[a:z, o:o + 512], ps[a:z, 5 + h, :], ACT.Copy).then_inc(fr[5 + h], 1)
                        act.wait_ge(fr[5 + h], n_of(5 + h) + 1)
                        act.dma_start(rows_out[bass.ds(row, z - a), 512 * h:512 * h + 512], orow[a:z, o:o + 512]
                                      ).then_inc(wr_s, 16)

                if narrow is None:
                    whole(False)
                else:
                    with act.If(narrow > 0):
                        whole(True)
                    with act.Else():
                        whole(False)
                    act.nop()

            with act.Fori(0, DEPTH) as l:
                act.dma_start(cache_v[:], A["cache_v"][0, bass.ds(l, 1)].rearrange("o t h d -> (o t) (h d)")).then_inc(cache_in, 16)
                act.dma_start(cache_k[:], A["cache_k"][0, bass.ds(l, 1)].rearrange("o t h d -> (o t) (h d)")).then_inc(cache_in, 16)

                squares(l * 2)
                b, n = use("rms1", 0, l)
                root(b, n)
                act.wait_ge(mod_r, l * 2 + 1)
                affine(l * 2, 0)

                for i in range(9):
                    b, n = use("qkv", i, l)
                    act.wait_ge(full[b], n + 1)
                    c, t = i // 3, i % 3
                    act.activation(qkv[:, t, c * 256:(c + 1) * 256], ps[:, b, 0:256], ACT.Copy).then_inc(freed[b], 1)
                act.wait_ge(freed[6], use("qkv", 8, l)[1] + 1)
                act.wait_ge(freed[5], use("qkv", 7, l)[1] + 1)
                act.wait_ge(freed[4], use("qkv", 6, l)[1] + 1)
                act.activation(qtmp[:, :, :], qkv[:, :, 0:640], ACT.Square).then_inc(qsq_r, 1)
                act.wait_ge(qss_r, l + 1)
                act.activation(ss[:], ss[:], ACT.Sqrt, scale=1.0 / HD, bias=eps[:]).then_inc(qrms_r, 1)

                for i in range(KC, 2 * KC):
                    b, n = use("u", i, l)
                    act.wait_ge(full[b], n + 1)
                    j = i - KC
                    if j >= 2:
                        act.wait_ge(usig_used, l * KC + (j - 1))
                    act.activation(sig[:, j % 2, :], ps[:, b, 0:T], ACT.Sigmoid).then_inc(freed[b], 1)
                for t in range(NT):
                    b, n = use("qT", t, l)
                    act.wait_ge(full[b], n + 1)
                    act.activation(qT[:, :, t * P:(t + 1) * P], ps[:, b, :].rearrange("p (k n) -> p k n", k=4),
                                   ACT.Copy).then_inc(freed[b], 1)
                for i in range(2):
                    b, n = use("kT", i, l)
                    act.wait_ge(full[b], n + 1)
                    for j in range(2):
                        last = act.activation(kT[:, :, (2 * i + j) * P:(2 * i + j + 1) * P],
                                              ps[:, b, 2 * j * P:2 * (j + 1) * P].rearrange("p (g n) -> p g n", g=2), ACT.Copy)
                    last.then_inc(freed[b], 1)

                def exponentials(i):
                    nk = P if i < 4 else 3 * P
                    act.wait_ge(sm_max, l * UNITS + (i + 1))
                    for e in range(2):
                        act.activation(probs[:, i % 2, e, 0:nk], probs[:, i % 2, e, 0:nk], ACT.Exp,
                                       bias=st[:, i % 2, e:e + 1], accum_out=st[:, i % 2, 4 + e:5 + e])
                    act.activation(st[:, i % 2, 2:4], st[:, i % 2, 2:4], ACT.Exp).then_inc(sm_exp, 1)

                def filler_out(j):
                    kind, q = FILLERS[j]
                    b, n = use(kind, q, l)
                    act.wait_ge(full[b], n + 1)
                    if kind == "gate":
                        act.activation(gates[:, q, :], ps[:, b, 0:T], ACT.Sigmoid).then_inc(freed[b], 1)
                        return
                    if q < 2:
                        act.wait_ge(full[2], use("mod", 0, l)[1] + 1)
                    else:
                        act.wait_ge(modrow_used, l * 10 + (3 + q - 1))
                    act.activation(modrow[:, q % 2, :], ps[:, b, :], ACT.Copy).then_inc(freed[b], 1)

                exponentials(0)
                for i in range(UNITS):
                    filler_out(2 * i)
                    nkt = 1 if i < 4 else 3
                    for e in range(2):
                        b, n = use("probsT", 2 * i + e, l)
                        act.wait_ge(full[b], n + 1)
                        if i >= 1:
                            vb, vn = use("pv", i - 1, l)
                            act.wait_ge(full[vb], vn + 1)
                        act.activation(probsT[:, e, 0:nkt, :], ps[:, b, 0:nkt * P].rearrange("p (k n) -> p k n", k=nkt),
                                       ACT.Copy).then_inc(freed[b], 1)
                    if i + 1 < UNITS:
                        exponentials(i + 1)
                    filler_out(2 * i + 1)
                    bk, p = i // 4, i % 4
                    b, n = use("pv", i, l)
                    act.wait_ge(full[b], n + 1)
                    act.activation(attnT[:, p, bk * P:(bk + 1) * P], ps[:, b, 0:P], ACT.Copy).then_inc(freed[b], 1)

                act.wait_ge(conv_c, l + 1)
                act.activation(csq[:], conv[:], ACT.Square).then_inc(csq_r, 1)
                b, n = use("ln", 1, l)
                act.wait_ge(full[b], n + 1)
                act.activation(mu[:], ps[:, b, 0:CO], ACT.Sqrt, scale=1.0 / CW, bias=eps[:]).then_inc(freed[b], 1)
                for k in range(KC):
                    act.wait_ge(cn_r, l * KC + (k + 1))
                    act.activation(csq[:, k, 0:TC], conv[:, k, 0:TC], ACT.Silu, scale=par[:, 68 + k:69 + k], bias=par[:, 72 + k:73 + k])
                    act.activation(csq[:, k, TC:T], conv[:, k, LAT0:LAT0 + TL], ACT.Silu, scale=par[:, 68 + k:69 + k],
                                   bias=par[:, 72 + k:73 + k]).then_inc(convT_r, 1)

                def mixer_out(k):
                    b, n = use("out", k, l)
                    act.wait_ge(freed[b], n + 1)
                squares(l * 2 + 1, mixer_out)
                b, n = use("rms2", 0, l)
                root(b, n)
                act.wait_ge(mod_r, l * 2 + 2)
                affine(l * 2 + 1, 1)
                for i in range(6):
                    b, n = use("h2n", i, l)
                    act.wait_ge(full[b], n + 1)
                    t, h = i // 2, i % 2
                    act.activation(nat[:, t, h * 512:(h + 1) * 512], ps[:, b, :], ACT.Copy).then_inc(freed[b], 1)
                    if i == 1:
                        b, n = use("logits", 0, l)
                        act.wait_ge(full[b], n + 1)
                        act.activation(sc[:], ps[:, b, 0:NT * NE].rearrange("p (t n) -> p t n", t=NT), ACT.Sigmoid).then_inc(freed[b], 1)

                b, n = use("params", 0, l)
                act.wait_ge(full[b], n + 1)
                load_params(bass.ds(l + 1, 1))

                act.wait_ge(scat, l * 96 + 96)
                act.wait_ge(scratch0, 16 * BLOCKS)
                act.dma_start(xg, rows_in[0:P, :]).then_inc(xg_in, 16)
                for h in range(2):
                    b, n = use("xT0", h, l)
                    act.wait_ge(full[b], n + 1)
                    act.activation(xgT[:, 4 * h:4 * h + 4, :], ps[:, b, :].rearrange("p (k n) -> p k n", k=4),
                                   ACT.Copy).then_inc(freed[b], 1)
                r1_ = act.value_load(row_at[0:1, 1:2], min_val=0, max_val=ROWS)
                act.dma_start(xg, rows_in[bass.ds(r1_, P), :]).then_inc(xg_in, 16)
                with act.Fori(0, NE) as e:
                    row = act.value_load(row_at[0:1, bass.ds(e, 1)], min_val=0, max_val=ROWS)
                    row2 = act.value_load(row_at[0:1, bass.ds(e + 2, 1)], min_val=0, max_val=ROWS)
                    moe_act(full, freed, lambda b: l * PER[b] + e + (INIT[b] + MOE_AT[b]),
                            xg_in, out_wr, l * (32 * NE) + e * 32 + 1, row, row2,
                            act.value_load(narrow_e[0:1, bass.ds(e, 1)], min_val=0, max_val=1))
                act.wait_ge(out_wr, l * (32 * NE) + 32 * NE + 1)
                act.wait_ge(xg_in, l * (16 * (NE + 2)) + 16 * (NE + 2))
                settle(act)
                over = act.value_load(overfull[0:1, 0:1], min_val=0, max_val=1)
                with act.If(over > 0):
                    act.dma_start(xg, rows_in[0:P, :]).then_inc(xg_in_o, 16)
                    for h in range(2):
                        act.wait_ge(full_o[h], l * (OSTEPS + 1) + 2)
                        act.activation(xgT[:, 4 * h:4 * h + 4, :], ps[:, h, :].rearrange("p (k n) -> p k n", k=4),
                                       ACT.Copy).then_inc(freed_o[h], 1)
                    r1_ = act.value_load(orow_at[0:1, 1:2], min_val=0, max_val=ROWS + 2 * P)
                    act.dma_start(xg, rows_in[bass.ds(r1_, P), :]).then_inc(xg_in_o, 16)
                    with act.Fori(0, OSTEPS) as i:
                        row = act.value_load(orow_at[0:1, bass.ds(i, 1)], min_val=0, max_val=ROWS + 2 * P)
                        row2 = act.value_load(orow_at[0:1, bass.ds(i + 2, 1)], min_val=0, max_val=ROWS + 2 * P)
                        moe_act(full_o, freed_o, lambda b: (l * (OSTEPS + 1) + i + 2) if b < 2 else l * OSTEPS + i + 1,
                                xg_in_o, out_wr_o, l * (32 * OSTEPS) + i * 32 + 1, row, row2)
                    act.wait_ge(out_wr_o, l * (32 * OSTEPS) + 32 * OSTEPS + 1)
                    act.wait_ge(xg_in_o, l * (16 * (OSTEPS + 2)) + 16 * (OSTEPS + 2))
                    settle(act)
                with act.Else():
                    for b in (0, 1, 2, 5, 6):
                        act.sem_inc(freed_o[b], OSTEPS + 1 if b < 2 else OSTEPS)
                    act.sem_inc(xg_in_o, 16 * (OSTEPS + 2))
                    act.sem_inc(out_wr_o, 32 * OSTEPS)
                act.nop()
                act.wait_ge(kv_out, l * 32 + 32)
                for q in range(3):
                    b, n = use("y", 3 + q, l)
                    act.wait_ge(freed[b], n + 1)

            squares(2 * DEPTH)
            root(3, DEPTH * PER[3] + INIT[3])
            for k in range(KD):
                act.wait_ge(xn_r, 2 * DEPTH * KD + k + 1)
                act.activation(hT[:, k, :], hT[:, k, :], ACT.Copy, scale=fnorm[:, k:k + 1]).then_inc(h_r, 1)
            for i in range(6):
                b = i % 3
                act.wait_ge(full[b], DEPTH * PER[b] + INIT[b] + i // 3 + 1)
                t, h = i // 2, i % 2
                act.activation(nat[:, t, h * 512:(h + 1) * 512], ps[:, b, :], ACT.Copy).then_inc(freed[b], 1)
                if h == 1:
                    for j in (i - 1, i):
                        act.wait_ge(freed[j % 3], DEPTH * PER[j % 3] + INIT[j % 3] + j // 3 + 1)
                    dst = A["y_prompt"][0] if t == 0 else A["y_sample"][0, (t - 1) * P:t * P, :]
                    act.dma_start(dst, nat[:, t, :]).then_inc(y_out, 16)
            act.wait_ge(y_out, 48)
            act.wait_ge(par_in, 32 * (DEPTH + 1))
            act.wait_ge(bc_in, 16 * (DEPTH + 1))

        @block.gpsimd
        def _(pool):
            pool.memset(orow, 0.0).then_inc(zeroed, 1)
            pool.memset(ident[:], 0.0).then_inc(chain_p, 1)
            pool.memset(ones[:], 1.0).then_inc(consts, 1)
            pool.memset(before[:], 1.0).then_inc(chain_p, 1)
            pool.memset(sel[:], 0.0).then_inc(chain_p, 1)
            pool.memset(mask[:], 0.0).then_inc(chain_p, 1)
            pool.wait_ge(chain_p, 4)
            pool.affine_select(out=ident[:], in_=ident[:], compare_op=ALU.not_equal, fill=1.0, base=0,
                               pattern=[[-1, P]], channel_multiplier=1).then_inc(consts, 1)
            pool.affine_select(out=before[:], in_=before[:], compare_op=ALU.is_gt, fill=0.0, base=0,
                               pattern=[[1, P]], channel_multiplier=-1).then_inc(consts, 1)
            pool.affine_select(out=mask[:, 0, 0:TL], in_=mask[:, 0, 0:TL], compare_op=ALU.is_ge, fill=NEG, base=P,
                               pattern=[[-1, TL]], channel_multiplier=1).then_inc(consts2, 1)
            pool.affine_select(out=mask[:, 1, 0:TL], in_=mask[:, 1, 0:TL], compare_op=ALU.is_ge, fill=NEG, base=0,
                               pattern=[[1, TL]], channel_multiplier=-1).then_inc(consts2, 1)
            for j in range(4):
                pool.affine_select(out=sel[:], in_=sel[:], compare_op=ALU.not_equal, fill=1.0, base=-32 * j,
                                   pattern=[[-1, 2]], channel_multiplier=1).then_inc(chain_p, 1)
                pool.wait_ge(chain_p, 5 + j)
            pool.iota(down_i[:], pattern=[[0, NT], [-1, NE]], base=NE, channel_multiplier=0,
                      allow_small_or_imprecise_dtypes=True).then_inc(consts2, 1)
            pool.iota(down_g[:], pattern=[[0, NT], [-1, NG]], base=NG, channel_multiplier=0,
                      allow_small_or_imprecise_dtypes=True).then_inc(consts2, 1)
            pool.memset(zero16[:], 0.0).then_inc(consts2, 1)

            pool.wait_ge(zeroed, 1)
            pool.wait_ge(h_r, KD)
            for r in range(BLOCKS):
                pool.dma_start(rows_in[ROWS + r * P:ROWS + (r + 1) * P, :], orow).then_inc(scratch0, 16)

            with pool.Fori(0, DEPTH) as l:
                pool.wait_ge(k_pre, l + 1)
                pool.dma_start(A["new_k"][0, bass.ds(l, 1)].rearrange("o t h d -> (o t) (h d)"), qkv[:, 0, 512:640]).then_inc(kv_out, 16)
                pool.dma_start(A["new_v"][0, bass.ds(l, 1)].rearrange("o t h d -> (o t) (h d)"), qkv[:, 0, 640:768]).then_inc(kv_out, 16)

                pool.wait_ge(pos_r, l + 1)
                for b in range(3):
                    n = use("h2n", 3 + b, l)[1]
                    pool.wait_ge(freed[USES["h2n"][3 + b][0]], n + 1)
                settle(pool)
                for t in range(NT):
                    for j in range(2):
                        pool.indirect_dma_start(out=rows_in[:, :], out_offset=bass.IndirectOffsetOnAxis(ap=pos[:, j, t:t + 1], axis=0),
                                                in_=nat[:, t, :], in_offset=None).then_inc(scat, 16)
                pool.wait_ge(out_wr, l * (32 * NE) + 32 * NE + 1)
                pool.wait_ge(out_wr_o, l * (32 * OSTEPS) + 32 * OSTEPS + 1)
                settle(pool)
                for t in range(NT):
                    for j in range(2):
                        pool.indirect_dma_start(out=gath[:, 2 * t + j, :], out_offset=None, in_=rows_out[0:ROWS, :],
                                                in_offset=bass.IndirectOffsetOnAxis(ap=pos[:, j, t:t + 1], axis=0)
                                                ).then_inc(gat[t], 16)
            pool.wait_ge(kv_out, 32 * DEPTH)

        @block.vector
        def _(dve):
            steps = [0]
            layer = [None]

            def link(ins):
                steps[0] += 1
                ins.then_inc(chain, 1)
                dve.wait_ge(chain, (layer[0] * CHAIN + steps[0]) if layer[0] is not None else steps[0])

            BASE = 4
            link(dve.memset(condT[:], 0.0))
            link(dve.memset(ub[:], 0.0))
            link(dve.memset(posf[:], 0.0))
            link(dve.memset(orowsf[:], float(ROWS)))
            dve.memset(eps[:], EPS).then_inc(consts_v, 1)
            for i in range(6):
                b, n = init_use("x", i)
                t, h = i // 2, i % 2
                dve.wait_ge(full[b], n + 1)
                dve.tensor_copy(xT[:, 4 * h:4 * h + 4, t * P:(t + 1) * P],
                                ps[:, b, :].rearrange("p (k n) -> p k n", k=4)).then_inc(freed[b], 1)
            dve.wait_ge(csig_r, 1)
            for c in range(2):
                dve.tensor_tensor(condT[:, :, c], ps[:, 7, 8 * c:8 * c + 8], csig[:, 8 * c:8 * c + 8], ALU.mult)
            dve.tensor_copy(fnorm[:], ps[:, 7, 16:24]).then_inc(freed[7], 1)
            dve.wait_ge(consts2, 5)
            dve.wait_ge(t_in, 32)
            assert steps[0] == BASE
            steps[0] = 0

            def ready(ins, s, value):
                ins.then_inc(s, 1)
                dve.wait_ge(s, value)

            def add_square(q, k):
                dve.wait_ge(xsq, q * KD + (k + 1))
                if k > 1:
                    dve.wait_ge(sq_added, q * (KD - 2) + (k - 1))
                dve.tensor_tensor(rstd[:], squared[:, 0, :] if k == 1 else rstd[:], squared[:, k, :], ALU.add
                                  ).then_inc(sq_sum if k == KD - 1 else sq_added, 1)

            def add_squares(q):
                for k in range(1, KD):
                    add_square(q, k)

            def norm_tiles(q, which=None):
                for k in range(KD):
                    dve.tensor_tensor(hT[:, k, :], xT[:, k, :], rstd[:], ALU.mult).then_inc(xn_r, 1)
                    if which is not None:
                        dve.wait_ge(xn_r, q * KD + (k + 1))
                        dve.tensor_scalar(hT[:, k, 0:TC], hT[:, k, 0:TC], coef[:, which, k, 0:1],
                                          mod[:, 24 * which + k, 0:1], ALU.mult, ALU.add).then_inc(h_ctx, 1)

            def moe_dve(fs, fr, n_of, narrow=None):
                def whole(cols):
                    dve.wait_ge(fr[2], n_of(2) + 1)
                    dve.wait_ge(fs[3], n_of(3) + 1)
                    dve.wait_ge(fs[4], n_of(4))
                    dve.tensor_tensor(hid[:, 0:cols], silu[:, 0:cols], ps[:, 3, 0:cols], ALU.mult).then_inc(fr[3], 1)
                    dve.wait_ge(fs[4], n_of(4) + 1)
                    dve.wait_ge(fs[6], n_of(6))
                    dve.tensor_copy(hidT[:, 0:cols // P, :], ps[:, 4, 0:cols].rearrange("p (k n) -> p k n", n=P)
                                    ).then_inc(fr[4], 1)

                if narrow is None:
                    whole(DE)
                else:
                    with dve.If(narrow > 0):
                        whole(256)
                    with dve.Else():
                        whole(DE)
                    dve.nop()

            with dve.Fori(0, DEPTH) as l:
                def link(ins):
                    steps[0] += 1
                    ins.then_inc(chain, 1)
                    dve.wait_ge(chain, l * CHAIN + (BASE + steps[0]))

                b, n = use("params", 0, l)
                dve.wait_ge(full[b], n + 1)
                dve.tensor_copy(par[:], ps[:, b, 0:76])
                ready(dve.tensor_copy(dw[:], ps[:, b, 128:128 + CK * KC]), freed[b], n + 1)
                dve.wait_ge(bc_in, l * 16 + 16)
                dve.tensor_scalar(nsink[:], sinkb, -1.0, None, ALU.mult)

                for g in range(4):
                    b, n = use("ada", g, l)
                    dve.wait_ge(full[b], n + 1)
                    if g >= 2:
                        dve.wait_ge(modrow_used, l * 10 + (g - 1))
                    dve.tensor_copy(modrow[:, g % 2, :], ps[:, b, :]).then_inc(freed[b], 1)

                def modulation(stage, m0, m1):
                    b, n = use(stage, 0, l)
                    dve.wait_ge(full[b], n + 1)
                    ready(dve.tensor_tensor(mod[:, m0:m1, :], ps[:, b, 2 * m0:2 * m1].rearrange("p (m c) -> p m c", c=2),
                                            par[:, m0:m1].unsqueeze(2).to_broadcast([P, m1 - m0, 2]), ALU.add), freed[b], n + 1)
                    w = m0 // 16
                    for c in range(2):
                        last = dve.scalar_tensor_tensor(coef[:, w, :, c], mod[:, 24 * w + 8:24 * w + 16, c] if w == 0 else
                                                        mod[:, 32:40, c], 1.0, par[:, 48 + 8 * w:56 + 8 * w], ALU.add, ALU.mult)
                    ready(last, mod_r, l * 2 + (1 if stage == "mod" else 2))

                modulation("mod", 0, 16)

                add_squares(l * 2)
                b, n = use("rms1", 0, l)
                dve.wait_ge(freed[b], n + 1)
                link(dve.reciprocal(rstd[:], rms[:]))
                norm_tiles(l * 2, 0)


                dve.wait_ge(qsq_r, l + 1)
                dve.tensor_reduce(ss[:], qtmp[:].rearrange("p t (h d) -> p (t h) d", d=HD), AX.X, ALU.add).then_inc(qss_r, 1)
                dve.wait_ge(qrms_r, l + 1)
                link(dve.reciprocal(ss[:], ss[:]))
                for t in range(NT):
                    qk = qkv[:, t, 0:640].rearrange("p (h d) -> p h d", d=HD)
                    tmp = qtmp[:, t, :].rearrange("p (h d) -> p h d", d=HD)
                    link(dve.tensor_tensor(tmp, qk, ss[:, 10 * t:10 * t + 10].unsqueeze(2).to_broadcast([P, 10, HD]), ALU.mult))
                    dve.tensor_tensor(qk[:, 0:NH, :], tmp[:, 0:NH, :], qkn[:, 0:1, :].to_broadcast([P, NH, HD]), ALU.mult)
                    i2 = dve.tensor_tensor(qk[:, NH:10, :], tmp[:, NH:10, :], qkn[:, 1:2, :].to_broadcast([P, 2, HD]), ALU.mult)
                    if t == 0:
                        ready(i2, k_pre, l + 1)
                    else:
                        link(i2)
                for t in range(1, NT):
                    qk = qkv[:, t, 0:640].rearrange("p (h d) -> p h d", d=HD)
                    tmp = qtmp[:, t, :].rearrange("p (h d) -> p h d", d=HD)
                    dve.tensor_tensor(tmp, qk, rope[:, t - 1, 0:1, :].to_broadcast([P, 10, HD]), ALU.mult)
                    t2 = qtmp2[:, t - 1, :].rearrange("p (h a s i) -> p h a s i", h=10, a=2, s=2)
                    qs = qkv[:, t, 0:640].rearrange("p (h a s i) -> p h a s i", h=10, a=2, s=2)
                    sn = rope[:, t - 1, 1:2, :].rearrange("p o (a s i) -> p o a s i", a=2, s=2)
                    for s_ in range(2):
                        for a_ in range(2):
                            last = dve.tensor_tensor(t2[:, :, a_, s_, :], qs[:, :, a_, 1 - s_, :],
                                                     sn[:, :, a_, s_, :].to_broadcast([P, 10, 16]), ALU.mult)
                    link(last)
                    link(dve.tensor_tensor(qk, tmp, qtmp2[:, t - 1, :].rearrange("p (h d) -> p h d", d=HD), ALU.add))
                dve.wait_ge(cache_in, l * 32 + 32)
                for t in range(4):
                    src = cache_k[:].rearrange("p (g d) -> p g d", g=2) if t == 3 else \
                        qkv[:, t, 512:640].rearrange("p (g d) -> p g d", g=2)
                    last = dve.tensor_copy(kdup[:, t, :, :].rearrange("p g (u d) -> p g u d", u=2),
                                           src.unsqueeze(2).to_broadcast([P, 2, 2, HD]))
                last.then_inc(q_r, 1)

                for i in range(KC):
                    b, n = use("u", i, l)
                    dve.wait_ge(full[b], n + 1)
                    dve.tensor_copy(ub[:, i, PAD:PAD + TC], ps[:, b, 0:TC])
                    ready(dve.tensor_copy(ub[:, i, SEG + PAD:SEG + PAD + TL], ps[:, b, TC:T]), freed[b], n + 1)
                for i in range(KC):
                    b, n = use("u", KC + i, l)
                    dve.wait_ge(freed[b], n + 1)
                    dve.tensor_tensor(ub[:, i, PAD:PAD + TC], ub[:, i, PAD:PAD + TC], sig[:, i % 2, 0:TC], ALU.mult)
                    u0 = SEG + PAD
                    ready(dve.tensor_tensor(ub[:, i, u0:u0 + TL], ub[:, i, u0:u0 + TL], sig[:, i % 2, TC:T], ALU.mult),
                          usig_used, l * KC + (i + 1))
                def tap(n):
                    j, i = n // KC, n % KC
                    src = ub[:, i, j:j + CO]
                    w = dw[:, n:n + 1]
                    if j == 0:
                        dve.tensor_scalar(conv[:, i, :], src, w, par[:, 64 + i:65 + i], ALU.mult, ALU.add).then_inc(tapped, 1)
                    else:
                        dve.wait_ge(tapped, l * (CK * KC) + (n - KC + 1))
                        dve.scalar_tensor_tensor(conv[:, i, :], src, w, conv[:, i, :], ALU.mult, ALU.add).then_inc(tapped, 1)

                def soft_a(i):
                    bk, p = i // 4, i % 4
                    nk = P if bk == 0 else 3 * P
                    bs = [use("scores", 2 * i + e, l) for e in range(2)]
                    for b, n in bs:
                        dve.wait_ge(full[b], n + 1)
                    if i >= 2:
                        for e in range(2):
                            tb, tn = use("probsT", 2 * (i - 2) + e, l)
                            dve.wait_ge(full[tb], tn + 1)
                    b0 = bs[0][0]
                    pr_ = probs[:, i % 2, :, 0:nk]
                    if bk == 0:
                        ins = dve.tensor_scalar(pr_, ps[:, b0:b0 + 2, 0:nk], HD ** -0.5, None, ALU.mult)
                    else:
                        ins = dve.scalar_tensor_tensor(pr_, ps[:, b0:b0 + 2, 0:nk], HD ** -0.5,
                                                       mask[:, bk - 1:bk, :].to_broadcast([P, 2, nk]), ALU.mult, ALU.add)
                    ready(ins, freed[b0], bs[0][1] + 1)
                    dve.sem_inc(freed[b0 + 1], 1)
                    s_ = st[:, i % 2, :]
                    link(dve.tensor_reduce(s_[:, 6:8], pr_, AX.X, ALU.max))
                    link(dve.scalar_tensor_tensor(s_[:, 0:2], s_[:, 6:8], -1.0, nsink[:, 2 * p:2 * p + 2], ALU.mult, ALU.min))
                    dve.tensor_tensor(s_[:, 2:4], s_[:, 0:2], sinkb[:, 2 * p:2 * p + 2], ALU.add).then_inc(sm_max, 1)

                def soft_b(i):
                    nk = P if i < 4 else 3 * P
                    s_ = st[:, i % 2, :]
                    dve.wait_ge(sm_exp, l * UNITS + (i + 1))
                    link(dve.tensor_tensor(s_[:, 6:8], s_[:, 2:4], s_[:, 4:6], ALU.add))
                    link(dve.reciprocal(s_[:, 6:8], s_[:, 6:8]))
                    for e in range(2):
                        last = dve.tensor_scalar(probs[:, i % 2, e, 0:nk], probs[:, i % 2, e, 0:nk], s_[:, 6 + e:7 + e], None, ALU.mult)
                    last.then_inc(p_r, 1)

                soft_a(0)
                dve.wait_ge(scratch0, 16 * BLOCKS)
                taps = 0
                for i in range(UNITS):
                    soft_b(i)
                    if i + 1 < UNITS:
                        soft_a(i + 1)
                    until = CK * KC * (i + 1) // UNITS
                    for n_tap in range(taps, until):
                        tap(n_tap)
                    taps = until

                modulation("mod2", 16, 48)

                b, n = use("ln", 0, l)
                dve.wait_ge(full[b], n + 1)
                ready(dve.tensor_scalar(mu[:], ps[:, b, 0:CO], 1.0 / CW, None, ALU.mult), freed[b], n + 1)
                dve.tensor_tensor(conv[:], conv[:], mu[:].unsqueeze(1).to_broadcast([P, KC, CO]), ALU.subtract).then_inc(conv_c, 1)
                def aproj(m):
                    b, n = use("aproj", m, l)
                    dve.wait_ge(full[b], n + 1)
                    dve.tensor_tensor(hT[:, m, :], ps[:, b, 0:T], gates[:, m, :], ALU.mult).then_inc(freed[b], 1)
                for m in range(4):
                    aproj(m)
                b, n = use("ln", 1, l)
                dve.wait_ge(freed[b], n + 1)
                link(dve.reciprocal(mu[:], mu[:]))
                for k in range(KC):
                    dve.tensor_tensor(conv[:, k, :], conv[:, k, :], mu[:], ALU.mult).then_inc(cn_r, 1)
                for m in range(4, KD):
                    aproj(m)
                for m in range(KD):
                    b, n = use("cproj", m, l)
                    dve.wait_ge(full[b], n + 1)
                    if m == 0:
                        for q in range(4, KD):
                            ab, an = use("aproj", q, l)
                            dve.wait_ge(freed[ab], an + 1)
                    link(dve.tensor_tensor(mixtmp[:, m % 2, :], ps[:, b, 0:T], gates[:, KD + m, :], ALU.mult))
                    dve.tensor_tensor(hT[:, m, :], hT[:, m, :], mixtmp[:, m % 2, :], ALU.add).then_inc(freed[b], 1)
                for m in range(KD):
                    b, n = use("out", m, l)
                    dve.wait_ge(full[b], n + 1)
                    dve.scalar_tensor_tensor(xT[:, m, 0:TC], ps[:, b, 0:TC], mod[:, 16 + m, 0:1], xT[:, m, 0:TC], ALU.mult, ALU.add)
                    dve.scalar_tensor_tensor(xT[:, m, TC:T], ps[:, b, TC:T], mod[:, 16 + m, 1:2], xT[:, m, TC:T],
                                             ALU.mult, ALU.add).then_inc(freed[b], 1)
                    if m >= 2:
                        add_square(l * 2 + 1, m - 1)
                add_square(l * 2 + 1, KD - 1)
                b, n = use("rms2", 0, l)
                dve.wait_ge(freed[b], n + 1)
                link(dve.reciprocal(rstd[:], rms[:]))
                norm_tiles(l * 2 + 1, 1)

                b, n = use("logitsT", 0, l)
                dve.wait_ge(full[b], n + 1)
                dve.tensor_copy(lgT[:], ps[0:NE, b, 0:T]).then_inc(freed[b], 1)
                b, n = use("logits", 0, l)
                dve.wait_ge(freed[b], n + 1)
                link(dve.tensor_tensor(se[:], sc[:], rbias[:].unsqueeze(1).to_broadcast([P, NT, NE]), ALU.add))
                s4 = se[:].rearrange("p t (g e) -> p (t g) e", e=EG)
                q = 0
                for a_ in range(EG):
                    for b_ in range(a_ + 1, EG):
                        last = dve.tensor_tensor(pair[:, :, q], s4[:, :, a_], s4[:, :, b_], ALU.add)
                        q += 1
                link(last)
                gsf = gs[:].rearrange("p t g -> p (t g)")
                link(dve.tensor_reduce(gsf, pair[:], AX.X, ALU.max))

                def first_max(out, x, tmp, downs, width):
                    link(dve.tensor_reduce(r1[:], x, AX.X, ALU.max))
                    link(dve.tensor_tensor(tmp, x, r1[:].unsqueeze(2).to_broadcast([P, NT, width]), ALU.is_equal))
                    link(dve.tensor_tensor(tmp, tmp, downs, ALU.mult))
                    link(dve.tensor_reduce(r1[:], tmp, AX.X, ALU.max))
                    link(dve.tensor_tensor(out, tmp, r1[:].unsqueeze(2).to_broadcast([P, NT, width]), ALU.is_equal))

                first_max(gt[:], gs[:], gs[:], down_g[:], NG)
                g4 = gt[:].rearrange("p t g -> p (t g)").unsqueeze(2).to_broadcast([P, NT * NG, EG])
                ra4 = ra[:].rearrange("p t (g e) -> p (t g) e", e=EG)
                rb4 = rb[:].rearrange("p t (g e) -> p (t g) e", e=EG)
                link(dve.tensor_tensor(rb4, s4, g4, ALU.mult))
                link(dve.tensor_scalar(ra4, g4, -NEG, NEG, ALU.mult, ALU.add))
                link(dve.tensor_tensor(ra[:], ra[:], rb[:], ALU.add))
                first_max(m1[:], ra[:], rb[:], down_i[:], NE)
                link(dve.scalar_tensor_tensor(ra[:], m1[:], 4 * NEG, ra[:], ALU.mult, ALU.add))
                first_max(m2[:], ra[:], rb[:], down_i[:], NE)
                dve.tensor_tensor(ra[:], m1[:], m2[:], ALU.add).then_inc(route_r, 1)
                for j, m_ in enumerate((m1, m2)):
                    link(dve.tensor_tensor(rb[:], sc[:], m_[:], ALU.mult))
                    link(dve.tensor_reduce(wk[:, j, :], rb[:], AX.X, ALU.add))
                link(dve.tensor_tensor(ws[:], wk[:, 0, :], wk[:, 1, :], ALU.add))
                link(dve.reciprocal(ws[:], ws[:]))
                dve.tensor_tensor(wk[:, 0, :], wk[:, 0, :], ws[:], ALU.mult)
                link(dve.tensor_tensor(wk[:, 1, :], wk[:, 1, :], ws[:], ALU.mult))
                b, n = use("rank", 0, l)
                dve.wait_ge(full[b], n + 1)
                link(dve.tensor_copy(cnt[:], ps[:, b, NT * NE:(NT + 1) * NE]))
                link(dve.tensor_tensor_scan(off[:], cnt[:], zero16[:], 0.0, ALU.add, ALU.add))
                link(dve.tensor_tensor(off[:], off[:], cnt[:], ALU.subtract))
                ready(dve.tensor_tensor(rb[:], ps[:, b, 0:NT * NE].rearrange("p (t n) -> p t n", t=NT),
                                        off[:].unsqueeze(1).to_broadcast([P, NT, NE]), ALU.add), freed[b], n + 1)
                for j, m_ in enumerate((m1, m2)):
                    link(dve.tensor_tensor(se[:], rb[:], m_[:], ALU.mult))
                    link(dve.tensor_reduce(posf[:, j, :], se[:], AX.X, ALU.add))
                dve.memset(rowsf[:], float(ROWS))
                link(dve.memset(full_f[:], 0.0))
                dve.tensor_copy(rowsf[:, 0:NE], off[0:1, :])
                for q in range(BLOCKS):
                    dve.tensor_scalar(orowsf[:, 0:OSTEPS].rearrange("p (e q) -> p e q", q=BLOCKS)[:, :, q], off[0:1, :],
                                      float(q * P), None, ALU.add)
                link(dve.tensor_reduce(full_f[:], cnt[0:1, :], AX.X, ALU.max))
                link(dve.tensor_scalar(full_f[:], full_f[:], float(P), None, ALU.is_gt))
                link(dve.tensor_scalar(narrow_f[:], cnt[0:1, :], float(P // 2), None, ALU.is_le))
                dve.tensor_copy(narrow_e[:], narrow_f[:])
                dve.tensor_copy(pos[:], posf[:])
                dve.tensor_copy(row_at[:], rowsf[:])
                dve.tensor_copy(orow_at[:], orowsf[:])
                dve.tensor_copy(overfull[:], full_f[:]).then_inc(pos_r, 1)
                dve.wait_ge(pos_r, l + 1)
                settle(dve)

                with dve.Fori(0, NE) as e:
                    moe_dve(full, freed, lambda b: l * PER[b] + e + (INIT[b] + MOE_AT[b]),
                            dve.value_load(narrow_e[0:1, bass.ds(e, 1)], min_val=0, max_val=1))
                over = dve.value_load(overfull[0:1, 0:1], min_val=0, max_val=1)
                with dve.If(over > 0):
                    with dve.Fori(0, OSTEPS) as i:
                        moe_dve(full_o, freed_o, lambda b: l * OSTEPS + i + 1)
                with dve.Else():
                    for b in (3, 4):
                        dve.sem_inc(freed_o[b], OSTEPS)
                dve.nop()

                for t in range(NT):
                    dve.wait_ge(gat[t], l * 32 + 32)
                    link(dve.tensor_scalar(nat[:, t, :], gath[:, 2 * t, :], wk[:, 0, t:t + 1], None, ALU.mult))
                    dve.scalar_tensor_tensor(nat[:, t, :], gath[:, 2 * t + 1, :], wk[:, 1, t:t + 1], nat[:, t, :],
                                             ALU.mult, ALU.add).then_inc(comb_r, 1)
                for i in range(6):
                    b, n = use("y", i, l)
                    dve.wait_ge(full[b], n + 1)
                    t, h = i // 2, i % 2
                    for k in range(4):
                        kk = 4 * h + k
                        x_ = xT[:, kk, t * P:(t + 1) * P]
                        last = dve.scalar_tensor_tensor(x_, ps[:, b, k * P:(k + 1) * P], mod[:, 40 + kk, min(t, 1):min(t, 1) + 1],
                                                        x_, ALU.mult, ALU.add)
                    last.then_inc(freed[b], 1)
                assert steps[0] <= CHAIN, steps
                dve.sem_inc(chain, CHAIN - steps[0])

            add_squares(2 * DEPTH)
            dve.wait_ge(freed[3], DEPTH * PER[3] + INIT[3] + 1)
            dve.reciprocal(rstd[:], rms[:]).then_inc(chain, 1)
            dve.wait_ge(chain, DEPTH * CHAIN + BASE + 1)
            norm_tiles(2 * DEPTH)


INPUTS = ["x_prompt", "x_sample", "cache_k", "cache_v", "c", "c_ctx", "w_ada", "w_in", "w_attn_proj", "w_conv_proj",
          "w_out", "w_router", "router_bias", "w_e_gate", "w_e_up", "w_e_down", "final_norm"]
OUTPUTS = [("y_prompt", (1, TC, D)), ("y_sample", (1, TL, D)), ("new_k", (1, DEPTH, TC, NKV, HD)),
           ("new_v", (1, DEPTH, TC, NKV, HD))]


def kernel(**inputs):
    import numpy as np
    import concourse.bacc as bacc
    from concourse.bass_utils import run_bass_kernel_spmd as run

    nc = bacc.Bacc("TRN2", target_bir_lowering=False, num_devices=1)
    arrays = {name: np.ascontiguousarray(inputs[name]) for name in INPUTS}
    def packed(names, shape):
        rows = np.concatenate([np.asarray(inputs[name]).reshape(DEPTH, -1) for name in names], axis=1)
        return np.concatenate([rows, np.zeros_like(rows[:1])]).reshape(DEPTH + 1, *shape)

    arrays["features"] = packed(["b_ada", "norm1", "norm2", "dw_b", "cln_g", "cln_b"], (76, P))
    arrays["taps"] = packed(["dw_w"], (CK * KC, P))
    arrays["every"] = packed(["q_norm", "k_norm", "sink"], (2 * HD + NH,))
    grid_w, pairs = 64, HD // 4
    inv = (np.float32(10000.0) ** (-np.arange(pairs, dtype=np.float32) / np.float32(pairs))).astype(np.float32)
    tok = np.arange(TL)
    halves = [(tok // grid_w).astype(np.float32)[:, None] * inv, (tok % grid_w).astype(np.float32)[:, None] * inv]
    cos = np.concatenate([np.cos(h) for h in halves for _ in range(2)], axis=1)
    sin = np.concatenate([s * np.sin(h) for h in halves for s in (-1, 1)], axis=1)
    arrays["rope"] = np.stack([cos, sin], axis=1).astype(np.float32)
    A = {}
    for name, a in arrays.items():
        A[name] = nc.dram_tensor("in_" + name, a.shape, mybir.dt.from_np(a.dtype), kind="ExternalInput").ap()
    for name, shape in OUTPUTS:
        A[name] = nc.dram_tensor("out_" + name, shape, F32, kind="ExternalOutput").ap()
    build(nc, A)
    r = run(nc, [{"in_" + name: a for name, a in arrays.items()}], core_ids=[0])
    return tuple(r.results[0]["out_" + name] for name, _ in OUTPUTS)
```

```python
from contextlib import ExitStack

import concourse.bass as bass
from concourse import mybir

F32 = mybir.dt.float32
F32R = mybir.dt.float32r
I32 = mybir.dt.int32
BF16 = mybir.dt.bfloat16
ALU = mybir.AluOpType
ACT = mybir.ActivationFunctionType
AX = mybir.AxisListType

P = 128
D = 1024
KD = D // P
DEPTH = 2
TC, TL = 128, 256
T = TC + TL
NT = T // P
HD = 64
NH, NKV = 8, 2
AW, KVW = NH * HD, NKV * HD
CW = D // 2
KC = CW // P
CK, PAD = 31, 15
NE, NG, EG = 16, 4, 4
DE = 512
KE = DE // P
EPS = 1e-6
NEG = -1e30
SEG = TC + 2 * PAD
UW = SEG + TL + 2 * PAD
CO = UW - 2 * PAD
LAT0 = SEG
ROWS = 2 * T
HALF = ROWS // 2
BLOCKS = NT
PLACES = ROWS + P

SLOTS = 6
SLOT = 2048
MOE_CHUNKS = 6
CHUNKS = [("ada", g, c) for g in range(4) for c in range(2)]
CHUNKS += [("qkv", c, 0) for c in range(3)] + [("u", c, 0) for c in range(4)]
for _g in range(8):
    CHUNKS += [("gate", _g, 0), ("ada", 4 + _g, 0), ("ada", 4 + _g, 1)]
CHUNKS += [("aproj", 0, 0), ("aproj", 1, 0), ("cproj", 0, 0), ("cproj", 1, 0)]
CHUNKS += [("out", c, 0) for c in range(4)] + [("router", 0, 0)]
SPLIT = [("cproj", 0), ("cproj", 1), ("out", 0), ("out", 1), ("out", 2), ("out", 3)]
CHUNK_AT = {c: i for i, c in enumerate(CHUNKS)}
NCHUNKS = len(CHUNKS)
assert NCHUNKS % SLOTS == 0
SLOT_USES = (NCHUNKS + MOE_CHUNKS * NE) // SLOTS

UNITS = NT * NH // 2
FILLERS = []
for _g in range(8):
    FILLERS += [("gate", 2 * _g), ("gate", 2 * _g + 1), ("ada2", _g)]
assert len(FILLERS) == 2 * UNITS


def attention_uses():
    uses = [("scores", [0, 1])]
    for i in range(UNITS):
        if i + 1 < UNITS:
            uses += [("scores", [0, 1])]
        uses += [(FILLERS[2 * i][0], [2]), ("probsT", [4, 5]), (FILLERS[2 * i + 1][0], [3]), ("pv", [6])]
    return uses


INIT_USES = [("x", [0, 1, 0, 1, 0, 1]), ("cond", [7])]
PRE_USES = [
    ("params", [7]), ("ada", [0, 1] * 2), ("mod", [2]), ("rms1", [3]),
    ("qkv", [4, 5, 6] * 3), ("u", [0, 1, 2, 3] * 2), ("qT", [4, 5, 6]), ("kT", [7, 4]),
    ("mod2", [7]), *attention_uses(), ("ln", [2, 4]), ("aproj", [0, 1, 2, 3] * 2), ("cproj", [4, 5, 6, 7] * 2),
    ("out", [0, 1, 2, 3] * 2), ("rms2", [4]), ("logitsT", [5]), ("h2n", [0, 1, 2, 3, 4, 7]),
    ("logits", [6]), ("rank", [5]), ("spread", [0, 1, 2, 3] * 4),
]
MOE_USES = {0: 2, 1: 2, 2: 1, 3: 1, 4: 2, 5: 1, 6: 1, 7: 2}
SUM_BANKS = [(0, 0), (1, 0), (4, 1), (7, 1), (0, 1), (1, 1)]
POST_USES = [("y", [0, 1, 7] * 2)]


def bank_table():
    init = [0] * 8
    table = {}
    for stage, banks in INIT_USES:
        table[stage] = []
        for b in banks:
            table[stage].append((b, init[b]))
            init[b] += 1
    at = [0] * 8
    for stage, banks in PRE_USES:
        table.setdefault(stage, [])
        for b in banks:
            table[stage].append((b, at[b]))
            at[b] += 1
    moe = list(at)
    for b, n in MOE_USES.items():
        at[b] += n * NE
    for stage, banks in POST_USES:
        table[stage] = []
        for b in banks:
            table[stage].append((b, at[b]))
            at[b] += 1
    return table, [n + 1 for n in init], moe, at


def build(nc, A):
    USES, INIT, MOE_AT, PER = bank_table()
    ctx = ExitStack()
    with ctx:
        start_of = {}

        def sb(name, shape, dt=F32):
            start_of[name] = (nc.sbuf_base + 31) // 32 * 32
            return ctx.enter_context(nc.sbuf_tensor(name, shape, dt))

        def sem(name):
            return ctx.enter_context(nc.semaphore(name))

        ring = [sb(f"ring{s}", [P, SLOT]) for s in range(SLOTS)]
        xT = sb("xT", [P, KD, T])
        hT = sb("hT", [P, KD, T])
        nat = sb("nat", [P, NT, D])
        qkv = sb("qkv", [P, NT, 768])
        qtmp = sb("qtmp", [P, NT, 640])
        qtmp2 = sb("qtmp2", [P, 2, 640])
        kdup = sb("kdup", [P, 4, 2, P])
        qT = sb("qT", [P, 4, T])
        kT = sb("kT", [P, 2, 4 * P])
        cache_k = sb("cache_k_sb", [P, P])
        cache_v = sb("cache_v_sb", [P, P])
        ub = sb("ub", [P, KC, UW])
        sig = sb("sig", [P, 2, T])
        conv = sb("conv", [P, KC, CO])
        csq = sb("csq", [P, KC, CO])
        mix = sb("mix", [P, 2 * KD * T + 4 * T])
        gates = mix[:, 0:2 * KD * T].rearrange("p (m n) -> p m n", n=T)
        attnT = mix[:, 2 * KD * T:].rearrange("p (m n) -> p m n", n=T)
        squared = gates[:, 0:KD, :]
        probs = sb("probs", [P, 2, 2, 3 * P])
        probsT = sb("probsT", [P, 2, 3, P])
        mixtmp = sb("mixtmp", [P, 2, T])
        rstd = sb("rstd", [P, T])
        rms = sb("rms", [P, T])
        mu = sb("mu", [P, CO])
        def flat(t, a, z):
            return t[:].rearrange("p a b -> p (a b)")[:, a:z]

        sortedT = mix[:, 0:KD * PLACES].rearrange("p (k n) -> p k n", k=KD)

        def placed_over(name, first, at, shape, dt=F32R):
            return nc.alloc_sbuf_tensor_at(name, shape, dt, offset=start_of[first] + 4 * at)

        place = placed_over("place", "hT", 0, [P, NT, ROWS])
        h_hi = placed_over("h_hi", "nat", 0, [P, KD, T])
        h_lo = placed_over("h_lo", "conv", 0, [P, KD, T])
        u_hi = [placed_over(f"u_hi{c}", "mix", c * SLOT, [P, SLOT]) for c in range(3)]
        u_hi.append(placed_over("u_hi3", "probs", 0, [P, SLOT]))
        assert start_of["mix"] >= start_of["conv"] + KD * T * 4 and start_of["mixtmp"] >= start_of["probs"] + SLOT * 4
        w_hi = placed_over("w_hi", "qkv", 0, [P, 3, SLOT])
        w_lo = [placed_over(f"w_lo{s}", f"ring{s}", 0, [P, SLOT]) for s in range(SLOTS)]
        conv_hi = placed_over("conv_hi", "qT", 0, [P, KC, T])
        conv_lo = placed_over("conv_lo", "csq", 0, [P, KC, CO])
        merged_hi = placed_over("merged_hi", "nat", 0, [P, KD, T])
        merged_lo = placed_over("merged_lo", "hT", 0, [P, KD, T])
        assert start_of["qT"] >= start_of["qkv"] + 3 * SLOT * 4
        nat_hi = placed_over("nat_hi", "qkv", 0, [P, NT, D])
        nat_lo = placed_over("nat_lo", "qkv", NT * D, [P, NT, D])
        assert start_of["qT"] >= start_of["qkv"] + 2 * NT * D * 4
        hid = flat(csq, 0, DE)
        silu = flat(csq, DE, 2 * DE)
        hidT = flat(conv, 0, DE).rearrange("p (k n) -> p k n", k=KE)
        own = flat(conv, DE, DE + NT * P).rearrange("p (t n) -> p t n", t=NT)
        orow_hi = placed_over("orow_hi", "qkv", D, [P, D])
        orow_lo = placed_over("orow_lo", "qkv", 2 * D, [P, D])
        ownT = placed_over("ownT", "qkv", 3 * D, [P, NT * P])
        xgT = placed_over("xgT", "probs", 0, [P, KD, P], F32)
        count768 = flat(kT, 0, ROWS)
        count64 = flat(kT, ROWS, ROWS + P)
        rank_at = flat(qT, 0, NT * BLOCKS * NE).rearrange("p (t n) -> p t n", t=NT)
        weight = flat(qT, NT * BLOCKS * NE, 2 * NT * BLOCKS * NE).rearrange("p (t n) -> p t n", t=NT)
        ident = sb("ident", [P, P])
        ones = sb("ones", [P, P])
        before = sb("before", [P, P])
        ones_b = sb("ones_b", [P, P], BF16)
        before_b = sb("before_b", [P, P], BF16)
        chosen_b = sb("chosen_b", [P, NT, NE], BF16)
        sel = sb("sel", [P, 2])
        mask = sb("mask", [P, 2, 3 * P])
        rope = sb("rope", [P, 2, 2, HD])
        eps = sb("eps", [P, 1])
        crow = sb("crow", [24, P])
        fnorm = sb("fnorm", [P, KD])
        condT = sb("condT", [P, KD, 32])
        csig = sb("csig", [P, 16])
        modrow = nat[:, 0, :].rearrange("p (i n) -> p i n", i=2)
        prow = sb("prow", [76, P])
        dwrow = sb("dwrow", [CK * KC, P])
        par = sb("par", [P, 76])
        dw = sb("dw", [P, CK * KC])
        mod = sb("mod", [P, 48, 2])
        coef = sb("coef", [P, 2, KD, 2])
        every = sb("every", [P, 2 * HD + NH])
        qkn = every[:, 0:2 * HD].rearrange("p (i d) -> p i d", i=2)
        sinkb = every[:, 2 * HD:]
        nsink = sb("nsink", [P, NH])
        rbias = sb("rbias", [P, NE])
        ss = sb("ss", [P, NT * 10])
        st = sb("st", [P, 2, 8])
        lgT = sb("lgT", [NE, T])
        sc = sb("sc", [P, NT, NE])
        se = sb("se", [P, NT, NE])
        m1 = sb("m1", [P, NT, NE])
        m2 = sb("m2", [P, NT, NE])
        ra = sb("ra", [P, NT, NE])
        rb = sb("rb", [P, NT, NE])
        pair = sb("pair", [P, NT * NG, 6])
        gs = sb("gs", [P, NT, NG])
        gt = sb("gt", [P, NT, NG])
        r1 = sb("r1", [P, NT])
        wk = sb("wk", [P, 2, NT])
        ws = sb("ws", [P, NT])
        cnt = sb("cnt", [P, NE])
        off = sb("off", [P, NE])
        down_i = sb("down_i", [P, NT, NE])
        down_g = sb("down_g", [P, NT, NG])
        zero16 = sb("zero16", [P, NE])
        posf = sb("posf", [P, 2, NT])
        placef = sb("placef", [1, BLOCKS * NE + 1])
        place_at = sb("place_at", [1, BLOCKS * NE + 1], I32)
        narrow_f = sb("narrow_f", [1, NE])
        narrow_e = sb("narrow_e", [1, NE], I32)
        full_f = sb("full_f", [1, 1])
        overfull = sb("overfull", [1, 1], I32)

        ps = ctx.enter_context(nc.psum_tensor("ps", [P, 8, 512], F32))

        landed = [sem(f"landed{s}") for s in range(SLOTS)]
        full = [sem(f"full{b}") for b in range(8)]
        freed = [sem(f"freed{b}") for b in range(8)]
        settled = sem("settled")
        half = sem("half")
        consts = sem("consts")
        consts_v = sem("consts_v")
        consts2 = sem("consts2")
        chain_p = sem("chain_p")
        x_in = sem("x_in")
        c_in = sem("c_in")
        t_in = sem("t_in")
        counts_r = sem("counts_r")
        ends_zero = sem("ends_zero")
        place_r = sem("place_r")
        own_r = sem("own_r")
        own_r_o = sem("own_r_o")
        xg_r = sem("xg_r")
        xg_r_o = sem("xg_r_o")
        nat_hi_r = sem("nat_hi_r")
        h_hi_r = sem("h_hi_r")
        h_split = sem("h_split")
        u_hi_r = sem("u_hi_r")
        u_split = sem("u_split")
        w_hi_r = sem("w_hi_r")
        w_split = sem("w_split")
        conv_hi_r = sem("conv_hi_r")
        conv_split = sem("conv_split")
        merged_hi_r = sem("merged_hi_r")
        merged_split = sem("merged_split")
        orow_hi_r = sem("orow_hi_r")
        orow_hi_r_o = sem("orow_hi_r_o")
        sums_zero = sem("sums_zero")
        par_in = sem("par_in")
        bc_in = sem("bc_in")
        cache_in = sem("cache_in")
        csig_r = sem("csig_r")
        modrow_used = sem("modrow_used")
        mod_r = sem("mod_r")
        xsq = sem("xsq")
        sq_added = sem("sq_added")
        sq_sum = sem("sq_sum")
        xn_r = sem("xn_r")
        h_r = sem("h_r")
        h_ctx = sem("h_ctx")
        usig_used = sem("usig_used")
        qsq_r = sem("qsq_r")
        qss_r = sem("qss_r")
        qrms_r = sem("qrms_r")
        k_pre = sem("k_pre")
        q_r = sem("q_r")
        kv_out = sem("kv_out")
        sm_max = sem("sm_max")
        sm_exp = sem("sm_exp")
        p_r = sem("p_r")
        conv_c = sem("conv_c")
        csq_r = sem("csq_r")
        cn_r = sem("cn_r")
        convT_r = sem("convT_r")
        route_r = sem("route_r")
        pos_r = sem("pos_r")
        chain = sem("chain")
        tapped = sem("tapped")
        y_out = sem("y_out")
        landed_o = [sem(f"landed_o{s}") for s in range(SLOTS)]
        full_o = [sem(f"full_o{b}") for b in range(8)]
        freed_o = [sem(f"freed_o{b}") for b in range(8)]
        half_o = sem("half_o")

        CHAIN = 200
        OSTEPS = NE * (BLOCKS - 1)

        def use(stage, i, l):
            b, n = USES[stage][i]
            return b, l * PER[b] + (INIT[b] + n)

        def init_use(stage, i):
            b, n = USES[stage][i]
            return b, n + 1

        def expert_use(b, l, e):
            return l * PER[b] + e * MOE_USES[b] + (INIT[b] + MOE_AT[b])

        def further_use(b, l, i):
            return l * (OSTEPS * MOE_USES[b]) + i * MOE_USES[b] + 1

        def by_width(eng, e, step):
            narrow = eng.value_load(narrow_e[0:1, bass.ds(e, 1)], min_val=0, max_val=1)
            with eng.If(narrow > 0):
                step(True)
            with eng.Else():
                step(False)
            eng.nop()

        w_ada = A["w_ada"].rearrange("l (c k p) n -> l c p k n", c=2, p=P)
        w_in = A["w_in"].rearrange("l (k p) n -> l p k n", p=P)
        w_ap = A["w_attn_proj"].rearrange("l (k p) n -> l p k n", p=P)
        w_cp = A["w_conv_proj"].rearrange("l (k p) n -> l p k n", p=P)
        w_out = A["w_out"].rearrange("l (k p) n -> l p k n", p=P)
        w_r = A["w_router"].rearrange("(k p) n -> p k n", p=P)
        w_g = A["w_e_gate"].rearrange("l e (k p) n -> (l e) p k n", p=P)
        w_u = A["w_e_up"].rearrange("l e (k p) n -> (l e) p k n", p=P)
        w_d = A["w_e_down"].rearrange("l e (k p) n -> (l e) p k n", p=P)

        def chunk_end(c):
            kind, i, part = CHUNKS[c]
            if kind == "ada":
                return ("half", i) if part == 0 else (("ada", i) if i < 4 else ("ada2", i - 4))
            return {"qkv": ("qkv", 3 * i + 2), "u": ("u", 2 * i + 1), "gate": ("gate", 2 * i + 1),
                    "aproj": ("aproj", 4 * i + 3), "cproj": ("cproj", 4 * i + 3), "out": ("out", 2 * i + 1),
                    "router": ("logitsT", 0)}[kind]

        HALF_PER = 12 + 2 * NE

        def settle(eng):
            eng.sem_inc(settled, 1)

        with nc.Block() as start:
            @start.sync
            def _(sp):
                for s in [*full, *freed, half, *full_o, *freed_o, half_o, own_r, own_r_o, xg_r, xg_r_o, orow_hi_r, orow_hi_r_o]:
                    sp.sem_inc(s, 1)

        block = ctx.enter_context(nc.Block())

        @block.sync
        def _(sp):
            def wait_chunk_used(c, l):
                stage, i = chunk_end(c)
                if stage == "half":
                    sp.wait_ge(half, l * HALF_PER + (i + 2))
                else:
                    b, n = use(stage, i, l)
                    sp.wait_ge(full[b], n + 1)

            def load(slot, landed_sem, src):
                n = src.shape[-1]
                k = src.shape[-2]
                dst = ring[slot][:, 0:k * n].rearrange("p (k n) -> p k n", k=k)
                sp.dma_start(dst, src).then_inc(landed_sem, 16)

            def expert_chunk(j, w):
                if j < 4:
                    src = w_g if j < 2 else w_u
                    return src[bass.ds(w, 1), :, :, (j % 2) * 256:(j % 2 + 1) * 256].rearrange("o p k n -> p (o k) n")
                return w_d[bass.ds(w, 1), :, :, (j - 4) * 512:(j - 3) * 512].rearrange("o p k n -> p (o k) n")

            for t in range(NT):
                src = A["x_prompt"][0] if t == 0 else A["x_sample"][0, (t - 1) * P:t * P, :]
                sp.dma_start(nat[:, t, :], src).then_inc(x_in, 16)

            with sp.Fori(0, DEPTH) as l:
                for c in range(NCHUNKS):
                    s = c % SLOTS
                    if c < SLOTS:
                        if c in (0, 2):
                            sp.wait_ge(half, l * HALF_PER + 1)
                        else:
                            b = {1: 2, 3: 3, 4: 5, 5: 6}[c]
                            sp.wait_ge(full[b], l * PER[b] + INIT[b])
                    else:
                        wait_chunk_used(c - SLOTS, l)
                    kind, i, part = CHUNKS[c]
                    if kind == "ada":
                        src = w_ada[bass.ds(l, 1), part, :, :, i * 512:(i + 1) * 512].rearrange("o p k n -> p (o k) n")
                    elif kind in ("aproj", "cproj"):
                        w = w_ap if kind == "aproj" else w_cp
                        src = w[bass.ds(l, 1), :, :, i * 512:(i + 1) * 512].rearrange("o p k n -> p (o k) n")
                    elif kind == "router":
                        src = w_r
                    else:
                        w = w_out if kind == "out" else w_in
                        m = i + {"qkv": 0, "u": 3, "gate": 7, "out": 0}[kind]
                        src = w[bass.ds(l, 1), :, :, m * 256:(m + 1) * 256].rearrange("o p k n -> p (o k) n")
                    load(s, landed[s], src)
                for j in range(MOE_CHUNKS):
                    wait_chunk_used(NCHUNKS - SLOTS + j, l)
                    load(j, landed[j], expert_chunk(j, l * NE))
                with sp.Fori(1, NE) as e:
                    for j in range(MOE_CHUNKS):
                        if j in (0, 2):
                            sp.wait_ge(half, l * HALF_PER + e * 2 + (12 - 2 + (2 if j == 0 else 3)))
                        else:
                            b = {1: 2, 3: 3, 4: 5, 5: 6}[j]
                            sp.wait_ge(full[b], l * PER[b] + e + (INIT[b] + MOE_AT[b]))
                        load(j, landed[j], expert_chunk(j, l * NE + e))

                sp.wait_ge(pos_r, l + 1)
                settle(sp)
                over = sp.value_load(overfull[0:1, 0:1], min_val=0, max_val=1)
                with sp.If(over > 0):
                    sp.wait_ge(full[6], l * PER[6] + (INIT[6] + MOE_AT[6] + NE))
                    settle(sp)
                    with sp.Fori(0, BLOCKS - 1) as q:
                        with sp.Fori(0, NE) as e:
                            for j in range(MOE_CHUNKS):
                                if j in (0, 2):
                                    sp.wait_ge(half_o, l * (2 * OSTEPS) + q * (2 * NE) + e * 2 + 1)
                                else:
                                    b = {1: 2, 3: 3, 4: 5, 5: 6}[j]
                                    sp.wait_ge(full_o[b], l * OSTEPS + q * NE + e + 1)
                                load(j, landed_o[j], expert_chunk(j, l * NE + e))
                    sp.wait_ge(full_o[6], l * OSTEPS + (OSTEPS + 1))
                    settle(sp)
                with sp.Else():
                    for s in range(SLOTS):
                        sp.sem_inc(landed_o[s], 16 * OSTEPS)
                sp.nop()

        def conv_tokens(k):
            return csq[:, k, 0:T]

        @block.tensor
        def _(pe):
            def begin(b, n):
                pe.wait_ge(freed[b], n)

            def chunk_in(c, l):
                pe.wait_ge(landed[c % SLOTS], l * (16 * SLOT_USES) + 16 * (c // SLOTS + 1))

            pe.wait_ge(consts, 3)
            pe.wait_ge(x_in, 48)
            for i in range(6):
                b, n = init_use("x", i)
                begin(b, n)
                t, h = i // 2, i % 2
                for k in range(4):
                    last = pe.transpose(ps[:, b, k * P:(k + 1) * P], nat[:, t, (4 * h + k) * P:(4 * h + k + 1) * P], ident[:])
                last.then_inc(full[b], 1)
            pe.wait_ge(c_in, 48)
            pe.wait_ge(chain_p, 8)
            pe.matmul(ps[:, 7, 0:24], crow[:, :], ident[0:24, 0:24], start=True, stop=True).then_inc(full[7], 1)
            pe.wait_ge(freed[7], 2)

            def expert_parts(n_of, fr, fs, landed_s, land_at, half_s, own_s, own_at, xg_s, xg_at):
                def products(which, b, small):
                    pe.wait_ge(fr[b], n_of(b))
                    pe.wait_ge(xg_s, xg_at)
                    if small:
                        for hh in range(2):
                            pe.wait_ge(landed_s[2 * which + hh], land_at)
                        for k in range(KD):
                            for hh in range(2):
                                last = pe.matmul(ps[64 * hh:64 * hh + 64, b, 0:256], xgT[:, k, 0:64],
                                                 ring[2 * which + hh][:, k * 256:(k + 1) * 256],
                                                 start=(k == 0), stop=(k == KD - 1))
                                if k == KD - 1:
                                    last.then_inc(half_s if hh == 0 else fs[b], 1)
                        return
                    for hh in range(2):
                        s = 2 * which + hh
                        pe.wait_ge(landed_s[s], land_at)
                        for k in range(KD):
                            last = pe.matmul(ps[:, b, hh * 256:(hh + 1) * 256], xgT[:, k, :],
                                             ring[s][:, k * 256:(k + 1) * 256], start=(k == 0), stop=(k == KD - 1))
                        last.then_inc(half_s if hh == 0 else fs[b], 1)

                def turn_own():
                    pe.wait_ge(own_s, own_at)
                    pe.wait_ge(fr[7], n_of(7))
                    for t in range(NT):
                        last = pe.transpose(ps[:, 7, t * P:(t + 1) * P], own[:, t, :], ident[:])
                    last.then_inc(fs[7], 1)

                def down(small):
                    pe.wait_ge(fr[3], n_of(3) + 1)
                    pe.wait_ge(fr[4], n_of(4))
                    for k in range(2 if small else KE):
                        last = pe.transpose(ps[:, 4, k * P:(k + 1) * P], hid[:, k * P:(k + 1) * P], ident[:])
                    last.then_inc(fs[4], 1)
                    turn_own()
                    pe.wait_ge(fr[4], n_of(4) + 1)
                    if small:
                        for h in range(2):
                            pe.wait_ge(fr[5 + h], n_of(5 + h))
                            pe.wait_ge(landed_s[4 + h], land_at)
                        for k in range(KE):
                            for h in range(2):
                                last = pe.matmul(ps[64 * h:64 * h + 64, 5 + h, :], hidT[:, k % 2, 64 * (k // 2):64 * (k // 2) + 64],
                                                 ring[4 + h][:, k * 512:(k + 1) * 512], start=(k == 0), stop=(k == KE - 1))
                                if k == KE - 1:
                                    last.then_inc(fs[5 + h], 1)
                        return
                    for h in range(2):
                        pe.wait_ge(fr[5 + h], n_of(5 + h))
                        pe.wait_ge(landed_s[4 + h], land_at)
                        for k in range(KE):
                            last = pe.matmul(ps[:, 5 + h, :], hidT[:, k, :], ring[4 + h][:, k * 512:(k + 1) * 512],
                                             start=(k == 0), stop=(k == KE - 1))
                        last.then_inc(fs[5 + h], 1)

                def gate_up(small):
                    products(0, 2, small)
                    products(1, 3, small)

                return gate_up, down

            def back(n_of, fr, fs, small):
                pe.wait_ge(fr[7], n_of(7) + 1)
                for h in range(2):
                    pe.wait_ge(fr[5 + h], n_of(5 + h) + 1)
                for t in range(NT):
                    for h in range(2):
                        b, u = SUM_BANKS[2 * t + h]
                        pe.wait_ge(fr[b], n_of(b) + u)
                        a, z, o = (64 * h, 64 * h + 64, 0) if small else (0, P, 512 * h)
                        pe.matmul(ps[:, b, :], ownT[a:z, t * P:(t + 1) * P], orow_hi[a:z, o:o + 512], start=True, stop=False)
                        pe.matmul(ps[:, b, :], ownT[a:z, t * P:(t + 1) * P], orow_lo[a:z, o:o + 512],
                                  start=False, stop=True).then_inc(fs[b], 1)

            def rms_sum(stage, l, q):
                b, n = use(stage, 0, l)
                begin(b, n)
                pe.wait_ge(sq_sum, q + 1)
                pe.matmul(ps[:, b, 0:T], ones[:], rstd[:], start=True, stop=True).then_inc(full[b], 1)

            with pe.Fori(0, DEPTH) as l:
                b, n = use("params", 0, l)
                begin(b, n)
                pe.wait_ge(par_in, l * 32 + 32)
                pe.matmul(ps[:, b, 0:76], prow[:, :], ident[0:76, 0:76], start=True, stop=True)
                pe.matmul(ps[:, b, 128:128 + CK * KC], dwrow[:, :], ident[0:CK * KC, 0:CK * KC],
                          start=True, stop=True).then_inc(full[b], 1)

                def ada_group(g):
                    stage, q = ("ada", g) if g < 4 else ("ada2", g - 4)
                    b, n = use(stage, q, l)
                    begin(b, n)
                    for cc in range(2):
                        c = CHUNK_AT["ada", g, cc]
                        chunk_in(c, l)
                        for k in range(4):
                            last = pe.matmul(ps[32 * k:32 * k + 32, b, :], condT[:, 4 * cc + k, :],
                                             ring[c % SLOTS][:, k * 512:(k + 1) * 512], start=(cc == 0), stop=(cc == 1))
                        last.then_inc(half if cc == 0 else full[b], 1)

                def mod_cols(g):
                    mb, mn = use("mod" if g < 4 else "mod2", 0, l)
                    ab, an = use("ada", g, l) if g < 4 else use("ada2", g - 4, l)
                    pe.wait_ge(freed[ab], an + 1)
                    if g in (0, 4):
                        begin(mb, mn)
                    for m in range(4):
                        last = pe.matmul(ps[:, mb, 2 * (4 * g + m):2 * (4 * g + m) + 2],
                                         modrow[:, g % 2, m * P:(m + 1) * P], sel[:, :], start=True, stop=True)
                    last.then_inc(full[mb] if g in (3, 11) else modrow_used, 1)

                for g in range(4):
                    ada_group(g)
                    if g >= 1:
                        mod_cols(g - 1)
                    if g == 1:
                        rms_sum("rms1", l, l * 2)
                mod_cols(3)

                def h_wait(which, k):
                    pe.wait_ge(h_ctx, l * (2 * KD) + (which * KD + k + 1))
                    pe.wait_ge(h_r, l * (2 * KD) + (which * KD + k + 1))

                for c in range(3):
                    q = CHUNK_AT["qkv", c, 0]
                    chunk_in(q, l)
                    for t in range(NT):
                        b, n = use("qkv", 3 * c + t, l)
                        begin(b, n)
                        for k in range(KD):
                            if c == 0 and t == 0:
                                h_wait(0, k)
                            last = pe.matmul(ps[:, b, 0:256], hT[:, k, t * P:(t + 1) * P],
                                             ring[q % SLOTS][:, k * 256:(k + 1) * 256], start=(k == 0), stop=(k == KD - 1))
                        last.then_inc(full[b], 1)

                def wide(stage, m, k_tiles, per_chunk, rhs):
                    c = CHUNK_AT[stage, m // per_chunk, 0]
                    if m % per_chunk == 0:
                        chunk_in(c, l)
                    b, n = use(stage, m, l)
                    begin(b, n)
                    w = per_chunk * P
                    for k in range(k_tiles):
                        o = k * w + (m % per_chunk) * P
                        last = pe.matmul(ps[:, b, 0:T], ring[c % SLOTS][:, o:o + P], rhs(k),
                                         start=(k == 0), stop=(k == k_tiles - 1))
                    last.then_inc(full[b], 1)

                def wide_split(stage, m, k_tiles, per_chunk, hi, lo):
                    c = m // per_chunk
                    if stage == "u":
                        weights_hi, split, n_split = u_hi[c][:], u_split, l * KC + (c + 1)
                    else:
                        q = SPLIT.index((stage, c))
                        weights_hi, split, n_split = w_hi[:, q % 3, :], w_split, l * len(SPLIT) + (q + 1)
                    if m % per_chunk == 0:
                        pe.wait_ge(split, n_split)
                    b, n = use(stage, m, l)
                    begin(b, n)
                    w = per_chunk * P
                    lower = w_lo[CHUNK_AT[stage, m // per_chunk, 0] % SLOTS]
                    for k in range(k_tiles):
                        o = k * w + (m % per_chunk) * P
                        upper = weights_hi[:, o:o + P]
                        pe.matmul(ps[:, b, 0:T], upper, hi[:, k, 0:T], start=(k == 0), stop=False)
                        pe.matmul(ps[:, b, 0:T], upper, lo[:, k, 0:T], start=False, stop=False)
                        last = pe.matmul(ps[:, b, 0:T], lower[:, o:o + P], hi[:, k, 0:T], start=False, stop=(k == k_tiles - 1))
                    last.then_inc(full[b], 1)

                pe.wait_ge(h_split, l * KD + KD)
                for m in range(2 * KC):
                    wide_split("u", m, KD, 2, h_hi, h_lo)

                def filler(j):
                    kind, q = FILLERS[j]
                    if kind == "gate":
                        wide("gate", q, KD, 2, lambda k: hT[:, k, :])
                    else:
                        ada_group(4 + q)
                        if q > 0:
                            mod_cols(3 + q)

                pe.wait_ge(q_r, l + 1)
                for t in range(NT):
                    b, n = use("qT", t, l)
                    begin(b, n)
                    for p in range(4):
                        last = pe.transpose(ps[:, b, p * P:(p + 1) * P], qkv[:, t, p * P:(p + 1) * P], ident[:])
                    last.then_inc(full[b], 1)
                for i in range(2):
                    b, n = use("kT", i, l)
                    begin(b, n)
                    for j in range(4):
                        last = pe.transpose(ps[:, b, j * P:(j + 1) * P], kdup[:, 2 * i + j // 2, j % 2, :], ident[:])
                    last.then_inc(full[b], 1)

                units = [(bk, p) for bk in range(NT) for p in range(4)]

                def scores(i):
                    bk, p = units[i]
                    if i == 0:
                        for st_, q in (("qT", 0), ("qT", 1), ("qT", 2), ("kT", 0), ("kT", 1)):
                            b, n = use(st_, q, l)
                            pe.wait_ge(freed[b], n + 1)
                    k0, nk = (0, P) if bk == 0 else (P, 3 * P)
                    for e in range(2):
                        b, n = use("scores", 2 * i + e, l)
                        begin(b, n)
                        pe.matmul(ps[:, b, 0:nk], qT[64 * e:64 * e + 64, p, bk * P:(bk + 1) * P],
                                  kT[64 * e:64 * e + 64, p // 2, k0:k0 + nk], start=True, stop=True).then_inc(full[b], 1)

                def turn_probs(i):
                    bk, p = units[i]
                    pe.wait_ge(p_r, l * UNITS + (i + 1))
                    for e in range(2):
                        b, n = use("probsT", 2 * i + e, l)
                        begin(b, n)
                        for kt in range(1 if bk == 0 else 3):
                            last = pe.transpose(ps[:, b, kt * P:(kt + 1) * P], probs[:, i % 2, e, kt * P:(kt + 1) * P], ident[:])
                        last.then_inc(full[b], 1)

                def pv(i):
                    bk, p = units[i]
                    for e in range(2):
                        b, n = use("probsT", 2 * i + e, l)
                        pe.wait_ge(freed[b], n + 1)
                    b, n = use("pv", i, l)
                    begin(b, n)
                    g = p // 2
                    for e in range(2):
                        tiles = [qkv[:, 0, :]] if bk == 0 else [qkv[:, 1, :], qkv[:, 2, :], None]
                        for kt, v in enumerate(tiles):
                            vv = cache_v[:, g * HD:(g + 1) * HD] if v is None else v[:, 640 + g * HD:640 + (g + 1) * HD]
                            last = pe.matmul(ps[64 * e:64 * e + 64, b, 0:P], vv, probsT[:, e, kt, :],
                                             start=(kt == 0), stop=(kt == len(tiles) - 1))
                    last.then_inc(full[b], 1)

                scores(0)
                for i in range(UNITS):
                    if i + 1 < UNITS:
                        scores(i + 1)
                    filler(2 * i)
                    turn_probs(i)
                    filler(2 * i + 1)
                    pv(i)
                mod_cols(11)

                for i, (s, v) in enumerate(((tapped, l * (CK * KC) + CK * KC), (csq_r, l + 1))):
                    b, n = use("ln", i, l)
                    begin(b, n)
                    pe.wait_ge(s, v)
                    for k in range(KC):
                        last = pe.matmul(ps[:, b, 0:CO], ones[:], (conv if i == 0 else csq)[:, k, :],
                                         start=(k == 0), stop=(k == KC - 1))
                    last.then_inc(full[b], 1)
                    if i == 0:
                        for q in (10, 11):
                            pb, pn = use("pv", q, l)
                            pe.wait_ge(freed[pb], pn + 1)
                        for m in range(4):
                            wide("aproj", m, KC, 4, lambda k: attnT[:, k, :])
                for m in range(4, KD):
                    wide("aproj", m, KC, 4, lambda k: attnT[:, k, :])
                pe.wait_ge(conv_split, l * KC + KC)
                for m in range(KD):
                    wide_split("cproj", m, KC, 4, conv_hi, conv_lo)
                pe.wait_ge(merged_split, l * KD + KD)
                for m in range(KD):
                    wide_split("out", m, KD, 2, merged_hi, merged_lo)

                rms_sum("rms2", l, l * 2 + 1)
                b, n = use("logitsT", 0, l)
                begin(b, n)
                chunk_in(CHUNK_AT["router", 0, 0], l)
                for k in range(KD):
                    h_wait(1, k)
                    last = pe.matmul(ps[0:NE, b, 0:T], ring[CHUNK_AT["router", 0, 0] % SLOTS][:, k * NE:(k + 1) * NE], hT[:, k, :],
                                     start=(k == 0), stop=(k == KD - 1))
                last.then_inc(full[b], 1)

                def h2n(i):
                    b, n = use("h2n", i, l)
                    begin(b, n)
                    t, h = i // 2, i % 2
                    for k in range(4):
                        last = pe.transpose(ps[:, b, k * P:(k + 1) * P], hT[:, 4 * h + k, t * P:(t + 1) * P], ident[:])
                    last.then_inc(full[b], 1)

                h2n(0)
                h2n(1)
                b, n = use("logitsT", 0, l)
                pe.wait_ge(freed[b], n + 1)
                b, n = use("logits", 0, l)
                begin(b, n)
                for t in range(NT):
                    last = pe.matmul(ps[:, b, t * NE:(t + 1) * NE], lgT[:, t * P:(t + 1) * P], ident[0:NE, 0:NE],
                                     start=True, stop=True)
                last.then_inc(full[b], 1)
                for i in range(2, 6):
                    h2n(i)
                pe.wait_ge(route_r, l + 1)
                b, n = use("rank", 0, l)
                begin(b, n)
                for t in range(NT):
                    for i in range(t + 1):
                        pe.matmul(ps[:, b, t * NE:(t + 1) * NE], before_b[:] if i == t else ones_b[:], chosen_b[:, i, :],
                                  start=(i == 0), stop=(i == t))
                for i in range(NT):
                    last = pe.matmul(ps[:, b, NT * NE:(NT + 1) * NE], ones_b[:], chosen_b[:, i, :], start=(i == 0), stop=(i == NT - 1))
                last.then_inc(full[b], 1)

                for i in range(6):
                    b, n = use("h2n", i, l)
                    pe.wait_ge(freed[b], n + 1)
                for half_at in range(2):
                    for k in range(KD):
                        b, n = use("spread", half_at * KD + k, l)
                        begin(b, n)
                        for i in range(2 * NT):
                            t, part = i // 2, (nat_hi, nat_lo)[i % 2]
                            if k == 0 and i % 2 == 0:
                                pe.wait_ge(place_r, l * (2 * NT) + (half_at * NT + t + 1))
                            last = pe.matmul(ps[:, b, 0:HALF], part[:, t, k * P:(k + 1) * P],
                                             place[:, t, half_at * HALF:(half_at + 1) * HALF], start=(i == 0), stop=(i == 2 * NT - 1))
                        last.then_inc(full[b], 1)

                for i in range(2 * KD - 4, 2 * KD):
                    b, n = use("spread", i, l)
                    pe.wait_ge(freed[b], n + 1)
                pe.wait_ge(ends_zero, l + 1)
                pe.wait_ge(pos_r, l + 1)
                settle(pe)
                def expert(e, before_e=None):
                    gate_up, down = expert_parts(
                        lambda b: expert_use(b, l, e), freed, full, landed, l * (16 * SLOT_USES) + (e * 16 + 16 * 9), half,
                        own_r, l * NE + (e + 2), xg_r, l * (NE + 1) + (e + 2))
                    by_width(pe, e, gate_up)
                    if before_e is not None:
                        by_width(pe, before_e, lambda small: back(lambda b: expert_use(b, l, before_e), freed, full, small))
                    by_width(pe, e, down)

                expert(0)
                with pe.Fori(0, NE - 1) as e:
                    expert(e + 1, e)
                by_width(pe, NE - 1, lambda small: back(lambda b: expert_use(b, l, NE - 1), freed, full, small))

                over = pe.value_load(overfull[0:1, 0:1], min_val=0, max_val=1)
                with pe.If(over > 0):
                    for b in range(8):
                        pe.wait_ge(freed[b], expert_use(b, l, NE))
                    pe.wait_ge(xg_r, l * (NE + 1) + (NE + 2))
                    settle(pe)
                    with pe.Fori(0, OSTEPS) as i:
                        gate_up, down = expert_parts(
                            lambda b: further_use(b, l, i), freed_o, full_o, landed_o, l * (16 * OSTEPS) + i * 16 + 16, half_o,
                            own_r_o, l * OSTEPS + i + 2, xg_r_o, l * OSTEPS + i + 1)
                        gate_up(False)
                        down(False)
                        back(lambda b: further_use(b, l, i), freed_o, full_o, False)
                with pe.Else():
                    for b in range(8):
                        pe.sem_inc(full_o[b], OSTEPS * MOE_USES[b])
                    pe.sem_inc(half_o, 2 * OSTEPS)
                pe.nop()

                for i in range(6):
                    b, n = use("y", i, l)
                    begin(b, n)
                    t, h = i // 2, i % 2
                    if i == 0:
                        for q in range(8):
                            if q in (0, 1, 4, 7):
                                pe.wait_ge(freed[q], expert_use(q, l, NE))
                            pe.wait_ge(freed_o[q], further_use(q, l, OSTEPS))
                    for k in range(4):
                        last = pe.transpose(ps[:, b, k * P:(k + 1) * P], nat[:, t, (4 * h + k) * P:(4 * h + k + 1) * P], ident[:])
                    last.then_inc(full[b], 1)

            pe.wait_ge(freed[3], DEPTH * PER[3] + INIT[3])
            pe.wait_ge(sq_sum, 2 * DEPTH + 1)
            pe.matmul(ps[:, 3, 0:T], ones[:], rstd[:], start=True, stop=True).then_inc(full[3], 1)
            pe.wait_ge(h_r, DEPTH * 2 * KD + KD)
            for i in range(6):
                b = i % 3
                pe.wait_ge(freed[b], DEPTH * PER[b] + INIT[b] + i // 3)
                t, h = i // 2, i % 2
                for k in range(4):
                    last = pe.transpose(ps[:, b, k * P:(k + 1) * P], hT[:, 4 * h + k, t * P:(t + 1) * P], ident[:])
                last.then_inc(full[b], 1)

        @block.scalar
        def _(act):
            def load_params(row):
                act.dma_start(prow[:, :], A["features"][row].rearrange("o r p -> (o r) p")).then_inc(par_in, 16)
                act.dma_start(dwrow[:, :], A["taps"][row].rearrange("o r p -> (o r) p")).then_inc(par_in, 16)
                act.dma_start(every[:], A["every"][row, :].broadcast_to([P, 2 * HD + NH])).then_inc(bc_in, 16)

            act.dma_start(crow[0:8, :], A["c_ctx"].rearrange("(k p) -> k p", p=P)).then_inc(c_in, 16)
            act.dma_start(crow[8:16, :], A["c"].rearrange("o (k p) -> (o k) p", p=P)).then_inc(c_in, 16)
            act.dma_start(crow[16:24, :], A["final_norm"].rearrange("(k p) -> k p", p=P)).then_inc(c_in, 16)
            load_params(slice(0, 1))
            act.dma_start(rope[:], A["rope"].rearrange("(t p) c d -> p t c d", p=P)).then_inc(t_in, 16)
            act.dma_start(rbias[:], A["router_bias"].rearrange("(o n) -> o n", o=1).broadcast_to([P, NE])).then_inc(t_in, 16)
            act.wait_ge(full[7], 2)
            act.activation(csig[:], ps[:, 7, 0:16], ACT.Sigmoid).then_inc(csig_r, 1)

            def squares(q, tile_ready=None):
                for k in range(KD):
                    if tile_ready:
                        tile_ready(k)
                    act.activation(squared[:, k, :], xT[:, k, :], ACT.Square).then_inc(xsq, 1)

            def root(bank, n):
                act.wait_ge(full[bank], n + 1)
                act.activation(rms[:], ps[:, bank, 0:T], ACT.Sqrt, scale=1.0 / D, bias=eps[:]).then_inc(freed[bank], 1)

            def affine(q, which):
                for k in range(KD):
                    act.wait_ge(xn_r, q * KD + (k + 1))
                    act.activation(hT[:, k, TC:T], hT[:, k, TC:T], ACT.Identity, scale=coef[:, which, k, 1:2],
                                   bias=mod[:, 24 * which + k, 1:2]).then_inc(h_r, 1)

            act.wait_ge(freed[0], INIT[0])
            act.wait_ge(freed[1], INIT[1])
            act.wait_ge(consts_v, 1)

            def copy_block(at, s):
                act.activation(xgT[:], sortedT[:, :, bass.ds(at, P)], ACT.Copy).then_inc(s, 1)

            def moe_act(fs, fr, n_of, xg_s, hi_s, next_at, small):
                cols = 256 if small else DE
                act.wait_ge(fs[2], n_of(2) + 1)
                act.wait_ge(fr[3], n_of(3))
                act.activation(silu[:, 0:cols], ps[:, 2, 0:cols], ACT.Silu).then_inc(fr[2], 1)
                act.wait_ge(fs[3], n_of(3) + 1)
                copy_block(next_at, xg_s)
                act.wait_ge(fs[4], n_of(4) + 1)
                act.wait_ge(fs[6], n_of(6))
                act.activation(hidT[:, 0:cols // P, :], ps[:, 4, 0:cols].rearrange("p (k n) -> p k n", n=P), ACT.Copy
                               ).then_inc(fr[4], 1)
                for h in range(2):
                    act.wait_ge(fs[h], n_of(h))
                act.wait_ge(fs[7], n_of(7) + 1)
                act.activation(ownT[:], ps[:, 7, 0:T], ACT.Copy).then_inc(fr[7], 1)
                for h in range(2):
                    act.wait_ge(fs[5 + h], n_of(5 + h) + 1)
                    a, z, o = (64 * h, 64 * h + 64, 0) if small else (0, P, 512 * h)
                    act.activation(orow_hi[a:z, o:o + 512], ps[a:z, 5 + h, :], ACT.Copy).then_inc(hi_s, 1)

            with act.Fori(0, DEPTH) as l:
                act.dma_start(cache_v[:], A["cache_v"][0, bass.ds(l, 1)].rearrange("o t h d -> (o t) (h d)")).then_inc(cache_in, 16)
                act.dma_start(cache_k[:], A["cache_k"][0, bass.ds(l, 1)].rearrange("o t h d -> (o t) (h d)")).then_inc(cache_in, 16)

                squares(l * 2)
                for g in range(4):
                    b, n = use("ada", g, l)
                    act.wait_ge(full[b], n + 1)
                    if g >= 2:
                        act.wait_ge(modrow_used, l * 10 + (g - 1))
                    act.activation(modrow[:, g % 2, :], ps[:, b, :], ACT.Copy).then_inc(freed[b], 1)
                    if g == 1:
                        root(*use("rms1", 0, l))
                act.wait_ge(mod_r, l * 2 + 1)
                affine(l * 2, 0)
                for k in range(KD):
                    act.wait_ge(h_ctx, l * (2 * KD) + (k + 1))
                    act.wait_ge(h_r, l * (2 * KD) + (k + 1))
                    act.activation(h_hi[:, k, :], hT[:, k, :], ACT.Copy).then_inc(h_hi_r, 1)

                for i in range(9):
                    b, n = use("qkv", i, l)
                    act.wait_ge(full[b], n + 1)
                    c, t = i // 3, i % 3
                    act.activation(qkv[:, t, c * 256:(c + 1) * 256], ps[:, b, 0:256], ACT.Copy).then_inc(freed[b], 1)
                    if i % 2 == 1:
                        at = CHUNK_AT["u", i // 2, 0]
                        act.wait_ge(landed[at % SLOTS], l * (16 * SLOT_USES) + 16 * (at // SLOTS + 1))
                        act.activation(u_hi[i // 2][:], ring[at % SLOTS][:], ACT.Copy).then_inc(u_hi_r, 1)
                act.wait_ge(freed[6], use("qkv", 8, l)[1] + 1)
                act.wait_ge(freed[5], use("qkv", 7, l)[1] + 1)
                act.wait_ge(freed[4], use("qkv", 6, l)[1] + 1)
                act.activation(qtmp[:, :, :], qkv[:, :, 0:640], ACT.Square).then_inc(qsq_r, 1)
                act.wait_ge(qss_r, l + 1)
                act.activation(ss[:], ss[:], ACT.Sqrt, scale=1.0 / HD, bias=eps[:]).then_inc(qrms_r, 1)

                for i in range(KC, 2 * KC):
                    b, n = use("u", i, l)
                    act.wait_ge(full[b], n + 1)
                    j = i - KC
                    if j >= 2:
                        act.wait_ge(usig_used, l * KC + (j - 1))
                    act.activation(sig[:, j % 2, :], ps[:, b, 0:T], ACT.Sigmoid).then_inc(freed[b], 1)
                for t in range(NT):
                    b, n = use("qT", t, l)
                    act.wait_ge(full[b], n + 1)
                    act.activation(qT[:, :, t * P:(t + 1) * P], ps[:, b, :].rearrange("p (k n) -> p k n", k=4),
                                   ACT.Copy).then_inc(freed[b], 1)
                for i in range(2):
                    b, n = use("kT", i, l)
                    act.wait_ge(full[b], n + 1)
                    for j in range(2):
                        last = act.activation(kT[:, :, (2 * i + j) * P:(2 * i + j + 1) * P],
                                              ps[:, b, 2 * j * P:2 * (j + 1) * P].rearrange("p (g n) -> p g n", g=2), ACT.Copy)
                    last.then_inc(freed[b], 1)

                def exponentials(i):
                    nk = P if i < 4 else 3 * P
                    act.wait_ge(sm_max, l * UNITS + (i + 1))
                    for e in range(2):
                        act.activation(probs[:, i % 2, e, 0:nk], probs[:, i % 2, e, 0:nk], ACT.Exp,
                                       bias=st[:, i % 2, e:e + 1], accum_out=st[:, i % 2, 4 + e:5 + e])
                    act.activation(st[:, i % 2, 2:4], st[:, i % 2, 2:4], ACT.Exp).then_inc(sm_exp, 1)

                def filler_out(j):
                    kind, q = FILLERS[j]
                    b, n = use(kind, q, l)
                    act.wait_ge(full[b], n + 1)
                    if kind == "gate":
                        act.activation(gates[:, q, :], ps[:, b, 0:T], ACT.Sigmoid).then_inc(freed[b], 1)
                        return
                    if q < 2:
                        act.wait_ge(full[2], use("mod", 0, l)[1] + 1)
                    else:
                        act.wait_ge(modrow_used, l * 10 + (3 + q - 1))
                    act.activation(modrow[:, q % 2, :], ps[:, b, :], ACT.Copy).then_inc(freed[b], 1)

                exponentials(0)
                for i in range(UNITS):
                    filler_out(2 * i)
                    nkt = 1 if i < 4 else 3
                    for e in range(2):
                        b, n = use("probsT", 2 * i + e, l)
                        act.wait_ge(full[b], n + 1)
                        if i >= 1:
                            vb, vn = use("pv", i - 1, l)
                            act.wait_ge(full[vb], vn + 1)
                        act.activation(probsT[:, e, 0:nkt, :], ps[:, b, 0:nkt * P].rearrange("p (k n) -> p k n", k=nkt),
                                       ACT.Copy).then_inc(freed[b], 1)
                    if i + 1 < UNITS:
                        exponentials(i + 1)
                    filler_out(2 * i + 1)
                    bk, p = i // 4, i % 4
                    b, n = use("pv", i, l)
                    act.wait_ge(full[b], n + 1)
                    act.activation(attnT[:, p, bk * P:(bk + 1) * P], ps[:, b, 0:P], ACT.Copy).then_inc(freed[b], 1)

                act.wait_ge(conv_c, l + 1)
                act.activation(csq[:], conv[:], ACT.Square).then_inc(csq_r, 1)

                def upper_weights(q):
                    c = CHUNK_AT[(*SPLIT[q], 0)]
                    act.wait_ge(landed[c % SLOTS], l * (16 * SLOT_USES) + 16 * (c // SLOTS + 1))
                    if q >= 3:
                        stage, i = chunk_end(CHUNK_AT[(*SPLIT[q - 3], 0)])
                        b, n = use(stage, i, l)
                        act.wait_ge(full[b], n + 1)
                    act.activation(w_hi[:, q % 3, :], ring[c % SLOTS][:], ACT.Copy).then_inc(w_hi_r, 1)

                act.wait_ge(kv_out, l * 32 + 32)
                for q in range(3):
                    upper_weights(q)
                b, n = use("ln", 1, l)
                act.wait_ge(full[b], n + 1)
                act.activation(mu[:], ps[:, b, 0:CO], ACT.Sqrt, scale=1.0 / CW, bias=eps[:]).then_inc(freed[b], 1)
                for k in range(KC):
                    act.wait_ge(cn_r, l * KC + (k + 1))
                    act.activation(csq[:, k, 0:TC], conv[:, k, 0:TC], ACT.Silu, scale=par[:, 68 + k:69 + k], bias=par[:, 72 + k:73 + k])
                    act.activation(csq[:, k, TC:T], conv[:, k, LAT0:LAT0 + TL], ACT.Silu, scale=par[:, 68 + k:69 + k],
                                   bias=par[:, 72 + k:73 + k]).then_inc(convT_r, 1)
                    act.wait_ge(convT_r, l * KC + (k + 1))
                    act.activation(conv_hi[:, k, :], conv_tokens(k), ACT.Copy).then_inc(conv_hi_r, 1)
                for m in range(KD):
                    b, n = use("cproj", m, l)
                    act.wait_ge(freed[b], n + 1)
                    act.activation(merged_hi[:, m, :], hT[:, m, :], ACT.Copy).then_inc(merged_hi_r, 1)
                    if m == 4:
                        upper_weights(3)
                upper_weights(4)
                upper_weights(5)

                def mixer_out(k):
                    b, n = use("out", k, l)
                    act.wait_ge(freed[b], n + 1)
                squares(l * 2 + 1, mixer_out)
                b, n = use("rms2", 0, l)
                root(b, n)
                act.wait_ge(mod_r, l * 2 + 2)
                affine(l * 2 + 1, 1)
                for i in range(6):
                    b, n = use("h2n", i, l)
                    act.wait_ge(full[b], n + 1)
                    t, h = i // 2, i % 2
                    act.activation(nat_hi[:, t, h * 512:(h + 1) * 512], ps[:, b, :], ACT.Copy).then_inc(nat_hi_r, 1)
                    if i == 1:
                        b, n = use("logits", 0, l)
                        act.wait_ge(full[b], n + 1)
                        act.activation(sc[:], ps[:, b, 0:NT * NE].rearrange("p (t n) -> p t n", t=NT), ACT.Sigmoid).then_inc(freed[b], 1)

                b, n = use("params", 0, l)
                act.wait_ge(full[b], n + 1)
                load_params(bass.ds(l + 1, 1))

                for i in range(2 * KD):
                    b, n = use("spread", i, l)
                    act.wait_ge(full[b], n + 1)
                    half_at, k = i // KD, i % KD
                    act.activation(sortedT[:, k, half_at * HALF:(half_at + 1) * HALF], ps[:, b, 0:HALF], ACT.Copy
                                   ).then_inc(freed[b], 1)
                    if i == KD - 1:
                        for j in range(KD - 4, KD):
                            b, n = use("spread", j, l)
                            act.wait_ge(freed[b], n + 1)
                        copy_block(0, xg_r)

                act.wait_ge(pos_r, l + 1)
                for i in range(2 * KD - 4, 2 * KD):
                    b, n = use("spread", i, l)
                    act.wait_ge(freed[b], n + 1)
                act.wait_ge(ends_zero, l + 1)
                settle(act)
                with act.Fori(0, NE) as e:
                    next_at = act.value_load(place_at[0:1, bass.ds(e + 1, 1)], min_val=0, max_val=ROWS)
                    by_width(act, e, lambda small: moe_act(full, freed, lambda b: expert_use(b, l, e), xg_r, orow_hi_r, next_at, small))
                over = act.value_load(overfull[0:1, 0:1], min_val=0, max_val=1)
                with act.If(over > 0):
                    with act.Fori(0, OSTEPS) as i:
                        moe_act(full_o, freed_o, lambda b: further_use(b, l, i), xg_r_o, orow_hi_r_o,
                                act.value_load(place_at[0:1, bass.ds(i + (NE + 1), 1)], min_val=0, max_val=ROWS), False)
                with act.Else():
                    for b in (2, 4, 7):
                        act.sem_inc(freed_o[b], OSTEPS)
                    act.sem_inc(orow_hi_r_o, 2 * OSTEPS)
                    act.sem_inc(xg_r_o, OSTEPS)
                act.nop()
                for q in range(3):
                    b, n = use("y", 3 + q, l)
                    act.wait_ge(freed[b], n + 1)

            squares(2 * DEPTH)
            root(3, DEPTH * PER[3] + INIT[3])
            for k in range(KD):
                act.wait_ge(xn_r, 2 * DEPTH * KD + k + 1)
                act.activation(hT[:, k, :], hT[:, k, :], ACT.Copy, scale=fnorm[:, k:k + 1]).then_inc(h_r, 1)
            for i in range(6):
                b = i % 3
                act.wait_ge(full[b], DEPTH * PER[b] + INIT[b] + i // 3 + 1)
                t, h = i // 2, i % 2
                act.activation(nat[:, t, h * 512:(h + 1) * 512], ps[:, b, :], ACT.Copy).then_inc(freed[b], 1)
                if h == 1:
                    for j in (i - 1, i):
                        act.wait_ge(freed[j % 3], DEPTH * PER[j % 3] + INIT[j % 3] + j // 3 + 1)
                    dst = A["y_prompt"][0] if t == 0 else A["y_sample"][0, (t - 1) * P:t * P, :]
                    act.dma_start(dst, nat[:, t, :]).then_inc(y_out, 16)
            act.wait_ge(y_out, 48)
            act.wait_ge(par_in, 32 * (DEPTH + 1))
            act.wait_ge(bc_in, 16 * (DEPTH + 1))

        @block.gpsimd
        def _(pool):
            pool.memset(ident[:], 0.0).then_inc(chain_p, 1)
            pool.memset(ones[:], 1.0).then_inc(consts, 1)
            pool.memset(before[:], 1.0).then_inc(chain_p, 1)
            pool.memset(sel[:], 0.0).then_inc(chain_p, 1)
            pool.memset(mask[:], 0.0).then_inc(chain_p, 1)
            pool.wait_ge(chain_p, 4)
            pool.affine_select(out=ident[:], in_=ident[:], compare_op=ALU.not_equal, fill=1.0, base=0,
                               pattern=[[-1, P]], channel_multiplier=1).then_inc(consts, 1)
            pool.affine_select(out=before[:], in_=before[:], compare_op=ALU.is_gt, fill=0.0, base=0,
                               pattern=[[1, P]], channel_multiplier=-1).then_inc(consts, 1)
            pool.affine_select(out=mask[:, 0, 0:TL], in_=mask[:, 0, 0:TL], compare_op=ALU.is_ge, fill=NEG, base=P,
                               pattern=[[-1, TL]], channel_multiplier=1).then_inc(consts2, 1)
            pool.affine_select(out=mask[:, 1, 0:TL], in_=mask[:, 1, 0:TL], compare_op=ALU.is_ge, fill=NEG, base=0,
                               pattern=[[1, TL]], channel_multiplier=-1).then_inc(consts2, 1)
            for j in range(4):
                pool.affine_select(out=sel[:], in_=sel[:], compare_op=ALU.not_equal, fill=1.0, base=-32 * j,
                                   pattern=[[-1, 2]], channel_multiplier=1).then_inc(chain_p, 1)
                pool.wait_ge(chain_p, 5 + j)
            pool.iota(down_i[:], pattern=[[0, NT], [-1, NE]], base=NE, channel_multiplier=0,
                      allow_small_or_imprecise_dtypes=True).then_inc(consts2, 1)
            pool.iota(down_g[:], pattern=[[0, NT], [-1, NG]], base=NG, channel_multiplier=0,
                      allow_small_or_imprecise_dtypes=True).then_inc(consts2, 1)
            pool.memset(zero16[:], 0.0).then_inc(consts2, 1)

            with pool.Fori(0, DEPTH) as l:
                pool.wait_ge(k_pre, l + 1)
                pool.dma_start(A["new_k"][0, bass.ds(l, 1)].rearrange("o t h d -> (o t) (h d)"), qkv[:, 0, 512:640]).then_inc(kv_out, 16)
                pool.dma_start(A["new_v"][0, bass.ds(l, 1)].rearrange("o t h d -> (o t) (h d)"), qkv[:, 0, 640:768]).then_inc(kv_out, 16)

                pool.wait_ge(h_r, l * (2 * KD) + 2 * KD)
                settle(pool)
                pool.iota(count768, pattern=[[1, ROWS]], base=0, channel_multiplier=0,
                          allow_small_or_imprecise_dtypes=True).then_inc(counts_r, 1)
                pool.iota(count64.rearrange("p (u n) -> p u n", u=2), pattern=[[0, 2], [1, P // 2]], base=0, channel_multiplier=0,
                          allow_small_or_imprecise_dtypes=True).then_inc(counts_r, 1)
                pool.memset(sortedT[:, :, ROWS:PLACES], 0.0).then_inc(ends_zero, 1)
            pool.wait_ge(kv_out, 32 * DEPTH)

        @block.vector
        def _(dve):
            steps = [0]
            layer = [None]

            def link(ins):
                steps[0] += 1
                ins.then_inc(chain, 1)
                dve.wait_ge(chain, (layer[0] * CHAIN + steps[0]) if layer[0] is not None else steps[0])

            BASE = 4
            link(dve.memset(condT[:], 0.0))
            link(dve.memset(ub[:], 0.0))
            link(dve.memset(posf[:], 0.0))
            link(dve.memset(placef[:], float(ROWS)))
            dve.memset(eps[:], EPS).then_inc(consts_v, 1)
            for i in range(6):
                b, n = init_use("x", i)
                t, h = i // 2, i % 2
                dve.wait_ge(full[b], n + 1)
                dve.tensor_copy(xT[:, 4 * h:4 * h + 4, t * P:(t + 1) * P],
                                ps[:, b, :].rearrange("p (k n) -> p k n", k=4)).then_inc(freed[b], 1)
            dve.wait_ge(csig_r, 1)
            for c in range(2):
                dve.tensor_tensor(condT[:, :, c], ps[:, 7, 8 * c:8 * c + 8], csig[:, 8 * c:8 * c + 8], ALU.mult)
            dve.tensor_copy(fnorm[:], ps[:, 7, 16:24]).then_inc(freed[7], 1)
            dve.wait_ge(consts, 3)
            dve.tensor_copy(ones_b[:], ones[:])
            dve.tensor_copy(before_b[:], before[:])
            dve.wait_ge(consts2, 5)
            dve.wait_ge(t_in, 32)
            assert steps[0] == BASE
            steps[0] = 0

            def ready(ins, s, value):
                ins.then_inc(s, 1)
                dve.wait_ge(s, value)

            def add_square(q, k):
                dve.wait_ge(xsq, q * KD + (k + 1))
                if k > 1:
                    dve.wait_ge(sq_added, q * (KD - 2) + (k - 1))
                dve.tensor_tensor(rstd[:], squared[:, 0, :] if k == 1 else rstd[:], squared[:, k, :], ALU.add
                                  ).then_inc(sq_sum if k == KD - 1 else sq_added, 1)

            def add_squares(q):
                for k in range(1, KD):
                    add_square(q, k)

            def context_affine(which, k):
                dve.tensor_scalar(hT[:, k, 0:TC], hT[:, k, 0:TC], coef[:, which, k, 0:1],
                                  mod[:, 24 * which + k, 0:1], ALU.mult, ALU.add).then_inc(h_ctx, 1)

            def norm_tiles(q, which=None):
                for k in range(KD):
                    dve.tensor_tensor(hT[:, k, :], xT[:, k, :], rstd[:], ALU.mult).then_inc(xn_r, 1)
                    if which is not None:
                        dve.wait_ge(xn_r, q * KD + (k + 1))
                        context_affine(which, k)

            def own_and_hid(fs, fr, n_of, own_s, at, own_read, hid_read, small):
                dve.wait_ge(fs[7], own_read)
                for t in range(NT):
                    last = dve.tensor_scalar(own[:, t, :], count64 if small else count768[:, 0:P],
                                             rank_at[:, t, bass.ds(at, 1)], None, ALU.is_equal)
                last.then_inc(own_s, 1)
                cols = 256 if small else DE
                dve.wait_ge(fr[2], n_of(2) + 1)
                dve.wait_ge(fs[3], n_of(3) + 1)
                dve.wait_ge(fs[4], hid_read)
                dve.tensor_tensor(hid[:, 0:cols], silu[:, 0:cols], ps[:, 3, 0:cols], ALU.mult).then_inc(fr[3], 1)

            def rows_lo(fr, hi_s, hi_at, small):
                for h in range(2):
                    dve.wait_ge(hi_s, hi_at + (h + 1))
                    a, z, o = (64 * h, 64 * h + 64, 0) if small else (0, P, 512 * h)
                    dve.tensor_tensor(orow_lo[a:z, o:o + 512], ps[a:z, 5 + h, :], orow_hi[a:z, o:o + 512].bitcast(F32),
                                      ALU.subtract).then_inc(fr[5 + h], 1)

            def add_rows(fs, fr, n_of, at):
                for b, u in SUM_BANKS[:4]:
                    dve.wait_ge(fr[b], n_of(b) + u)
                for t in range(NT):
                    for h in range(2):
                        b, u = SUM_BANKS[2 * t + h]
                        dve.wait_ge(fs[b], n_of(b) + (u + 1))
                        sums = nat[:, t, 512 * h:512 * h + 512]
                        dve.scalar_tensor_tensor(sums, ps[:, b, :], weight[:, t, bass.ds(at, 1)], sums,
                                                 ALU.mult, ALU.add).then_inc(fr[b], 1)

            with dve.Fori(0, DEPTH) as l:
                def link(ins):
                    steps[0] += 1
                    ins.then_inc(chain, 1)
                    dve.wait_ge(chain, l * CHAIN + (BASE + steps[0]))

                b, n = use("params", 0, l)
                dve.wait_ge(full[b], n + 1)
                dve.tensor_copy(par[:], ps[:, b, 0:76])
                ready(dve.tensor_copy(dw[:], ps[:, b, 128:128 + CK * KC]), freed[b], n + 1)
                dve.wait_ge(bc_in, l * 16 + 16)
                dve.tensor_scalar(nsink[:], sinkb, -1.0, None, ALU.mult)

                def modulation(stage, m0, m1):
                    b, n = use(stage, 0, l)
                    dve.wait_ge(full[b], n + 1)
                    ready(dve.tensor_tensor(mod[:, m0:m1, :], ps[:, b, 2 * m0:2 * m1].rearrange("p (m c) -> p m c", c=2),
                                            par[:, m0:m1].unsqueeze(2).to_broadcast([P, m1 - m0, 2]), ALU.add), freed[b], n + 1)
                    w = m0 // 16
                    for c in range(2):
                        last = dve.scalar_tensor_tensor(coef[:, w, :, c], mod[:, 24 * w + 8:24 * w + 16, c] if w == 0 else
                                                        mod[:, 32:40, c], 1.0, par[:, 48 + 8 * w:56 + 8 * w], ALU.add, ALU.mult)
                    ready(last, mod_r, l * 2 + (1 if stage == "mod" else 2))


                add_squares(l * 2)
                b, n = use("rms1", 0, l)
                dve.wait_ge(freed[b], n + 1)
                link(dve.reciprocal(rstd[:], rms[:]))
                norm_tiles(l * 2)
                modulation("mod", 0, 16)
                dve.wait_ge(xn_r, l * (2 * KD) + KD)
                for k in range(KD):
                    context_affine(0, k)


                for k in range(KD):
                    dve.wait_ge(h_hi_r, l * KD + (k + 1))
                    dve.tensor_tensor(h_lo[:, k, :], hT[:, k, :], h_hi[:, k, :].bitcast(F32), ALU.subtract).then_inc(h_split, 1)
                for c in range(KC):
                    s = CHUNK_AT["u", c, 0] % SLOTS
                    dve.wait_ge(u_hi_r, l * KC + (c + 1))
                    dve.tensor_tensor(w_lo[s][:], ring[s][:], u_hi[c][:].bitcast(F32), ALU.subtract).then_inc(u_split, 1)

                dve.wait_ge(qsq_r, l + 1)
                dve.tensor_reduce(ss[:], qtmp[:].rearrange("p t (h d) -> p (t h) d", d=HD), AX.X, ALU.add).then_inc(qss_r, 1)
                dve.wait_ge(qrms_r, l + 1)
                link(dve.reciprocal(ss[:], ss[:]))
                for t in range(NT):
                    qk = qkv[:, t, 0:640].rearrange("p (h d) -> p h d", d=HD)
                    tmp = qtmp[:, t, :].rearrange("p (h d) -> p h d", d=HD)
                    link(dve.tensor_tensor(tmp, qk, ss[:, 10 * t:10 * t + 10].unsqueeze(2).to_broadcast([P, 10, HD]), ALU.mult))
                    dve.tensor_tensor(qk[:, 0:NH, :], tmp[:, 0:NH, :], qkn[:, 0:1, :].to_broadcast([P, NH, HD]), ALU.mult)
                    i2 = dve.tensor_tensor(qk[:, NH:10, :], tmp[:, NH:10, :], qkn[:, 1:2, :].to_broadcast([P, 2, HD]), ALU.mult)
                    if t == 0:
                        ready(i2, k_pre, l + 1)
                    else:
                        link(i2)
                for t in range(1, NT):
                    qk = qkv[:, t, 0:640].rearrange("p (h d) -> p h d", d=HD)
                    tmp = qtmp[:, t, :].rearrange("p (h d) -> p h d", d=HD)
                    dve.tensor_tensor(tmp, qk, rope[:, t - 1, 0:1, :].to_broadcast([P, 10, HD]), ALU.mult)
                    t2 = qtmp2[:, t - 1, :].rearrange("p (h a s i) -> p h a s i", h=10, a=2, s=2)
                    qs = qkv[:, t, 0:640].rearrange("p (h a s i) -> p h a s i", h=10, a=2, s=2)
                    sn = rope[:, t - 1, 1:2, :].rearrange("p o (a s i) -> p o a s i", a=2, s=2)
                    for s_ in range(2):
                        for a_ in range(2):
                            last = dve.tensor_tensor(t2[:, :, a_, s_, :], qs[:, :, a_, 1 - s_, :],
                                                     sn[:, :, a_, s_, :].to_broadcast([P, 10, 16]), ALU.mult)
                    link(last)
                    link(dve.tensor_tensor(qk, tmp, qtmp2[:, t - 1, :].rearrange("p (h d) -> p h d", d=HD), ALU.add))
                dve.wait_ge(cache_in, l * 32 + 32)
                for t in range(4):
                    src = cache_k[:].rearrange("p (g d) -> p g d", g=2) if t == 3 else \
                        qkv[:, t, 512:640].rearrange("p (g d) -> p g d", g=2)
                    last = dve.tensor_copy(kdup[:, t, :, :].rearrange("p g (u d) -> p g u d", u=2),
                                           src.unsqueeze(2).to_broadcast([P, 2, 2, HD]))
                last.then_inc(q_r, 1)

                for i in range(KC):
                    b, n = use("u", i, l)
                    dve.wait_ge(full[b], n + 1)
                    dve.tensor_copy(ub[:, i, PAD:PAD + TC], ps[:, b, 0:TC])
                    ready(dve.tensor_copy(ub[:, i, SEG + PAD:SEG + PAD + TL], ps[:, b, TC:T]), freed[b], n + 1)
                for i in range(KC):
                    b, n = use("u", KC + i, l)
                    dve.wait_ge(freed[b], n + 1)
                    dve.tensor_tensor(ub[:, i, PAD:PAD + TC], ub[:, i, PAD:PAD + TC], sig[:, i % 2, 0:TC], ALU.mult)
                    u0 = SEG + PAD
                    ready(dve.tensor_tensor(ub[:, i, u0:u0 + TL], ub[:, i, u0:u0 + TL], sig[:, i % 2, TC:T], ALU.mult),
                          usig_used, l * KC + (i + 1))
                def tap(n):
                    j, i = n // KC, n % KC
                    src = ub[:, i, j:j + CO]
                    w = dw[:, n:n + 1]
                    if j == 0:
                        dve.tensor_scalar(conv[:, i, :], src, w, par[:, 64 + i:65 + i], ALU.mult, ALU.add).then_inc(tapped, 1)
                    else:
                        dve.wait_ge(tapped, l * (CK * KC) + (n - KC + 1))
                        dve.scalar_tensor_tensor(conv[:, i, :], src, w, conv[:, i, :], ALU.mult, ALU.add).then_inc(tapped, 1)

                def soft_a(i):
                    bk, p = i // 4, i % 4
                    nk = P if bk == 0 else 3 * P
                    bs = [use("scores", 2 * i + e, l) for e in range(2)]
                    for b, n in bs:
                        dve.wait_ge(full[b], n + 1)
                    if i >= 2:
                        for e in range(2):
                            tb, tn = use("probsT", 2 * (i - 2) + e, l)
                            dve.wait_ge(full[tb], tn + 1)
                    b0 = bs[0][0]
                    pr_ = probs[:, i % 2, :, 0:nk]
                    if bk == 0:
                        ins = dve.tensor_scalar(pr_, ps[:, b0:b0 + 2, 0:nk], HD ** -0.5, None, ALU.mult)
                    else:
                        ins = dve.scalar_tensor_tensor(pr_, ps[:, b0:b0 + 2, 0:nk], HD ** -0.5,
                                                       mask[:, bk - 1:bk, :].to_broadcast([P, 2, nk]), ALU.mult, ALU.add)
                    ready(ins, freed[b0], bs[0][1] + 1)
                    dve.sem_inc(freed[b0 + 1], 1)
                    s_ = st[:, i % 2, :]
                    link(dve.tensor_reduce(s_[:, 6:8], pr_, AX.X, ALU.max))
                    link(dve.scalar_tensor_tensor(s_[:, 0:2], s_[:, 6:8], -1.0, nsink[:, 2 * p:2 * p + 2], ALU.mult, ALU.min))
                    dve.tensor_tensor(s_[:, 2:4], s_[:, 0:2], sinkb[:, 2 * p:2 * p + 2], ALU.add).then_inc(sm_max, 1)

                def soft_b(i):
                    nk = P if i < 4 else 3 * P
                    s_ = st[:, i % 2, :]
                    dve.wait_ge(sm_exp, l * UNITS + (i + 1))
                    link(dve.tensor_tensor(s_[:, 6:8], s_[:, 2:4], s_[:, 4:6], ALU.add))
                    link(dve.reciprocal(s_[:, 6:8], s_[:, 6:8]))
                    for e in range(2):
                        last = dve.tensor_scalar(probs[:, i % 2, e, 0:nk], probs[:, i % 2, e, 0:nk], s_[:, 6 + e:7 + e], None, ALU.mult)
                    last.then_inc(p_r, 1)

                soft_a(0)
                taps = 0
                for i in range(UNITS):
                    soft_b(i)
                    if i + 1 < UNITS:
                        soft_a(i + 1)
                    until = CK * KC * (i + 1) // UNITS
                    for n_tap in range(taps, until):
                        tap(n_tap)
                    taps = until

                modulation("mod2", 16, 48)

                b, n = use("ln", 0, l)
                dve.wait_ge(full[b], n + 1)
                ready(dve.tensor_scalar(mu[:], ps[:, b, 0:CO], 1.0 / CW, None, ALU.mult), freed[b], n + 1)
                dve.tensor_tensor(conv[:], conv[:], mu[:].unsqueeze(1).to_broadcast([P, KC, CO]), ALU.subtract).then_inc(conv_c, 1)
                def aproj(m):
                    b, n = use("aproj", m, l)
                    dve.wait_ge(full[b], n + 1)
                    dve.tensor_tensor(hT[:, m, :], ps[:, b, 0:T], gates[:, m, :], ALU.mult).then_inc(freed[b], 1)
                def lower_weights(q):
                    s = CHUNK_AT[(*SPLIT[q], 0)] % SLOTS
                    dve.wait_ge(w_hi_r, l * len(SPLIT) + (q + 1))
                    dve.tensor_tensor(w_lo[s][:], ring[s][:], w_hi[:, q % 3, :].bitcast(F32), ALU.subtract).then_inc(w_split, 1)

                for m in range(4):
                    aproj(m)
                    if m >= 1:
                        lower_weights(m - 1)
                b, n = use("ln", 1, l)
                dve.wait_ge(freed[b], n + 1)
                link(dve.reciprocal(mu[:], mu[:]))
                for k in range(KC):
                    dve.tensor_tensor(conv[:, k, :], conv[:, k, :], mu[:], ALU.mult).then_inc(cn_r, 1)

                def lower_merged(m):
                    dve.wait_ge(merged_hi_r, l * KD + (m + 1))
                    dve.tensor_tensor(merged_lo[:, m, :], hT[:, m, :], merged_hi[:, m, :].bitcast(F32), ALU.subtract
                                      ).then_inc(merged_split, 1)

                for k in range(KC):
                    dve.wait_ge(conv_hi_r, l * KC + (k + 1))
                    dve.tensor_tensor(conv_lo[:, k, 0:T], conv_tokens(k), conv_hi[:, k, :].bitcast(F32), ALU.subtract
                                      ).then_inc(conv_split, 1)
                for m in range(4, KD):
                    aproj(m)
                for m in range(KD):
                    b, n = use("cproj", m, l)
                    dve.wait_ge(full[b], n + 1)
                    if m == 0:
                        for q in range(4, KD):
                            ab, an = use("aproj", q, l)
                            dve.wait_ge(freed[ab], an + 1)
                    link(dve.tensor_tensor(mixtmp[:, m % 2, :], ps[:, b, 0:T], gates[:, KD + m, :], ALU.mult))
                    dve.tensor_tensor(hT[:, m, :], hT[:, m, :], mixtmp[:, m % 2, :], ALU.add).then_inc(freed[b], 1)
                    if m >= 1:
                        lower_merged(m - 1)
                lower_merged(KD - 1)
                lower_weights(3)
                for m in range(KD):
                    b, n = use("out", m, l)
                    dve.wait_ge(full[b], n + 1)
                    dve.scalar_tensor_tensor(xT[:, m, 0:TC], ps[:, b, 0:TC], mod[:, 16 + m, 0:1], xT[:, m, 0:TC], ALU.mult, ALU.add)
                    dve.scalar_tensor_tensor(xT[:, m, TC:T], ps[:, b, TC:T], mod[:, 16 + m, 1:2], xT[:, m, TC:T],
                                             ALU.mult, ALU.add).then_inc(freed[b], 1)
                    if m in (1, 3):
                        lower_weights(4 if m == 1 else 5)
                    if m >= 2:
                        add_square(l * 2 + 1, m - 1)
                add_square(l * 2 + 1, KD - 1)
                b, n = use("rms2", 0, l)
                dve.wait_ge(freed[b], n + 1)
                link(dve.reciprocal(rstd[:], rms[:]))
                norm_tiles(l * 2 + 1, 1)

                b, n = use("logitsT", 0, l)
                dve.wait_ge(full[b], n + 1)
                dve.tensor_copy(lgT[:], ps[0:NE, b, 0:T]).then_inc(freed[b], 1)
                b, n = use("logits", 0, l)
                dve.wait_ge(freed[b], n + 1)
                link(dve.tensor_tensor(se[:], sc[:], rbias[:].unsqueeze(1).to_broadcast([P, NT, NE]), ALU.add))
                s4 = se[:].rearrange("p t (g e) -> p (t g) e", e=EG)
                q = 0
                for a_ in range(EG):
                    for b_ in range(a_ + 1, EG):
                        last = dve.tensor_tensor(pair[:, :, q], s4[:, :, a_], s4[:, :, b_], ALU.add)
                        q += 1
                link(last)
                gsf = gs[:].rearrange("p t g -> p (t g)")
                link(dve.tensor_reduce(gsf, pair[:], AX.X, ALU.max))

                def first_max(out, x, tmp, downs, width):
                    link(dve.tensor_reduce(r1[:], x, AX.X, ALU.max))
                    link(dve.tensor_tensor(tmp, x, r1[:].unsqueeze(2).to_broadcast([P, NT, width]), ALU.is_equal))
                    link(dve.tensor_tensor(tmp, tmp, downs, ALU.mult))
                    link(dve.tensor_reduce(r1[:], tmp, AX.X, ALU.max))
                    link(dve.tensor_tensor(out, tmp, r1[:].unsqueeze(2).to_broadcast([P, NT, width]), ALU.is_equal))

                first_max(gt[:], gs[:], gs[:], down_g[:], NG)
                g4 = gt[:].rearrange("p t g -> p (t g)").unsqueeze(2).to_broadcast([P, NT * NG, EG])
                ra4 = ra[:].rearrange("p t (g e) -> p (t g) e", e=EG)
                rb4 = rb[:].rearrange("p t (g e) -> p (t g) e", e=EG)
                link(dve.tensor_tensor(rb4, s4, g4, ALU.mult))
                link(dve.tensor_scalar(ra4, g4, -NEG, NEG, ALU.mult, ALU.add))
                link(dve.tensor_tensor(ra[:], ra[:], rb[:], ALU.add))
                first_max(m1[:], ra[:], rb[:], down_i[:], NE)
                link(dve.scalar_tensor_tensor(ra[:], m1[:], 4 * NEG, ra[:], ALU.mult, ALU.add))
                first_max(m2[:], ra[:], rb[:], down_i[:], NE)
                dve.tensor_tensor(chosen_b[:], m1[:], m2[:], ALU.add).then_inc(route_r, 1)
                dve.tensor_tensor(ra[:], m1[:], m2[:], ALU.add)
                for i in range(6):
                    b, n = use("h2n", i, l)
                    dve.wait_ge(nat_hi_r, l * 6 + (i + 1))
                    t, h = i // 2, i % 2
                    dve.tensor_tensor(nat_lo[:, t, h * 512:(h + 1) * 512], ps[:, b, :],
                                      nat_hi[:, t, h * 512:(h + 1) * 512].bitcast(F32), ALU.subtract).then_inc(freed[b], 1)
                b, n = use("rank", 0, l)
                dve.wait_ge(full[b], n + 1)
                link(dve.tensor_copy(cnt[:], ps[:, b, NT * NE:(NT + 1) * NE]))
                link(dve.tensor_tensor_scan(off[:], cnt[:], zero16[:], 0.0, ALU.add, ALU.add))
                link(dve.tensor_tensor(off[:], off[:], cnt[:], ALU.subtract))
                ranks = ps[:, b, 0:NT * NE].rearrange("p (t n) -> p t n", t=NT)
                link(dve.tensor_tensor(rb[:], ranks, off[:].unsqueeze(1).to_broadcast([P, NT, NE]), ALU.add))
                for j, m_ in enumerate((m1, m2)):
                    link(dve.tensor_tensor(se[:], rb[:], m_[:], ALU.mult))
                    link(dve.tensor_reduce(posf[:, j, :], se[:], AX.X, ALU.add))
                dve.wait_ge(counts_r, l * 2 + 2)
                for i in range(6):
                    hb, hn = use("h2n", i, l)
                    dve.wait_ge(full[hb], hn + 1)
                for half_at in range(2):
                    a, z = half_at * HALF, (half_at + 1) * HALF
                    for t in range(NT):
                        link(dve.tensor_scalar(place[:, t, a:z], count768[:, a:z], posf[:, 0, t:t + 1], None, ALU.is_equal))
                        dve.scalar_tensor_tensor(place[:, t, a:z], count768[:, a:z], posf[:, 1, t:t + 1],
                                                 place[:, t, a:z].bitcast(F32), ALU.is_equal, ALU.add).then_inc(place_r, 1)
                for j, m_ in enumerate((m1, m2)):
                    link(dve.tensor_tensor(rb[:], sc[:], m_[:], ALU.mult))
                    link(dve.tensor_reduce(wk[:, j, :], rb[:], AX.X, ALU.add))
                link(dve.tensor_tensor(ws[:], wk[:, 0, :], wk[:, 1, :], ALU.add))
                link(dve.reciprocal(ws[:], ws[:]))
                dve.tensor_tensor(wk[:, 0, :], wk[:, 0, :], ws[:], ALU.mult)
                link(dve.tensor_tensor(wk[:, 1, :], wk[:, 1, :], ws[:], ALU.mult))
                link(dve.scalar_tensor_tensor(rb[:], ranks, 1.0, ra[:], ALU.add, ALU.mult))
                ready(dve.tensor_scalar(rank_at[:, :, 0:NE], rb[:], -1.0, None, ALU.add), freed[b], n + 1)
                for q in range(1, BLOCKS):
                    dve.tensor_scalar(rank_at[:, :, q * NE:(q + 1) * NE], rb[:], -1.0 - q * P, None, ALU.add)
                link(dve.tensor_tensor(se[:], m1[:], wk[:, 0, :].unsqueeze(2).to_broadcast([P, NT, NE]), ALU.mult))
                link(dve.tensor_tensor(sc[:], m2[:], wk[:, 1, :].unsqueeze(2).to_broadcast([P, NT, NE]), ALU.mult))
                for q in range(BLOCKS):
                    dve.tensor_tensor(weight[:, :, q * NE:(q + 1) * NE], se[:], sc[:], ALU.add)
                for q in range(BLOCKS):
                    last = dve.tensor_scalar(placef[:, q * NE:(q + 1) * NE], off[0:1, :], float(q * P), float(ROWS), ALU.add, ALU.min)
                link(last)
                link(dve.tensor_reduce(full_f[:], cnt[0:1, :], AX.X, ALU.max))
                link(dve.tensor_scalar(full_f[:], full_f[:], float(P), None, ALU.is_gt))
                link(dve.tensor_scalar(narrow_f[:], cnt[0:1, :], float(P // 2), None, ALU.is_le))
                dve.tensor_copy(narrow_e[:], narrow_f[:])
                dve.tensor_copy(place_at[:], placef[:])
                ready(dve.tensor_copy(overfull[:], full_f[:]), pos_r, l + 1)
                ready(dve.memset(nat[:], 0.0), sums_zero, l + 1)
                settle(dve)

                def expert(e, before_e=None):
                    def n_of(b):
                        return expert_use(b, l, e)

                    late = 0 if before_e is None else 1
                    by_width(dve, e, lambda small: own_and_hid(full, freed, n_of, own_r, e, n_of(7) - late, n_of(4) - late, small))
                    if before_e is not None:
                        add_rows(full, freed, lambda b: expert_use(b, l, before_e), before_e)
                    by_width(dve, e, lambda small: rows_lo(freed, orow_hi_r, l * (2 * NE) + e * 2 + 1, small))

                expert(0)
                with dve.Fori(0, NE - 1) as e:
                    expert(e + 1, e)
                add_rows(full, freed, lambda b: expert_use(b, l, NE - 1), NE - 1)
                over = dve.value_load(overfull[0:1, 0:1], min_val=0, max_val=1)
                with dve.If(over > 0):
                    for b in (0, 1, 4, 7):
                        dve.wait_ge(freed[b], expert_use(b, l, NE))
                    settle(dve)
                    with dve.Fori(0, OSTEPS) as i:
                        own_and_hid(full_o, freed_o, lambda b: further_use(b, l, i), own_r_o, i + NE,
                                    further_use(7, l, i), further_use(4, l, i), False)
                        rows_lo(freed_o, orow_hi_r_o, l * (2 * OSTEPS) + i * 2 + 1, False)
                        add_rows(full_o, freed_o, lambda b: further_use(b, l, i), i + NE)
                with dve.Else():
                    for b, n in ((0, 2), (1, 2), (3, 1), (4, 1), (5, 1), (6, 1), (7, 1)):
                        dve.sem_inc(freed_o[b], n * OSTEPS)
                    dve.sem_inc(own_r_o, OSTEPS)
                dve.nop()

                for i in range(6):
                    b, n = use("y", i, l)
                    dve.wait_ge(full[b], n + 1)
                    t, h = i // 2, i % 2
                    for k in range(4):
                        kk = 4 * h + k
                        x_ = xT[:, kk, t * P:(t + 1) * P]
                        last = dve.scalar_tensor_tensor(x_, ps[:, b, k * P:(k + 1) * P], mod[:, 40 + kk, min(t, 1):min(t, 1) + 1],
                                                        x_, ALU.mult, ALU.add)
                    last.then_inc(freed[b], 1)
                assert steps[0] <= CHAIN, steps
                dve.sem_inc(chain, CHAIN - steps[0])

            add_squares(2 * DEPTH)
            dve.wait_ge(freed[3], DEPTH * PER[3] + INIT[3] + 1)
            dve.reciprocal(rstd[:], rms[:]).then_inc(chain, 1)
            dve.wait_ge(chain, DEPTH * CHAIN + BASE + 1)
            norm_tiles(2 * DEPTH)


INPUTS = ["x_prompt", "x_sample", "cache_k", "cache_v", "c", "c_ctx", "w_ada", "w_in", "w_attn_proj", "w_conv_proj",
          "w_out", "w_router", "router_bias", "w_e_gate", "w_e_up", "w_e_down", "final_norm"]
OUTPUTS = [("y_prompt", (1, TC, D)), ("y_sample", (1, TL, D)), ("new_k", (1, DEPTH, TC, NKV, HD)),
           ("new_v", (1, DEPTH, TC, NKV, HD))]


def kernel(**inputs):
    import numpy as np
    import concourse.bacc as bacc
    from concourse.bass_utils import run_bass_kernel_spmd as run

    nc = bacc.Bacc("TRN2", target_bir_lowering=False, num_devices=1)
    arrays = {name: np.ascontiguousarray(inputs[name]) for name in INPUTS}
    def packed(names, shape):
        rows = np.concatenate([np.asarray(inputs[name]).reshape(DEPTH, -1) for name in names], axis=1)
        return np.concatenate([rows, np.zeros_like(rows[:1])]).reshape(DEPTH + 1, *shape)

    arrays["features"] = packed(["b_ada", "norm1", "norm2", "dw_b", "cln_g", "cln_b"], (76, P))
    arrays["taps"] = packed(["dw_w"], (CK * KC, P))
    arrays["every"] = packed(["q_norm", "k_norm", "sink"], (2 * HD + NH,))
    grid_w, pairs = 64, HD // 4
    inv = (np.float32(10000.0) ** (-np.arange(pairs, dtype=np.float32) / np.float32(pairs))).astype(np.float32)
    tok = np.arange(TL)
    halves = [(tok // grid_w).astype(np.float32)[:, None] * inv, (tok % grid_w).astype(np.float32)[:, None] * inv]
    cos = np.concatenate([np.cos(h) for h in halves for _ in range(2)], axis=1)
    sin = np.concatenate([s * np.sin(h) for h in halves for s in (-1, 1)], axis=1)
    arrays["rope"] = np.stack([cos, sin], axis=1).astype(np.float32)
    A = {}
    for name, a in arrays.items():
        A[name] = nc.dram_tensor("in_" + name, a.shape, mybir.dt.from_np(a.dtype), kind="ExternalInput").ap()
    for name, shape in OUTPUTS:
        A[name] = nc.dram_tensor("out_" + name, shape, F32, kind="ExternalOutput").ap()
    build(nc, A)
    r = run(nc, [{"in_" + name: a for name, a in arrays.items()}], core_ids=[0])
    return tuple(r.results[0]["out_" + name] for name, _ in OUTPUTS)
```
